# Optimizing a Trainium2 kernel written in Bass

```python
import jax, jax.numpy as jnp
from jax import lax
import numpy as np
import math

D_MODEL = 1024
BATCH = 1
SEQ = 256
DEPTH = 1

HEAD_DIM = 64
FOX_HEADS = 8
NSA_HEADS = 8
NSA_GROUPS = 2
NSA_HPG = NSA_HEADS // NSA_GROUPS
BRANCH_WIDTH = 512
N_BRANCH = 2
N_NSA_BRANCH = 3
ROPE_DIM = HEAD_DIM // 4
ROPE_THETA = 500000.0
Q_BLOCK = 128
CMP_LEN = 32
CMP_STRIDE = 16
CMP_HIDDEN = 2 * HEAD_DIM
SLC_LEN = 64
SLC_TOP = 16
WINDOW = 512
FORGET_BIAS_INIT = 4.0
FORCED_SCORE = 1e9
NEG_INF = -1e30
PEER_HEADS = 8
N_KEYS = 128
N_EXPERTS = N_KEYS * N_KEYS
PEER_QDIM = 256
PEER_TOPK = 16
PEER_CHUNK = 128
RMS_EPS = 1e-6

KV_WIDTH = NSA_GROUPS * HEAD_DIM
IN_SPLITS = (BRANCH_WIDTH, BRANCH_WIDTH, BRANCH_WIDTH, FOX_HEADS, BRANCH_WIDTH,
             KV_WIDTH, KV_WIDTH, KV_WIDTH, KV_WIDTH, KV_WIDTH, KV_WIDTH,
             NSA_HEADS * N_NSA_BRANCH, N_BRANCH * D_MODEL)
D_IN = sum(IN_SPLITS)


def rmsnorm(x, g):
    xf = x.astype(jnp.float32)
    y = xf * lax.rsqrt(jnp.mean(xf * xf, axis=-1, keepdims=True) + RMS_EPS)
    return (y * g.astype(jnp.float32)).astype(x.dtype)

def split_columns(t, sizes):
    offs = np.cumsum((0,) + tuple(sizes))
    return [t[..., int(a):int(b)] for a, b in zip(offs[:-1], offs[1:])]

def rope_tables(pos):
    inv = jnp.power(ROPE_THETA, -jnp.arange(0, ROPE_DIM, 2, dtype=jnp.float32) / ROPE_DIM)
    ang = pos[:, None] * inv[None, :]
    return jnp.cos(ang), jnp.sin(ang)

def apply_partial_rope(x, cos, sin):
    half = ROPE_DIM // 2
    xr = x[..., :ROPE_DIM].astype(jnp.float32)
    x1, x2 = xr[..., :half], xr[..., half:]
    c, s = cos[:, None, :], sin[:, None, :]
    rot = jnp.concatenate([x1 * c - x2 * s, x1 * s + x2 * c], axis=-1)
    return jnp.concatenate([rot.astype(x.dtype), x[..., ROPE_DIM:]], axis=-1)

def fox_attention(q, k, v, log_f):
    B_, S_, H, Dh = q.shape
    scale = Dh ** -0.5
    c = jnp.swapaxes(jnp.cumsum(log_f, axis=1), 1, 2)
    k_pos = jnp.arange(S_)

    def block(i):
        q0 = i * Q_BLOCK
        q_pos = q0 + jnp.arange(Q_BLOCK)
        qb = lax.dynamic_slice_in_dim(q, q0, Q_BLOCK, axis=1)
        cb = lax.dynamic_slice_in_dim(c, q0, Q_BLOCK, axis=2)
        logits = jnp.einsum('bqhd,bkhd->bhqk', qb, k).astype(jnp.float32) * scale
        logits = logits + (cb[..., :, None] - c[..., None, :])
        mask = k_pos[None, :] <= q_pos[:, None]
        p = jax.nn.softmax(jnp.where(mask, logits, NEG_INF), axis=-1)
        return jnp.einsum('bhqk,bkhd->bqhd', p.astype(v.dtype), v).reshape(B_, Q_BLOCK, H * Dh)

    out = lax.map(block, jnp.arange(S_ // Q_BLOCK))
    return jnp.moveaxis(out, 0, 1).reshape(B_, S_, H * Dh)

def compress_kv(k, v, cmp_pos, w1, w2):
    B_, S_ = k.shape[0], k.shape[1]
    n_cmp = (S_ - CMP_LEN) // CMP_STRIDE + 1
    starts = np.arange(n_cmp) * CMP_STRIDE
    idx = starts[:, None] + np.arange(CMP_LEN)[None, :]

    def phi(t, j):
        blocks = t[:, idx] + cmp_pos[j][None, None, :, None, :]
        flat = jnp.swapaxes(blocks, 2, 3).reshape(B_, n_cmp, NSA_GROUPS, CMP_LEN * HEAD_DIM)
        return jax.nn.gelu(flat @ w1[j], approximate=False) @ w2[j]

    return phi(k, 0), phi(v, 1), jnp.asarray(starts + CMP_LEN - 1, dtype=jnp.int32)

def nsa_attention(q, k_cmp, v_cmp, cmp_end, k_slc, v_slc, k_win, v_win, gates):
    B_, S_, H, Dh = q.shape
    G = NSA_GROUPS
    scale = Dh ** -0.5
    n_cmp = k_cmp.shape[1]
    n_slc = S_ // SLC_LEN
    top = min(SLC_TOP, n_slc)
    cs = np.arange(n_cmp)[:, None] * CMP_STRIDE
    ss = np.arange(n_slc)[None, :] * SLC_LEN
    ov = np.clip(np.minimum(cs + CMP_LEN, ss + SLC_LEN) - np.maximum(cs, ss), 0, None) / CMP_LEN
    overlap = jnp.asarray(ov, dtype=jnp.float32)
    kb = k_slc.reshape(B_, n_slc, SLC_LEN, G, Dh).transpose(0, 3, 1, 2, 4)
    vb = v_slc.reshape(B_, n_slc, SLC_LEN, G, Dh).transpose(0, 3, 1, 2, 4)
    pad = ((0, 0), (WINDOW, 0), (0, 0), (0, 0))
    kwp, vwp = jnp.pad(k_win, pad), jnp.pad(v_win, pad)
    bi = jnp.arange(B_)[:, None, None, None]
    gi = jnp.arange(G)[None, :, None, None]
    blk_ids = jnp.arange(n_slc)

    def block(i):
        q0 = i * Q_BLOCK
        q_pos = q0 + jnp.arange(Q_BLOCK)
        qb = lax.dynamic_slice_in_dim(q, q0, Q_BLOCK, axis=1).reshape(B_, Q_BLOCK, G, NSA_HPG, Dh)
        gb = lax.dynamic_slice_in_dim(gates, q0, Q_BLOCK, axis=1).reshape(B_, Q_BLOCK, G, NSA_HPG, N_NSA_BRANCH)
        lc = jnp.einsum('bqghd,bngd->bghqn', qb, k_cmp).astype(jnp.float32) * scale
        mc = cmp_end[None, :] <= q_pos[:, None]
        pc = jax.nn.softmax(jnp.where(mc, lc, NEG_INF), axis=-1) * mc
        o_cmp = jnp.einsum('bghqn,bngd->bqghd', pc.astype(v_cmp.dtype), v_cmp)
        imp = jnp.einsum('bghqn,nj->bgqj', pc, overlap)
        q_blk = q_pos // SLC_LEN
        forced = (blk_ids[None, :] == 0) | (blk_ids[None, :] == q_blk[:, None]) | (blk_ids[None, :] == q_blk[:, None] - 1)
        causal = blk_ids[None, :] <= q_blk[:, None]
        score = jnp.where(forced, FORCED_SCORE, jnp.where(causal, imp, -1.0))
        _, sel = lax.top_k(score, top)
        k_sel = kb[bi, gi, sel]
        v_sel = vb[bi, gi, sel]
        ls = jnp.einsum('bqghd,bgqkld->bghqkl', qb, k_sel).astype(jnp.float32) * scale
        tok = sel[..., None] * SLC_LEN + jnp.arange(SLC_LEN)
        ms = (tok <= q_pos[None, None, :, None, None])[:, :, None]
        ls = jnp.where(ms, ls, NEG_INF).reshape(B_, G, NSA_HPG, Q_BLOCK, top * SLC_LEN)
        ps = jax.nn.softmax(ls, axis=-1).reshape(B_, G, NSA_HPG, Q_BLOCK, top, SLC_LEN)
        o_slc = jnp.einsum('bghqkl,bgqkld->bqghd', ps.astype(v_sel.dtype), v_sel)
        kwb = lax.dynamic_slice_in_dim(kwp, q0, WINDOW + Q_BLOCK, axis=1)
        vwb = lax.dynamic_slice_in_dim(vwp, q0, WINDOW + Q_BLOCK, axis=1)
        k_pos = q0 - WINDOW + jnp.arange(WINDOW + Q_BLOCK)
        lw = jnp.einsum('bqghd,bkgd->bghqk', qb, kwb).astype(jnp.float32) * scale
        rel = q_pos[:, None] - k_pos[None, :]
        mw = (rel >= 0) & (rel < WINDOW) & (k_pos[None, :] >= 0)
        pw = jax.nn.softmax(jnp.where(mw, lw, NEG_INF), axis=-1)
        o_win = jnp.einsum('bghqk,bkgd->bqghd', pw.astype(vwb.dtype), vwb)
        o = gb[..., 0:1] * o_cmp + gb[..., 1:2] * o_slc + gb[..., 2:3] * o_win
        return o.astype(q.dtype).reshape(B_, Q_BLOCK, H * Dh)

    out = lax.map(block, jnp.arange(S_ // Q_BLOCK))
    return jnp.moveaxis(out, 0, 1).reshape(B_, S_, H * Dh)

def hybrid_mixer(h, w_in, fox_f_bias, cmp_pos, cmp_w1, cmp_w2, w_branch, w_out):
    B_, S_, _ = h.shape
    proj = h @ w_in
    (fq, fk, fv, f_logit, nq, kc, vc, ksl, vsl, kwn, vwn,
     nsa_gate_logit, merge_logit) = split_columns(proj, IN_SPLITS)
    heads = lambda t, n: t.reshape(B_, S_, n, HEAD_DIM)
    log_f = jax.nn.log_sigmoid(f_logit.astype(jnp.float32) + fox_f_bias.astype(jnp.float32))
    y_fox = fox_attention(heads(fq, FOX_HEADS), heads(fk, FOX_HEADS), heads(fv, FOX_HEADS), log_f)
    cos, sin = rope_tables(jnp.arange(S_, dtype=jnp.float32))
    q_nsa = apply_partial_rope(heads(nq, NSA_HEADS), cos, sin)
    k_slc = apply_partial_rope(heads(ksl, NSA_GROUPS), cos, sin)
    k_win = apply_partial_rope(heads(kwn, NSA_GROUPS), cos, sin)
    k_cmp, v_cmp, cmp_end = compress_kv(heads(kc, NSA_GROUPS), heads(vc, NSA_GROUPS), cmp_pos, cmp_w1, cmp_w2)
    k_cmp = apply_partial_rope(k_cmp, *rope_tables(cmp_end.astype(jnp.float32)))
    gates = jax.nn.sigmoid(nsa_gate_logit.astype(jnp.float32)).reshape(B_, S_, NSA_HEADS, N_NSA_BRANCH)
    y_nsa = nsa_attention(q_nsa, k_cmp, v_cmp, cmp_end, k_slc, heads(vsl, NSA_GROUPS),
                          k_win, heads(vwn, NSA_GROUPS), gates)
    g = jax.nn.sigmoid(merge_logit.astype(jnp.float32)).reshape(B_, S_, N_BRANCH, D_MODEL).astype(h.dtype)
    ys = jnp.stack([y_fox, y_nsa], axis=2)
    up = jnp.einsum('bsnc,ncd->bsnd', ys, w_branch)
    merged = jnp.sum(g * up, axis=2)
    return merged @ w_out

def peer_ffn(h, wq, subkeys, u, v):
    B_, S_, D = h.shape
    T = B_ * S_
    hf = h.reshape(T, D)
    q = (hf @ wq).reshape(T, PEER_HEADS, 2, PEER_QDIM // 2)
    s = jnp.einsum('thpd,hpnd->thpn', q, subkeys).astype(jnp.float32)
    s1, i1 = lax.top_k(s[:, :, 0], PEER_TOPK)
    s2, i2 = lax.top_k(s[:, :, 1], PEER_TOPK)
    cand = (s1[..., :, None] + s2[..., None, :]).reshape(T, PEER_HEADS, PEER_TOPK * PEER_TOPK)
    cand_idx = (i1[..., :, None] * N_KEYS + i2[..., None, :]).reshape(T, PEER_HEADS, PEER_TOPK * PEER_TOPK)
    top_s, pos = lax.top_k(cand, PEER_TOPK)
    idx = jnp.take_along_axis(cand_idx, pos, axis=-1)
    w = jax.nn.softmax(top_s, axis=-1)

    def chunk(args):
        x_c, idx_c, w_c = args
        act = jax.nn.gelu(jnp.einsum('cd,chkd->chk', x_c, u[idx_c]).astype(jnp.float32), approximate=False)
        coef = (w_c * act).astype(v.dtype)
        return jnp.einsum('chk,chkd->cd', coef, v[idx_c])

    nc = T // PEER_CHUNK
    out = lax.map(chunk, (hf.reshape(nc, PEER_CHUNK, D),
                          idx.reshape(nc, PEER_CHUNK, PEER_HEADS, PEER_TOPK),
                          w.reshape(nc, PEER_CHUNK, PEER_HEADS, PEER_TOPK)))
    return out.reshape(B_, S_, D)

def first_inputs(seed: int = 0) -> dict:
    key = jax.random.key(seed)
    ks = jax.random.split(key, 16)
    f32 = jnp.float32
    nrm = lambda k, shape, scale: scale * jax.random.normal(k, shape, f32)
    L = DEPTH
    return {
        "x": jax.random.normal(ks[0], (BATCH, SEQ, D_MODEL), f32),
        "norm_mix": 1.0 + nrm(ks[1], (L, D_MODEL), 0.02),
        "w_in": nrm(ks[2], (L, D_MODEL, D_IN), D_MODEL ** -0.5),
        "fox_f_bias": FORGET_BIAS_INIT + nrm(ks[3], (L, FOX_HEADS), 0.1),
        "nsa_cmp_pos": nrm(ks[4], (L, 2, CMP_LEN, HEAD_DIM), 0.02),
        "nsa_cmp_w1": nrm(ks[5], (L, 2, CMP_LEN * HEAD_DIM, CMP_HIDDEN), (CMP_LEN * HEAD_DIM) ** -0.5),
        "nsa_cmp_w2": nrm(ks[6], (L, 2, CMP_HIDDEN, HEAD_DIM), CMP_HIDDEN ** -0.5),
        "w_branch": nrm(ks[7], (L, N_BRANCH, BRANCH_WIDTH, D_MODEL), BRANCH_WIDTH ** -0.5),
        "w_out": nrm(ks[8], (L, D_MODEL, D_MODEL), D_MODEL ** -0.5),
        "norm_ffn": 1.0 + nrm(ks[9], (L, D_MODEL), 0.02),
        "peer_wq": nrm(ks[10], (L, D_MODEL, PEER_HEADS * PEER_QDIM), D_MODEL ** -0.5),
        "peer_subkeys": nrm(ks[11], (L, PEER_HEADS, 2, N_KEYS, PEER_QDIM // 2), (PEER_QDIM // 2) ** -0.5),
        "peer_u": nrm(ks[12], (L, N_EXPERTS, D_MODEL), D_MODEL ** -0.5),
        "peer_v": nrm(ks[13], (L, N_EXPERTS, D_MODEL), (PEER_HEADS * PEER_TOPK) ** -0.5),
        "norm_final": 1.0 + nrm(ks[14], (D_MODEL,), 0.02),
    }

def first_block(x, norm_mix, w_in, fox_f_bias, nsa_cmp_pos, nsa_cmp_w1, nsa_cmp_w2, w_branch, w_out,
              norm_ffn, peer_wq, peer_subkeys, peer_u, peer_v, norm_final):
    h = x
    for l in range(DEPTH):
        h = h + hybrid_mixer(rmsnorm(h, norm_mix[l]), w_in[l], fox_f_bias[l], nsa_cmp_pos[l],
                             nsa_cmp_w1[l], nsa_cmp_w2[l], w_branch[l], w_out[l])
        h = h + peer_ffn(rmsnorm(h, norm_ffn[l]), peer_wq[l], peer_subkeys[l], peer_u[l], peer_v[l])
    return rmsnorm(h, norm_final)


DELTA_HEAD_DIM = 128
DELTA_WIDTH = D_MODEL // 2
N_DELTA_HEADS = DELTA_WIDTH // DELTA_HEAD_DIM
SHORT_CONV = 5
CHUNK = 64
POOL_WINDOWS = (2, 4, 8, 16)
N_POOL_GROUPS = len(POOL_WINDOWS)
POOL_WIDTH = D_MODEL - DELTA_WIDTH
POOL_GROUP_DIM = POOL_WIDTH // N_POOL_GROUPS
MIX_WIDTH = DELTA_WIDTH + POOL_WIDTH
IN_COLS = 4 * DELTA_WIDTH + 4 * N_DELTA_HEADS + POOL_WIDTH
N_EXPERTS_2 = 16
EC_CAPACITY = 2
EXPERT_FF = 2 * D_MODEL


def _rmsnorm(x, w):
    xf = x.astype(jnp.float32)
    y = xf * lax.rsqrt(jnp.mean(xf * xf, axis=-1, keepdims=True) + RMS_EPS)
    return (y * w.astype(jnp.float32)).astype(x.dtype)

def _l2norm(x):
    xf = x.astype(jnp.float32)
    return xf * lax.rsqrt(jnp.sum(xf * xf, axis=-1, keepdims=True) + RMS_EPS)

def _centred_dwconv(x, w):
    K = w.shape[0]
    return lax.conv_general_dilated(
        x, w[:, None, :].astype(x.dtype), window_strides=(1,),
        padding=[(K // 2, K // 2)], dimension_numbers=('NWC', 'WIO', 'NWC'),
        feature_group_count=x.shape[-1])

def _chunk_gated_delta_rule(q, k, v, g, beta):
    out_dtype = v.dtype
    q, k, v, g, beta = (a.astype(jnp.float32) for a in (q, k, v, g, beta))
    B, H, T, Dk = q.shape
    Dv = v.shape[-1]
    N = T // CHUNK
    q = q.reshape(B, H, N, CHUNK, Dk)
    k = k.reshape(B, H, N, CHUNK, Dk)
    v = v.reshape(B, H, N, CHUNK, Dv)
    beta = beta.reshape(B, H, N, CHUNK)
    g = jnp.cumsum(g.reshape(B, H, N, CHUNK), axis=-1)
    incl = jnp.tril(jnp.ones((CHUNK, CHUNK), dtype=bool))
    strict = jnp.tril(jnp.ones((CHUNK, CHUNK), dtype=bool), -1)
    diff = g[..., :, None] - g[..., None, :]
    decay = jnp.where(incl, jnp.exp(jnp.where(incl, diff, 0.0)), 0.0)
    kk = jnp.einsum('bhncd,bhnsd->bhncs', k, k)
    a_mat = jnp.where(strict, beta[..., :, None] * kk * decay, 0.0) + jnp.eye(CHUNK, dtype=jnp.float32)
    rhs = jnp.concatenate([v * beta[..., None], k * (beta * jnp.exp(g))[..., None]], axis=-1)
    sol = lax.linalg.triangular_solve(a_mat, rhs, left_side=True, lower=True, unit_diagonal=True)
    u, w = sol[..., :Dv], sol[..., Dv:]
    qk = jnp.where(incl, jnp.einsum('bhncd,bhnsd->bhncs', q, k) * decay, 0.0)
    q_dec = q * jnp.exp(g)[..., None]
    g_last = g[..., -1]
    k_dec = k * jnp.exp(g_last[..., None] - g)[..., None]

    def step(S, xs):
        q_c, k_c, u_c, w_c, qk_c, gl_c = xs
        v_new = u_c - jnp.einsum('bhcd,bhde->bhce', w_c, S)
        o_c = jnp.einsum('bhcd,bhde->bhce', q_c, S) + jnp.einsum('bhcs,bhse->bhce', qk_c, v_new)
        S = S * jnp.exp(gl_c)[..., None, None] + jnp.einsum('bhcd,bhce->bhde', k_c, v_new)
        return S, o_c

    xs = tuple(jnp.moveaxis(a, 2, 0) for a in (q_dec, k_dec, u, w, qk, g_last))
    _, o = lax.scan(step, jnp.zeros((B, H, Dk, Dv), jnp.float32), xs)
    return jnp.moveaxis(o, 0, 2).reshape(B, H, T, Dv).astype(out_dtype)

def _log_decay(a, a_log, dt_bias):
    gl = -jnp.exp(a_log.astype(jnp.float32)) * jax.nn.softplus(a.astype(jnp.float32) + dt_bias.astype(jnp.float32))
    return jnp.swapaxes(gl, 1, 2)

def _centred_mean_pool(u, window):
    B, T, C = u.shape
    lo = window // 2
    hi = window - lo - 1
    csum = jnp.concatenate([jnp.zeros((B, 1, C), jnp.float32), jnp.cumsum(u.astype(jnp.float32), axis=1)], axis=1)
    t = jnp.arange(T)
    start = jnp.maximum(t - lo, 0)
    end = jnp.minimum(t + hi + 1, T)
    total = csum[:, end] - csum[:, start]
    count = (end - start).astype(jnp.float32)
    return (total / count[None, :, None]).astype(u.dtype)

def _hybrid_mixer(xn, w_in, conv_w, a_log_fwd, dt_bias_fwd, a_log_bwd, dt_bias_bwd,
                  head_norm_w, pool_w, pool_scale, w_out):
    B, T, _ = xn.shape
    H, Dh = N_DELTA_HEADS, DELTA_HEAD_DIM
    proj = jnp.einsum('btd,dc->btc', xn, w_in)
    qkv, z, ab, u = jnp.split(proj, [3 * DELTA_WIDTH, 4 * DELTA_WIDTH, 4 * DELTA_WIDTH + 4 * H], axis=-1)
    qkv = jax.nn.silu(_centred_dwconv(qkv, conv_w))
    q, k, v = jnp.split(qkv, 3, axis=-1)
    to_heads = lambda a: jnp.swapaxes(a.reshape(B, T, H, Dh), 1, 2)
    q = (_l2norm(to_heads(q)) * (Dh ** -0.5)).astype(xn.dtype)
    k = _l2norm(to_heads(k)).astype(xn.dtype)
    v = to_heads(v)
    a_f, b_f, a_b, b_b = jnp.split(ab, 4, axis=-1)
    g_f = _log_decay(a_f, a_log_fwd, dt_bias_fwd)
    g_b = _log_decay(a_b, a_log_bwd, dt_bias_bwd)
    beta_f = jnp.swapaxes(jax.nn.sigmoid(b_f.astype(jnp.float32)), 1, 2)
    beta_b = jnp.swapaxes(jax.nn.sigmoid(b_b.astype(jnp.float32)), 1, 2)
    o_fwd = _chunk_gated_delta_rule(q, k, v, g_f, beta_f)
    rev = lambda a: jnp.flip(a, axis=2)
    o_bwd = rev(_chunk_gated_delta_rule(rev(q), rev(k), rev(v), rev(g_b), rev(beta_b)))
    o = jnp.swapaxes(o_fwd + o_bwd, 1, 2)
    o = _rmsnorm(o, head_norm_w) * jax.nn.silu(z.reshape(B, T, H, Dh))
    o_delta = o.reshape(B, T, DELTA_WIDTH)
    ug = u.reshape(B, T, N_POOL_GROUPS, POOL_GROUP_DIM)
    pooled = jnp.stack([_centred_mean_pool(ug[:, :, i], w) for i, w in enumerate(POOL_WINDOWS)], axis=2)
    o_pool = jnp.einsum('btgc,gcd->btgd', pooled - ug, pool_w).reshape(B, T, POOL_WIDTH) * pool_scale
    return jnp.einsum('btc,cd->btd', jnp.concatenate([o_delta, o_pool], axis=-1), w_out)

def _expert_choice_ffn(xn, router_w, w_gate, w_up, w_down):
    B, T, D = xn.shape
    cap = EC_CAPACITY * T // N_EXPERTS_2
    probs = jax.nn.softmax(jnp.einsum('btd,de->bte', xn, router_w).astype(jnp.float32), axis=-1)
    gate, idx = lax.top_k(jnp.swapaxes(probs, 1, 2), cap)
    bidx = jnp.arange(B)[:, None, None]
    xg = xn[bidx, idx]
    h = jax.nn.silu(jnp.einsum('becd,edf->becf', xg, w_gate)) * jnp.einsum('becd,edf->becf', xg, w_up)
    y = jnp.einsum('becf,efd->becd', h, w_down) * gate[..., None].astype(xn.dtype)
    return jnp.zeros_like(xn).at[bidx, idx].add(y)

def second_inputs(seed: int = 0) -> dict:
    key = jax.random.key(seed)
    ks = jax.random.split(key, 20)
    H = N_DELTA_HEADS
    nrm = lambda k, shape, fan_in: jax.random.normal(k, shape, jnp.float32) * (fan_in ** -0.5)
    gain = lambda k, shape: 1.0 + 0.02 * jax.random.normal(k, shape, jnp.float32)
    def dt_bias(k):
        dt = jnp.exp(jax.random.uniform(k, (DEPTH, H), jnp.float32, math.log(1e-3), math.log(1e-1)))
        return dt + jnp.log(-jnp.expm1(-dt))
    return {
        'x': jax.random.normal(ks[0], (BATCH, SEQ, D_MODEL), jnp.float32),
        'norm_mix_w': gain(ks[1], (DEPTH, D_MODEL)),
        'w_in': nrm(ks[2], (DEPTH, D_MODEL, IN_COLS), D_MODEL),
        'conv_w': nrm(ks[3], (DEPTH, SHORT_CONV, 3 * DELTA_WIDTH), SHORT_CONV),
        'a_log_fwd': jnp.log(jax.random.uniform(ks[4], (DEPTH, H), jnp.float32, 1.0, 16.0)),
        'dt_bias_fwd': dt_bias(ks[5]),
        'a_log_bwd': jnp.log(jax.random.uniform(ks[6], (DEPTH, H), jnp.float32, 1.0, 16.0)),
        'dt_bias_bwd': dt_bias(ks[7]),
        'head_norm_w': gain(ks[8], (DEPTH, DELTA_HEAD_DIM)),
        'pool_w': nrm(ks[9], (DEPTH, N_POOL_GROUPS, POOL_GROUP_DIM, POOL_GROUP_DIM), POOL_GROUP_DIM),
        'pool_scale': gain(ks[10], (DEPTH, POOL_WIDTH)),
        'w_out': nrm(ks[11], (DEPTH, MIX_WIDTH, D_MODEL), MIX_WIDTH),
        'norm_ffn_w': gain(ks[12], (DEPTH, D_MODEL)),
        'router_w': nrm(ks[13], (DEPTH, D_MODEL, N_EXPERTS_2), D_MODEL),
        'expert_w_gate': nrm(ks[14], (DEPTH, N_EXPERTS_2, D_MODEL, EXPERT_FF), D_MODEL),
        'expert_w_up': nrm(ks[15], (DEPTH, N_EXPERTS_2, D_MODEL, EXPERT_FF), D_MODEL),
        'expert_w_down': nrm(ks[16], (DEPTH, N_EXPERTS_2, EXPERT_FF, D_MODEL), EXPERT_FF),
        'norm_final_w': gain(ks[17], (D_MODEL,)),
    }

def second_block(x, norm_mix_w, w_in, conv_w, a_log_fwd, dt_bias_fwd, a_log_bwd, dt_bias_bwd,
              head_norm_w, pool_w, pool_scale, w_out, norm_ffn_w, router_w,
              expert_w_gate, expert_w_up, expert_w_down, norm_final_w):
    h = x
    for i in range(DEPTH):
        h = h + _hybrid_mixer(_rmsnorm(h, norm_mix_w[i]), w_in[i], conv_w[i],
                              a_log_fwd[i], dt_bias_fwd[i], a_log_bwd[i], dt_bias_bwd[i],
                              head_norm_w[i], pool_w[i], pool_scale[i], w_out[i])
        h = h + _expert_choice_ffn(_rmsnorm(h, norm_ffn_w[i]), router_w[i],
                                   expert_w_gate[i], expert_w_up[i], expert_w_down[i])
    return _rmsnorm(h, norm_final_w)


def setup_inputs(seed=0):
    out = dict(first_inputs(seed))
    for name, value in second_inputs(seed + 1).items():
        if name != "x":
            out[name + "_2"] = value
    return out


def reference(
    x, norm_mix, w_in, fox_f_bias, nsa_cmp_pos, nsa_cmp_w1, nsa_cmp_w2, w_branch, w_out,
    norm_ffn, peer_wq, peer_subkeys, peer_u, peer_v, norm_final, norm_mix_w_2, w_in_2, conv_w_2,
    a_log_fwd_2, dt_bias_fwd_2, a_log_bwd_2, dt_bias_bwd_2, head_norm_w_2, pool_w_2,
    pool_scale_2, w_out_2, norm_ffn_w_2, router_w_2, expert_w_gate_2, expert_w_up_2,
    expert_w_down_2, norm_final_w_2,
):
    x = first_block(
        x, norm_mix, w_in, fox_f_bias, nsa_cmp_pos, nsa_cmp_w1, nsa_cmp_w2, w_branch, w_out,
        norm_ffn, peer_wq, peer_subkeys, peer_u, peer_v, norm_final,
    )
    return second_block(
        x, norm_mix_w_2, w_in_2, conv_w_2, a_log_fwd_2, dt_bias_fwd_2, a_log_bwd_2,
        dt_bias_bwd_2, head_norm_w_2, pool_w_2, pool_scale_2, w_out_2, norm_ffn_w_2, router_w_2,
        expert_w_gate_2, expert_w_up_2, expert_w_down_2, norm_final_w_2,
    )


_drawn_inputs = setup_inputs


def setup_inputs(seed=0):
    import zlib

    import numpy as np

    out = dict(_drawn_inputs(seed))
    spreads = {}
    factors = {'norm_mix': 4.918,
     'fox_f_bias': 16.986,
     'nsa_cmp_pos': 7.747,
     'norm_ffn': 17.191,
     'norm_mix_w_2': 3.113,
     'head_norm_w_2': 5.809,
     'pool_scale_2': 4.03,
     'norm_ffn_w_2': 4.252,
     'norm_final_w_2': 8.081}
    for name, (base, spread) in spreads.items():
        noise = np.random.default_rng([zlib.crc32(name.encode()), seed]).standard_normal(out[name].shape)
        drawn = base * np.exp(spread * noise) if base else spread * noise
        out[name] = __import__('jax').numpy.asarray(drawn.astype(out[name].dtype))
    for name, factor in factors.items():
        out[name] = (out[name] * factor).astype(out[name].dtype)
    return out
```

```python
import concourse.bass as bass
from concourse import mybir
from contextlib import ExitStack

F32 = mybir.dt.float32
F32R = mybir.dt.float32r
U32 = mybir.dt.uint32
ALU = mybir.AluOpType
ACT = mybir.ActivationFunctionType
AX = mybir.AxisListType

P = 128
D = 1024
KB = D // P
S = 256
NT = S // P
HW = 1024
PW = 2048
BANK = 512
DH = 64
HEADS = 8
NCMP, CMP_LEN, CMP_STRIDE = 15, 32, 16
TOPK = 16
NKEYS = 128
NEXP, CAP = 16, 32
EPS = 1e-6
NEG = -1e30
SCALE = DH ** -0.5
RING1, RING2 = 4, 8


class Link:

    def __init__(self, eng, sem, n=0):
        self.eng, self.sem, self.n = eng, sem, n

    def __call__(self, ins):
        self.n += 1
        ins.then_inc(self.sem, 1)
        self.eng.wait_ge(self.sem, self.n)


class Carve:

    def __init__(self, tile):
        self.tile, self.at = tile, 0

    def __call__(self, *shape):
        n = 1
        for x in shape:
            n *= x
        part = self.tile[:, self.at:self.at + n]
        self.at += n
        names = "abcd"[:len(shape)]
        if len(shape) > 1:
            part = part.rearrange(f"p ({' '.join(names)}) -> p {' '.join(names)}", **dict(zip(names, shape)))
        return part


class Ring:

    def __init__(self, buf, slots, loaded, used):
        self.buf, self.slots, self.loaded, self.used = buf, slots, loaded, used
        self.issued = 0

    def piece(self, g):
        return self.buf[:, g % self.slots, :]

    def issue(self, sync, g, src, turn=0):
        if g >= self.slots:
            sync.wait_ge(self.used, g - self.slots + 1 + turn * self.slots)
        sync.dma_start(self.piece(g), src).then_inc(self.loaded[g % self.slots], 16)

    def arrived(self, eng, g, turn=0):
        eng.wait_ge(self.loaded[g % self.slots], 16 * (g // self.slots + 1) + 16 * turn)


def build_kernel(nc, A, out, debug=None):
    ctx = ExitStack()
    with ctx:
        def sb(stack, name, shape, dt=F32):
            return stack.enter_context(nc.sbuf_tensor(name, shape, dt))

        stage_sems = []

        def lasting_sem(name):
            return ctx.enter_context(nc.semaphore(name))

        def sem(name):
            stage_sems.append(nc.alloc_semaphore(name))
            return stage_sems[-1]

        def next_block():
            nc.clear_and_free_semaphores(stage_sems)
            stage_sems.clear()
            with nc.Block():
                pass

        ident = sb(ctx, "ident", [P, P])
        h = sb(ctx, "h", [P, NT, D])
        gains = sb(ctx, "gains", [P, 4, KB])
        ss = sb(ctx, "ss", [P, 4])
        ps = ctx.enter_context(nc.psum_tensor("ps", [P, 8, BANK], F32))
        arena = sb(ctx, "arena", [P, NKEYS * S])
        first = ExitStack()
        ring1 = Ring(sb(first, "ring1", [P, RING1, HW]), RING1, [sem(f"ring1_loaded{i}") for i in range(RING1)], sem("ring1_used"))
        ring2_sems = [lasting_sem(f"ring2_loaded{i}") for i in range(RING2)], lasting_sem("ring2_used")
        consts_loaded = sem("consts_loaded")
        stored = lasting_sem("stored")
        chain_act, chain_dve = lasting_sem("chain_act"), lasting_sem("chain_dve")
        links = {}

        def link(eng, name, s):
            old = links.get(name)
            links[name] = Link(eng, s, old.n if old else 0)
            return links[name]

        def dump(stage, pairs):
            if debug is None or debug[0] != stage:
                return False
            with nc.Block() as block:
                @block.sync
                def _(sync):
                    for n, t in enumerate(pairs):
                        sync.dma_start(debug[1][n], t).then_inc(stored, 16)
                    sync.wait_ge(stored, 16 * len(pairs))
            return True

        class T:
            pass
        T.nc, T.A, T.ctx, T.sb, T.sem, T.link, T.ps = nc, A, ctx, sb, sem, link, ps
        T.chain_act, T.chain_dve = chain_act, chain_dve
        T.ident, T.h, T.gains, T.ss = ident, h, gains, ss
        T.dump, T.out, T.arena = dump, out, arena
        T.ring1, T.ring2_sems = ring1, ring2_sems

        def stream1(g):
            return A["stream1"][g]
        T.stream1 = stream1

        def stream2(g):
            if g < G2_EXP:
                return A["stream2"][g]
            r = g - G2_EXP
            return A["experts_in"][0, r // KB, r % KB]
        T.stream2 = stream2

        x_loaded = sem("x_loaded")
        with nc.Block() as block:
            @block.sync
            def _(sync):
                sync.dma_start(h[:, :, :], A["x"].rearrange("(t p) d -> p t d", p=P)).then_inc(x_loaded, 16)
                for g in range(RING1):
                    ring1.issue(sync, g, stream1(g))
                ring1.issued = RING1

            @block.scalar
            def _(act):
                act.dma_start(gains[:, :, :], A["gains"]).then_inc(consts_loaded, 16)
                act.dma_start(ident[:, :], A["ident"]).then_inc(consts_loaded, 16)
                act.wait_ge(consts_loaded, 32)
                act.wait_ge(x_loaded, 16)
        if dump("x", [h[:, :, :]]):
            first.close()
            return
        T.parts = first.enter_context(nc.sbuf_tensor("h_parts", [P, 2, KB, S], F32R))
        T.hT_stack = ExitStack()
        T.hT = sb(T.hT_stack, "hT", [P, KB, S])
        if mixer1(T) or peer(T):
            T.hT_stack.close()
            first.close()
            return
        first.close()
        next_block()
        T.low = sb(ctx, "low", [P, 4 * PW])
        T.hT = sb(ctx, "hT2", [P, KB, S])
        second_block(T)


def front(T, name, gain, ring, g0, groups, small, refill, xs=None):
    nc, ps, hT, h, ss = T.nc, T.ps, T.hT, T.h, T.ss
    sem = T.sem
    squares_done, mean_done, root_done, scaled = (sem(f"{name}_{s}") for s in ("squares", "mean", "root", "scaled"))
    bank_ready, bank_free = sem(f"{name}_bank_ready"), sem(f"{name}_bank_free")
    small_done = sem(f"{name}_small_done")
    TB = 4
    per = 2 if ring.slots == RING1 else 1
    stack = ExitStack()
    if xs is None:
        xs = T.sb(stack, f"{name}_xs", [P, NT, D])
    with nc.Block() as block:
        @block.sync
        def _(sync):
            refill(sync)

        @block.scalar
        def _(act):
            for t in range(NT):
                nc.scalar.activation(xs[:, t, :], h[:, t, :], ACT.Square, accum_out=ss[:, t:t + 1]).then_inc(squares_done, 1)
            act.wait_ge(mean_done, 1)
            nc.scalar.activation(ss[:, 2:4], ss[:, 2:4], ACT.Sqrt).then_inc(root_done, 1)
            for b in range(TB):
                act.wait_ge(bank_ready, b + 1)
                for kk in range(2):
                    k = 2 * b + kk
                    nc.scalar.activation(hT[:, k, :], ps[:, b, kk * S:(kk + 1) * S], ACT.Copy,
                                         scale=T.gains[:, gain, k:k + 1]).then_inc(bank_free, 1)
            done = 0
            for mode, pieces, dst, func in groups:
                loops = pieces // 4 if pieces >= 8 and ring.slots == 4 else 0
                if loops:
                    with act.Fori(0, loops) as i:
                        for r in range(4):
                            act.wait_ge(ring.used, i * (4 * per) + (g0 + per * (done + r + 1)))
                            nc.scalar.activation(dst[:, i * 4 + r, :], ps[:, (done + r) % 4, :], func).then_inc(bank_free, 1)
                for p in range(4 * loops, pieces):
                    act.wait_ge(ring.used, g0 + per * (done + p + 1))
                    nc.scalar.activation(dst[:, p, :], ps[:, (done + p) % 4, :], func).then_inc(bank_free, 1)
                done += pieces

        @block.vector
        def _(dve):
            link = T.link(dve, "dve", T.chain_dve)
            dve.wait_ge(squares_done, NT)
            nc.vector.tensor_scalar(ss[:, 2:4], ss[:, 0:2], 1.0 / D, EPS, ALU.mult, ALU.add).then_inc(mean_done, 1)
            dve.wait_ge(root_done, 1)
            link(nc.vector.reciprocal(ss[:, 2:4], ss[:, 2:4]))
            for t in range(NT):
                nc.vector.tensor_scalar(xs[:, t, :], h[:, t, :], ss[:, 2 + t:3 + t], None, ALU.mult).then_inc(scaled, 1)

        @block.tensor
        def _(pe):
            pe.wait_ge(scaled, NT)
            for b in range(TB):
                for kk in range(2):
                    for t in range(NT):
                        k = 2 * b + kk
                        last = nc.tensor.transpose(ps[:, b, kk * S + t * P:kk * S + (t + 1) * P],
                                                   xs[:, t, k * P:(k + 1) * P], T.ident[:, :])
                last.then_inc(bank_ready, 1)
            pe.wait_ge(bank_free, KB)

            def column_block(mode, g, bank, half, turn=0):
                ring.arrived(pe, g, turn)
                w = ring.piece(g).rearrange("p (k c) -> p k c", k=KB)
                for t in range(1 if mode == "F" else NT):
                    for k in range(KB):
                        if mode == "F":
                            cols, lhsT, rhs = slice(half * S, (half + 1) * S), w[:, k, :], hT[:, k, :]
                        else:
                            at = t * S + half * P
                            cols, lhsT, rhs = slice(at, at + P), hT[:, k, t * P:(t + 1) * P], w[:, k, :]
                        last = nc.tensor.matmul(ps[:, bank, cols], lhsT, rhs, start=(k == 0), stop=(k == KB - 1))
                last.then_inc(ring.used, 1)

            def piece(mode, n, bank, turn=0):
                g = g0 + n * per
                if per == 2:
                    for half in range(2):
                        column_block(mode, g + half, bank, half, turn)
                    return
                ring.arrived(pe, g, turn)
                w = ring.piece(g).rearrange("p (k c) -> p k c", k=KB)
                for half in range(2):
                    for k in range(KB):
                        if mode == "F":
                            lhsT, rhs = w[:, k, half * P:(half + 1) * P], hT[:, k, :]
                        else:
                            lhsT, rhs = hT[:, k, half * P:(half + 1) * P], w[:, k, :]
                        last = nc.tensor.matmul(ps[:, bank, half * S:(half + 1) * S], lhsT, rhs,
                                                start=(k == 0), stop=(k == KB - 1))
                last.then_inc(ring.used, 1)

            done = 0
            for mode, pieces, dst, func in groups:
                loops = pieces // 4 if pieces >= 8 and ring.slots == 4 else 0
                if loops:
                    with pe.Fori(0, loops) as i:
                        for r in range(4):
                            pe.wait_ge(bank_free, i * 4 + (KB + done + r - 3))
                            piece(mode, done + r, (done + r) % 4, i * 2)
                for p in range(4 * loops, pieces):
                    pe.wait_ge(bank_free, KB + done + p - 3)
                    piece(mode, done + p, (done + p) % 4)
                done += pieces
            small(pe, small_done)
    stack.close()
    return small_done


FQ, FK, NQ, KSL, KWN, KC, VC, MERGE = 0, 4, 8, 12, 14, 16, 17, 18
G_CMP, G_BRANCH, G_OUT, G_WQ, G_SUBK, G_PEER = 40, 48, 56, 64, 80, 82


def mixer1(T):
    nc, A, ps, sem = T.nc, T.A, T.ps, T.sem
    stack = ExitStack()
    sb = lambda name, shape: T.sb(stack, name, shape)
    h, hT, ident, ring = T.h, T.hT, T.ident, T.ring1
    carve = T.carve = Carve(T.arena)
    proj = carve(34, S)
    vtok = carve(3, NT, 256)
    small_w = sb("small_w", [P, KB, 160])
    tables = sb("tables", [P, 2, S])
    tables_cmp = sb("tables_cmp", [P, 2, 16])
    rot = sb("rot", [P, P])
    causal = sb("causal", [P, S])
    mask_cmp = sb("mask_cmp", [P, 2, NT, 16])
    sel8 = carve(8, S)
    pos = sb("pos", [P, 2, CMP_LEN])
    w2 = sb("w2", [P, 2, P])
    fbias = sb("fbias", [P, 1])
    loads = [(small_w[:, :, :], "small_w"), (tables[:, :, :], "tables"), (tables_cmp[:, :, :], "tables_cmp"),
             (rot[:, :], "rot"), (causal[:, :], "causal"), (mask_cmp[:, :, :, :], "mask_cmp"),
             (sel8[:, :, :], "sel8"), (pos[:, :, :], "cmp_pos"), (w2[:, :, :], "cmp_w2"), (fbias[:, :], "fbias")]
    mix_consts = sem("mix_consts")

    def refill(sync):
        for g in range(RING1, G_CMP + RING1):
            ring.issue(sync, g, T.stream1(g))
            if g == RING1:
                for dst, name in loads:
                    sync.dma_start(dst, A[name]).then_inc(mix_consts, 16)

    def small(pe, done):
        pe.wait_ge(mix_consts, 16 * len(loads))
        for k in range(KB):
            nc.tensor.matmul(ps[:, 4, 0:S], small_w[:, k, 0:P], hT[:, k, :], start=(k == 0), stop=(k == KB - 1))
        for t in range(NT):
            for k in range(KB):
                last = nc.tensor.matmul(ps[:, 5, t * 24:(t + 1) * 24], hT[:, k, t * P:(t + 1) * P],
                                        small_w[:, k, P:P + 24], start=(k == 0), stop=(k == KB - 1))
        last.then_inc(done, 1)

    pieces = lambda t, a, b: t[:, 2 * a:2 * b, :].rearrange("p (n c) s -> p n (c s)", c=2)
    vdst = vtok[:, :, :, :].rearrange("p n t c -> p n (t c)")
    front(T, "mix", 0, ring, 0, [("F", 9, pieces(proj, 0, 9), ACT.Copy),
                                 ("F", 8, pieces(proj, 9, 17), ACT.Sigmoid),
                                 ("T", 3, vdst, ACT.Copy)], small, refill)
    if T.dump("proj", [proj[:, :, :], vtok[:, :, :, :]]):
        stack.close()
        return True

    gates = sb("gates", [P, NT, 24])
    clog = sb("clog", [P, 2, S])
    ft = sb("ft", [P, 4, S])
    ones_row = sb("ones_row", [P, S])
    rtmp = sb("rtmp", [P, 2, 2 * S])
    kb = sb("kb", [P, 2, CMP_LEN, 16])
    hid = sb("hid", [P, 2, 2, 16])
    kcmp = sb("kcmp", [P, 2, 16])
    kc_raw = sb("kc_raw", [P, 2, 16])
    vcmp = sb("vcmp", [16, 2, DH])
    rot_done, rot_used, kb_ready, hid_ps, hid_ready = (sem(n) for n in ("rot_done", "rot_used", "kb_ready", "hid_ps", "hid_ready"))
    kc_ps, kc_sb, kcr_ps, fz_ready, fe_ready, gates_ready = (sem(n) for n in ("kc_ps", "kc_sb", "kcr_ps", "fz_ready", "fe_ready", "gates_ready"))
    with nc.Block() as block:
        @block.sync
        def _(sync):
            for g in range(G_CMP + RING1, G_BRANCH + RING1):
                ring.issue(sync, g, T.stream1(g))

        @block.tensor
        def _(pe):
            for j in range(4):
                b = NQ + 2 * j
                if j >= 2:
                    pe.wait_ge(rot_used, j - 1)
                nc.tensor.matmul(ps[:, j % 2, :], rot[:, :], proj[:, b:b + 2, :].rearrange("p b s -> p (b s)"),
                                 start=True, stop=True).then_inc(rot_done, 1)
            pe.wait_ge(kb_ready, 4)
            for j in range(2):
                if j == 1:
                    pe.wait_ge(fz_ready, 1)
                    pe.wait_ge(gates_ready, 1)
                for lh in range(4):
                    g = G_CMP + 4 * j + lh
                    ring.arrived(pe, g)
                    w1 = ring.piece(g).rearrange("p (l c) -> p l c", l=8)
                    for ll in range(8):
                        for grp in range(2):
                            lo = DH * grp
                            last = nc.tensor.matmul(ps[:, 2 + 2 * j + grp, 0:NCMP], w1[lo:lo + DH, ll, :],
                                                    kb[lo:lo + DH, j, 8 * lh + ll, 0:NCMP],
                                                    start=(lh == 0 and ll == 0), stop=(lh == 3 and ll == 7))
                    last.then_inc(ring.used, 1)
            pe.wait_ge(hid_ready, 4)
            for grp in range(2):
                nc.tensor.matmul(ps[:, 6, 16 * grp:16 * grp + NCMP], w2[:, 0, :], hid[:, 0, grp, 0:NCMP],
                                 start=True, stop=True)
            for grp in range(2):
                last = nc.tensor.matmul(ps[0:NCMP, 7, DH * grp:DH * (grp + 1)], hid[:, 1, grp, 0:NCMP],
                                        w2[:, 1, 0:DH], start=True, stop=True)
            last.then_inc(kc_ps, 1)
            pe.wait_ge(kc_sb, 1)
            nc.tensor.matmul(ps[:, 0, 0:32], rot[:, :], kc_raw[:, :, :].rearrange("p g n -> p (g n)"),
                             start=True, stop=True).then_inc(kcr_ps, 1)

        @block.scalar
        def _(act):
            link = T.link(act, "act", T.chain_act)
            nc.scalar.activation(gates[:, :, :], ps[:, 5, 0:48].rearrange("p (t c) -> p t c", t=NT), ACT.Sigmoid).then_inc(gates_ready, 1)
            act.wait_ge(fz_ready, 1)
            link(nc.scalar.activation(ft[:, 2, :], ft[:, 0, :], ACT.Abs))
            link(nc.scalar.activation(ft[:, 2, :], ft[:, 2, :], ACT.Exp, scale=-1.0))
            nc.scalar.activation(ft[:, 2, :], ft[:, 2, :], ACT.Ln, bias=1.0).then_inc(fe_ready, 1)
            for j in range(2):
                act.wait_ge(ring.used, G_CMP + 4 * (j + 1))
                for grp in range(2):
                    nc.scalar.activation(hid[:, j, grp, 0:NCMP], ps[:, 2 + 2 * j + grp, 0:NCMP], ACT.Gelu).then_inc(hid_ready, 1)

        @block.vector
        def _(dve):
            link = T.link(dve, "dve", T.chain_dve)
            for j in range(2):
                tok = proj[:, KC + j, :].rearrange("p (a b) -> p a b", b=16)
                for lh in range(2):
                    nc.vector.tensor_tensor(
                        kb[:, j, 16 * lh:16 * (lh + 1), 0:NCMP],
                        tok[:, lh:lh + NCMP, :].rearrange("p n l -> p l n"),
                        pos[:, j, 16 * lh:16 * (lh + 1)].unsqueeze(2).broadcast_to([P, 16, NCMP]),
                        ALU.add).then_inc(kb_ready, 1)
            nc.vector.tensor_scalar(ft[:, 0, :], ps[:, 4, 0:S], fbias[:, 0:1], None, ALU.add).then_inc(fz_ready, 1)
            dve.wait_ge(fz_ready, 1)
            link(nc.vector.tensor_scalar(ft[:, 1, :], ft[:, 0, :], 0.0, None, ALU.min))
            link(nc.vector.memset(ones_row[:, :], 1.0))
            link(nc.vector.memset(kc_raw[:, :, :], 0.0))
            cos = tables[:, 0, :].unsqueeze(1).broadcast_to([P, 2, S])
            sin = tables[:, 1, :].unsqueeze(1).broadcast_to([P, 2, S])
            for j in range(4):
                b = NQ + 2 * j
                dve.wait_ge(rot_done, j + 1)
                tmp = rtmp[:, j % 2, :].rearrange("p (b s) -> p b s", b=2)
                nc.vector.tensor_tensor(tmp, ps[:, j % 2, :].rearrange("p (b s) -> p b s", b=2), sin,
                                        ALU.mult).then_inc(rot_used, 1)
                link(nc.vector.tensor_tensor(proj[:, b:b + 2, :], proj[:, b:b + 2, :], cos, ALU.mult))
                dve.wait_ge(rot_used, j + 1)
                link(nc.vector.tensor_tensor(proj[:, b:b + 2, :], proj[:, b:b + 2, :], tmp, ALU.add))
            dve.wait_ge(fe_ready, 1)
            link(nc.vector.tensor_tensor(ft[:, 3, :], ft[:, 1, :], ft[:, 2, :], ALU.subtract))
            link(nc.vector.tensor_tensor_scan(clog[:, 0, :], ones_row[:, :], ft[:, 3, :], 0.0, ALU.mult, ALU.add))
            nc.vector.tensor_scalar(clog[:, 1, :], clog[:, 0, :], -1.0, None, ALU.mult)
            dve.wait_ge(kc_ps, 1)
            nc.vector.tensor_copy(vcmp[0:NCMP, :, :], ps[0:NCMP, 7, 0:P].rearrange("p (g d) -> p g d", g=2))
            nc.vector.tensor_copy(kc_raw[:, :, 0:NCMP], ps[:, 6, 0:32].rearrange("p (g n) -> p g n", g=2)[:, :, 0:NCMP]).then_inc(kc_sb, 1)
            dve.wait_ge(kc_sb, 1)
            cc = tables_cmp[:, 0, :].unsqueeze(1).broadcast_to([P, 2, 16])
            cs = tables_cmp[:, 1, :].unsqueeze(1).broadcast_to([P, 2, 16])
            link(nc.vector.tensor_tensor(kcmp[:, :, :], kc_raw[:, :, :], cc, ALU.mult))
            dve.wait_ge(kcr_ps, 1)
            link(nc.vector.tensor_tensor(kc_raw[:, :, :], ps[:, 0, 0:32].rearrange("p (g n) -> p g n", g=2), cs, ALU.mult))
            link(nc.vector.tensor_tensor(kcmp[:, :, :], kcmp[:, :, :], kc_raw[:, :, :], ALU.add))
    if T.dump("prep", [proj[:, :, :], clog[:, :, :], kcmp[:, :, :], vcmp[0:NCMP, :, :], gates[:, :, :]]):
        stack.close()
        return True
    return attention(T, stack, proj, vtok, gates, clog, kcmp, vcmp, causal, mask_cmp, sel8)


FOX, CMP, SLC, WIN = range(4)


def attention(T, stack, proj, vtok, gates, clog, kcmp, vcmp, causal, mask_cmp, sel8):
    nc, A, ps, sem = T.nc, T.A, T.ps, T.sem
    ring = T.ring1
    yT = T.carve(2, 4, S)
    lg = T.carve(2, 4, S)
    stat = T.sb(stack, "stat", [P, 2, 4, 4])
    pT = T.carve(2, 4, 2, P)
    masked, max_ready, exp_done, p_ready = (sem(n) for n in ("att_masked", "att_max", "att_exp", "att_p"))
    scores, pt_ps, pt_sb, out_ps, out_sb = (sem(n) for n in ("att_scores", "att_pt_ps", "att_pt_sb", "att_out_ps", "att_out_sb"))
    units = [(t, hg, kind) for t in range(NT) for hg in range(2) for kind in (FOX, CMP, SLC, WIN)]
    sc = lambda n: ps[:, 2 * (n % 2):2 * (n % 2) + 2, :].rearrange("p a (b s) -> p a b s", b=2)
    slots = [(par, hp) for par in range(2) for hp in range(2)]
    width = lambda t, kind: NCMP if kind == CMP else P * (t + 1)
    quad = lambda ap: ap.rearrange("p (a b) s -> p a b s", a=2)

    with nc.Block() as block:
        @block.tensor
        def _(pe):
            def score(n):
                t, hg, kind = units[n]
                w = width(t, kind)
                if n >= 2:
                    pe.wait_ge(masked, n - 1)
                rows = slice(t * P, (t + 1) * P)
                for par, hp in slots:
                    lo, pair = DH * par, 2 * hg + hp
                    hd = 2 * pair + par
                    half = slice(lo, lo + DH)
                    dst = sc(n)[:, par, hp, 0:w]
                    if kind == FOX:
                        nc.tensor.matmul(dst, proj[half, FQ + pair, rows], proj[half, FK + pair, 0:w], start=True, stop=False)
                        nc.tensor.matmul(dst, clog[half, 0, rows], sel8[half, hd, 0:w], start=False, stop=False)
                        last = nc.tensor.matmul(dst, sel8[half, hd, 0:P], clog[half, 1, 0:w], start=False, stop=True)
                    else:
                        k = {CMP: kcmp[half, hg, 0:NCMP], SLC: proj[half, KSL + hg, 0:w], WIN: proj[half, KWN + hg, 0:w]}[kind]
                        last = nc.tensor.matmul(dst, proj[half, NQ + pair, rows], k, start=True, stop=True)
                last.then_inc(scores, 1)

            def values(n):
                t, hg, kind = units[n]
                pe.wait_ge(p_ready, n + 1)
                if n >= 1:
                    pe.wait_ge(pt_sb, n)
                blocks = 1 if kind == CMP else t + 1
                for q in range(4):
                    for b in range(blocks):
                        cols = slice(0, NCMP) if kind == CMP else slice(b * P, (b + 1) * P)
                        rows = NCMP if kind == CMP else P
                        at = ps[0:rows, 4 + q // 2, (q % 2) * S + b * P:(q % 2) * S + (b + 1) * P]
                        last = nc.tensor.transpose(at, lg[:, n % 2, q, cols], T.ident[:, :])
                last.then_inc(pt_ps, 1)
                pe.wait_ge(pt_sb, n + 1)
                first = kind in (FOX, CMP)
                done = sum(1 for u in units[:n] if u[2] in (FOX, WIN))
                if first and done:
                    pe.wait_ge(out_sb, done)
                for q, (par, hp) in enumerate(slots):
                    hl = 2 * hp + par
                    dst = ps[DH * par:DH * (par + 1), 6 + hp, 0:P]
                    for b in range(blocks):
                        v = {FOX: vtok[:, hg, b, hl * DH:(hl + 1) * DH], CMP: vcmp[0:NCMP, hg, :],
                             SLC: vtok[:, 2, b, hg * DH:(hg + 1) * DH],
                             WIN: vtok[:, 2, b, P + hg * DH:P + (hg + 1) * DH]}[kind]
                        rows = NCMP if kind == CMP else P
                        last = nc.tensor.matmul(dst, v, pT[0:rows, n % 2, q, b, :], start=(first and b == 0),
                                                stop=(kind in (FOX, WIN) and b == blocks - 1))
                if kind in (FOX, WIN):
                    last.then_inc(out_ps, 1)

            for n in range(len(units) + 1):
                if n < len(units):
                    score(n)
                if n:
                    values(n - 1)

        @block.vector
        def _(dve):
            link = T.link(dve, "dve", T.chain_dve)

            def mask_max(n):
                t, hg, kind = units[n]
                w = width(t, kind)
                dve.wait_ge(scores, n + 1)
                if n >= 2:
                    dve.wait_ge(pt_ps, n - 1)
                if kind == CMP:
                    m = mask_cmp[:, 0, t, 0:w]
                else:
                    m = causal[:, S - w:S]
                x = lg[:, n % 2, :, 0:w]
                nc.vector.tensor_tensor(quad(x), sc(n)[:, :, :, 0:w],
                                        m.unsqueeze(1).unsqueeze(1).broadcast_to([P, 2, 2, w]), ALU.add).then_inc(masked, 1)
                dve.wait_ge(masked, n + 1)
                link(nc.vector.reduce_max(stat[:, n % 2, 0, :], x, AX.X))
                nc.vector.tensor_scalar(stat[:, n % 2, 1, :], stat[:, n % 2, 0, :], -SCALE, None, ALU.mult).then_inc(max_ready, 1)

            def normalise(n):
                t, hg, kind = units[n]
                w = width(t, kind)
                x = lg[:, n % 2, :, 0:w]
                dve.wait_ge(exp_done, 4 * (n + 1))
                link(nc.vector.reciprocal(stat[:, n % 2, 3, :], stat[:, n % 2, 2, :]))
                if kind != FOX:
                    g = gates[:, t, :].rearrange("p (g b a c) -> p g a b c", g=2, b=2, a=2)[:, hg, :, :, kind - 1]
                    r = stat[:, n % 2, 3, :].rearrange("p (a b) -> p a b", a=2)
                    link(nc.vector.tensor_tensor(r, r, g, ALU.mult))
                if kind == CMP:
                    m = mask_cmp[:, 1, t, 0:w].unsqueeze(1).broadcast_to([P, 4, w])
                    link(nc.vector.tensor_tensor(x, x, m, ALU.mult))
                nc.vector.tensor_tensor(x, x, stat[:, n % 2, 3, :].unsqueeze(2).broadcast_to([P, 4, w]), ALU.mult).then_inc(p_ready, 1)

            for n in range(len(units) + 1):
                if n < len(units):
                    mask_max(n)
                if n:
                    normalise(n - 1)

        @block.scalar
        def _(act):
            def exps(n):
                t, hg, kind = units[n]
                w = width(t, kind)
                act.wait_ge(max_ready, n + 1)
                for q in range(4):
                    x = lg[:, n % 2, q, 0:w]
                    nc.scalar.activation(x, x, ACT.Exp, bias=stat[:, n % 2, 1, q:q + 1], scale=SCALE,
                                         accum_out=stat[:, n % 2, 2, q:q + 1]).then_inc(exp_done, 1)

            def evacuate(n):
                t, hg, kind = units[n]
                act.wait_ge(pt_ps, n + 1)
                rows, blocks = (NCMP, 1) if kind == CMP else (P, t + 1)
                src = ps[0:rows, 4:6, :].rearrange("p c (q b s) -> p (c q) b s", q=2, b=2)[:, :, 0:blocks, :]
                nc.scalar.activation(pT[0:rows, n % 2, :, 0:blocks, :], src, ACT.Copy).then_inc(pt_sb, 1)
                if kind in (FOX, WIN):
                    done = sum(1 for u in units[:n] if u[2] in (FOX, WIN))
                    act.wait_ge(out_ps, done + 1)
                    nc.scalar.activation(yT[:, kind == WIN, 2 * hg:2 * hg + 2, t * P:(t + 1) * P],
                                         ps[:, 6:8, 0:P], ACT.Copy).then_inc(out_sb, 1)

            for n in range(len(units) + 1):
                if n < len(units):
                    exps(n)
                if n:
                    evacuate(n - 1)

    if T.dump("att", [yT[:, :, :, :]]):
        stack.close()
        return True

    merged = T.carve(KB, S)
    mt = T.carve(2, 2, 2 * S)
    up_used, merge_ready, res_done = sem("up_used"), sem("merge_ready"), sem("res_done")
    h, ident = T.h, T.ident
    with nc.Block() as block:
        @block.sync
        def _(sync):
            for g in range(G_BRANCH + RING1, G_WQ + RING1):
                ring.issue(sync, g, T.stream1(g))

        @block.tensor
        def _(pe):
            for c in range(4):
                if c >= 2:
                    pe.wait_ge(up_used, 2 * (c - 1))
                for half in range(2):
                    g = G_BRANCH + 2 * c + half
                    ring.arrived(pe, g)
                    w = ring.piece(g).rearrange("p (k c) -> p k c", k=KB)
                    for n in range(2):
                        for k in range(4):
                            last = nc.tensor.matmul(ps[:, 2 * (c % 2) + n, half * S:(half + 1) * S], w[:, 4 * n + k, :],
                                                    yT[:, n, k, :], start=(k == 0), stop=(k == 3))
                    last.then_inc(ring.used, 1)
            pe.wait_ge(merge_ready, 4)
            for c in range(8):
                g = G_OUT + c
                ring.arrived(pe, g)
                w = ring.piece(g).rearrange("p (k c) -> p k c", k=KB)
                for t in range(NT):
                    at = t * S + (c % 2) * P
                    for k in range(KB):
                        last = nc.tensor.matmul(ps[:, 4 + c // 2, at:at + P], merged[:, k, t * P:(t + 1) * P],
                                                w[:, k, :], start=(k == 0), stop=(k == KB - 1))
                last.then_inc(ring.used, 1)

        @block.vector
        def _(dve):
            for c in range(4):
                dve.wait_ge(ring.used, G_BRANCH + 2 * (c + 1))
                if c >= 2:
                    dve.wait_ge(merge_ready, c - 1)
                for n in range(2):
                    gate = proj[:, MERGE + 8 * n + 2 * c:MERGE + 8 * n + 2 * c + 2, :].rearrange("p b s -> p (b s)")
                    nc.vector.tensor_tensor(mt[:, c % 2, n, :], ps[:, 2 * (c % 2) + n, :], gate, ALU.mult).then_inc(up_used, 1)
                dve.wait_ge(up_used, 2 * (c + 1))
                nc.vector.tensor_tensor(merged[:, 2 * c:2 * c + 2, :].rearrange("p b s -> p (b s)"),
                                        mt[:, c % 2, 0, :], mt[:, c % 2, 1, :], ALU.add).then_inc(merge_ready, 1)
            for c in range(4):
                dve.wait_ge(ring.used, G_OUT + 2 * (c + 1))
                x = h[:, :, 256 * c:256 * (c + 1)]
                nc.vector.tensor_tensor(x, x, ps[:, 4 + c, :].rearrange("p (t c) -> p t c", t=NT), ALU.add).then_inc(res_done, 1)
    stack.close()
    return T.dump("h1", [h[:, :, :]])


def top16(T, dve, link, src, work, vals, idxs):
    nc = T.nc
    step = lambda f: [f(n) for n in range(len(src))][-1]
    link(step(lambda n: nc.vector.max(vals[n][:, 0:8], src[n])))
    step(lambda n: nc.vector.max_index(idxs[n][:, 0:8], vals[n][:, 0:8], src[n]))
    link(step(lambda n: nc.vector.match_replace(work[n], vals[n][:, 0:8], src[n], -3e38)))
    link(step(lambda n: nc.vector.max(vals[n][:, 8:16], work[n])))
    return link(step(lambda n: nc.vector.max_index(idxs[n][:, 8:16], vals[n][:, 8:16], work[n])))


def peer(T):
    nc, A, ps, sem, ring = T.nc, T.A, T.ps, T.sem, T.ring1
    h, hT, ident = T.h, T.hT, T.ident
    arena = T.arena
    HK = HEADS * TOPK
    outer = ExitStack()
    keyT = T.sb(outer, "keyT", [P, 3, S])

    stack = ExitStack()
    qT = arena[:, 0:16 * S].rearrange("p (h s) -> p h s", h=16)
    dst = qT.rearrange("p (n c) s -> p n (c s)", c=2)

    def refill(sync):
        for g in range(G_WQ + RING1, G_PEER):
            ring.issue(sync, g, T.stream1(g))

    front(T, "ffn", 1, ring, G_WQ, [("F", 8, dst, ACT.Copy)], lambda pe, done: None, refill)

    sc = arena[:, 4096:8192].rearrange("p (t n k) -> p t n k", t=NT, n=16)
    work = arena[:, 8192:12288].rearrange("p (t n k) -> p t n k", t=NT, n=16)
    cand = arena[:, 12288:14336].rearrange("p (h i j) -> p h i j", h=HEADS, i=TOPK)
    work2 = arena[:, 14336:16384].rearrange("p (h i) -> p h i", h=HEADS)
    eq = arena[:, 16384:18432].rearrange("p (m j) -> p m j", j=TOPK)
    v16 = T.sb(stack, "v16", [P, NT, 16, TOPK])
    i16 = T.sb(stack, "i16", [P, NT, 16, TOPK], U32)
    i16f = T.sb(stack, "i16f", [P, NT, 16, TOPK])
    top = T.sb(stack, "top", [P, NT, HEADS, TOPK])
    place = T.sb(stack, "place", [P, NT, HEADS, TOPK], U32)
    ab = T.sb(stack, "ab", [P, 2, HK], U32)
    abf = T.sb(stack, "abf", [P, 2, HK])
    key = T.sb(stack, "key", [P, NT, 3, HK])
    sm = T.sb(stack, "sm", [P, NT, HEADS])
    iota16 = T.sb(stack, "iota16", [P, TOPK])
    iota_loaded, sc_ps, sc_sb, w_sub, w_exp, key_ready, key_ps = (sem(n) for n in (
        "iota_loaded", "key_sc_ps", "key_sc_sb", "key_sub", "key_exp", "key_ready", "key_ps"))
    key_sb, high_ready, low_ready = sem("key_sb"), sem("h_high_ready"), sem("h_low_ready")
    with nc.Block() as block:
        @block.sync
        def _(sync):
            sync.dma_start(iota16[:, :], A["iota16"]).then_inc(iota_loaded, 16)

        @block.tensor
        def _(pe):
            for n in range(2):
                ring.arrived(pe, G_SUBK + n)
            for b in range(8):
                t, n0 = b // 4, 4 * (b % 4)
                for n in range(n0, n0 + 4):
                    sub = ring.piece(G_SUBK + n // 8).rearrange("p (h k) -> p h k", h=8)
                    last = nc.tensor.matmul(ps[:, b, (n - n0) * P:(n - n0 + 1) * P], qT[:, n, t * P:(t + 1) * P],
                                            sub[:, n % 8, :], start=True, stop=True)
                last.then_inc(sc_ps, 1)
            for t in range(NT):
                pe.wait_ge(key_ready, 3 * (t + 1))
                for c in range(3):
                    last = nc.tensor.transpose(ps[:, t, c * P:(c + 1) * P], key[:, t, c, :], ident[:, :])
                last.then_inc(key_ps, 1)

        @block.scalar
        def _(act):
            for b in range(8):
                t, n0 = b // 4, 4 * (b % 4)
                act.wait_ge(sc_ps, b + 1)
                nc.scalar.activation(sc[:, t, n0:n0 + 4, :], ps[:, b, :].rearrange("p (n k) -> p n k", n=4),
                                     ACT.Copy).then_inc(sc_sb, 1)
            nc.scalar.activation(T.parts[:, 0, :, :], hT[:, :, :], ACT.Copy).then_inc(high_ready, 1)
            for t in range(NT):
                act.wait_ge(w_sub, t + 1)
                nc.scalar.activation(key[:, t, 2, :], key[:, t, 2, :], ACT.Exp).then_inc(w_exp, 1)
            for t in range(NT):
                act.wait_ge(key_ps, t + 1)
                nc.scalar.activation(keyT[:, :, t * P:(t + 1) * P], ps[:, t, 0:3 * P].rearrange("p (c s) -> p c s", c=3),
                                     ACT.Copy).then_inc(key_sb, 1)

        @block.vector
        def _(dve):
            link = T.link(dve, "dve", T.chain_dve)
            dve.wait_ge(iota_loaded, 16)
            for t in range(NT):
                dve.wait_ge(sc_sb, 4 * (t + 1))
                top16(T, dve, link, [sc[:, t, n, :] for n in range(16)], [work[:, t, n, :] for n in range(16)],
                      [v16[:, t, n, :] for n in range(16)], [i16[:, t, n, :] for n in range(16)])
                nc.vector.tensor_copy(i16f[:, t, :, :], i16[:, t, :, :])
                halves = v16[:, t, :, :].rearrange("p (h c) k -> p h c k", c=2)
                if t:
                    dve.wait_ge(key_ready, 3 * t)
                full = [P, HEADS, TOPK, TOPK]
                link(nc.vector.tensor_tensor(cand[:, :, :, :], halves[:, :, 0, :].unsqueeze(3).broadcast_to(full),
                                             halves[:, :, 1, :].unsqueeze(2).broadcast_to(full), ALU.add))
                flat = cand[:, :, :, :].rearrange("p h i j -> p h (i j)")
                top16(T, dve, link, [flat[:, n, :] for n in range(HEADS)], [work2[:, n, :] for n in range(HEADS)],
                      [top[:, t, n, :] for n in range(HEADS)], [place[:, t, n, :] for n in range(HEADS)])
                flat_place = place[:, t, :, :].rearrange("p h k -> p (h k)")
                nc.vector.tensor_scalar(ab[:, 0, :], flat_place, 4, None, ALU.logical_shift_right)
                link(nc.vector.tensor_scalar(ab[:, 1, :], flat_place, 15, None, ALU.bitwise_and))
                link(nc.vector.tensor_copy(abf[:, :, :], ab[:, :, :]))
                if t == 0:
                    dve.wait_ge(high_ready, 1)
                    nc.vector.tensor_tensor(T.parts[:, 1, :, :], hT[:, :, :], T.parts[:, 0, :, :].bitcast(F32),
                                            ALU.subtract).then_inc(low_ready, 1)
                idx = i16f[:, t, :, :].rearrange("p (h c) k -> p h c k", c=2)
                for c in range(2):
                    link(nc.vector.tensor_tensor(eq[:, :, :], abf[:, c, :].unsqueeze(2).broadcast_to([P, HK, TOPK]),
                                                 iota16[:, :].unsqueeze(1).broadcast_to([P, HK, TOPK]), ALU.is_equal))
                    by_head = eq[:, :, :].rearrange("p (h k) j -> p h k j", h=HEADS)
                    link(nc.vector.tensor_tensor(by_head, by_head, idx[:, :, c, :].unsqueeze(2).broadcast_to(full), ALU.mult))
                    nc.vector.reduce_sum(key[:, t, c, :], eq[:, :, :], AX.X).then_inc(key_ready, 1)
                    dve.wait_ge(key_ready, 3 * t + c + 1)
                w = key[:, t, 2, :].rearrange("p (h k) -> p h k", h=HEADS)
                nc.vector.tensor_tensor(w, top[:, t, :, :], top[:, t, :, 0:1].broadcast_to([P, HEADS, TOPK]),
                                        ALU.subtract).then_inc(w_sub, 1)
                dve.wait_ge(w_exp, t + 1)
                link(nc.vector.reduce_sum(sm[:, t, :], w, AX.X))
                link(nc.vector.reciprocal(sm[:, t, :], sm[:, t, :]))
                nc.vector.tensor_tensor(w, w, sm[:, t, :].unsqueeze(2).broadcast_to([P, HEADS, TOPK]),
                                        ALU.mult).then_inc(key_ready, 1)
    stack.close()
    if T.dump("keys", [keyT[:, :, :], hT[:, :, :]]):
        outer.close()
        return True

    wt = arena[:, :].rearrange("p (a s) -> p a s", a=NKEYS)
    oh1 = T.sb(outer, "oh1", [P, 2, 4, NKEYS])
    oh2 = T.sb(outer, "oh2", [P, 2, 4, NKEYS])
    iota128 = T.sb(outer, "iota128", [P, NKEYS])
    i128_loaded, oh1_ready, oh2_ready, wt_ps, wt_sb = (sem(n) for n in (
        "i128_loaded", "oh1_ready", "oh2_ready", "wt_ps", "wt_sb"))
    with nc.Block() as block:
        @block.sync
        def _(sync):
            sync.dma_start(iota128[:, :], A["iota128"]).then_inc(i128_loaded, 16)
            for g in range(G_PEER, G_PEER + RING1):
                sync.dma_start(ring.piece(g), A["peer"][(g - G_PEER) // 2, (g - G_PEER) % 2]).then_inc(ring.loaded[g % RING1], 16)

        steps = S // 4

        def tokens(eng, body):
            for r in range(2):
                body(r, r, 0, True)
            with eng.Fori(1, steps // 2) as i:
                for r in range(2):
                    body(i * 2 + r, r, i, False)

        @block.vector
        def _(dve):
            dve.wait_ge(i128_loaded, 16)

            def body(n, r, i, first):
                if not first:
                    dve.wait_ge(wt_ps, i * 2 + (r - 1))
                base = n * 4
                for q in range(4):
                    last = nc.vector.tensor_scalar(oh2[:, r, q, :], iota128[:, :], keyT[:, 1, bass.ds(base + q, 1)], None, ALU.is_equal)
                last.then_inc(oh2_ready, 1)
                for q in range(4):
                    last = nc.vector.tensor_scalar(oh1[:, r, q, :], iota128[:, :], keyT[:, 0, bass.ds(base + q, 1)],
                                                   keyT[:, 2, bass.ds(base + q, 1)], ALU.is_equal, ALU.mult)
                last.then_inc(oh1_ready, 1)
            tokens(dve, body)

        @block.tensor
        def _(pe):
            def body(n, r, i, first):
                pe.wait_ge(oh2_ready, i * 2 + (r + 1))
                pe.wait_ge(oh1_ready, i * 2 + (r + 1))
                if not first:
                    pe.wait_ge(wt_sb, i * 2 + (r - 1))
                for q in range(4):
                    last = nc.tensor.matmul(ps[:, r, q * P:(q + 1) * P], oh2[:, r, q, :], oh1[:, r, q, :], start=True, stop=True)
                last.then_inc(wt_ps, 1)
            tokens(pe, body)

        @block.scalar
        def _(act):
            def body(n, r, i, first):
                act.wait_ge(wt_ps, i * 2 + (r + 1))
                nc.scalar.activation(wt[:, :, bass.ds(n * 4, 4)].rearrange("p a s -> p s a"),
                                     ps[:, r, :].rearrange("p (s a) -> p s a", s=4), ACT.Copy).then_inc(wt_sb, 1)
            tokens(act, body)
    if T.dump("wt", [wt]):
        outer.close()
        return True

    outer.close()
    T.hT_stack.close()
    stack = ExitStack()
    part = lambda name, *shape: stack.enter_context(nc.sbuf_tensor(name, [P, *shape], F32R))
    uh, ul, vh, vl = (part(n, 2, HW) for n in ("u_high", "u_low", "v_high", "v_low"))
    ch, cl = part("coef_high", 2, S), part("coef_low", 2, S)
    coef = T.sb(stack, "coef", [P, 2, S])
    names = ("uh", "ul", "vh", "vl", "a_ps", "gelu", "coef", "ch", "cl", "o_done", "res")
    uh_ready, ul_ready, vh_ready, vl_ready, a_ps, gelu_ready, coef_ready, ch_ready, cl_ready, o_done, peer_res = (
        sem(f"peer_{n}") for n in names)
    raw_u = lambda r: ring.piece(G_PEER + 2 * (r % 2))
    raw_v = lambda r: ring.piece(G_PEER + 2 * (r % 2) + 1)
    TURNS = NKEYS // 2

    def steps(eng, step):
        step(0, 0, 2)
        step(1, 0, 2)
        with eng.Fori(1, TURNS - 1) as i:
            step(0, i, 2)
            step(1, i, 2)
        step(0, TURNS - 1, 1)
        step(1, TURNS - 1, 0)

    is_first = lambda n: isinstance(n, int) and n == 0

    with nc.Block() as block:
        @block.sync
        def _(sync):
            with sync.Fori(1, TURNS) as i:
                for r in range(4):
                    sync.wait_ge(vl_ready if r % 2 else ul_ready, i * 2 + (r // 2 - 1))
                    sync.dma_start(ring.piece(G_PEER + r), A["peer"][i * 2 + r // 2, r % 2]).then_inc(ring.loaded[(G_PEER + r) % RING1], 16)

        @block.scalar
        def _(act):
            def u_high(r, turn):
                ring.arrived(act, G_PEER + 2 * (r % 2), turn)
                nc.scalar.activation(uh[:, r % 2, :], raw_u(r), ACT.Copy).then_inc(uh_ready, 1)

            def v_high(r, turn):
                ring.arrived(act, G_PEER + 2 * (r % 2) + 1, turn)
                nc.scalar.activation(vh[:, r % 2, :], raw_v(r), ACT.Copy).then_inc(vh_ready, 1)

            def activate(r, n):
                act.wait_ge(a_ps, n + 1)
                nc.scalar.activation(coef[:, r % 2, :], ps[:, 4 + r % 2, 0:S], ACT.Gelu).then_inc(gelu_ready, 1)
                act.wait_ge(coef_ready, n + 1)
                nc.scalar.activation(ch[:, r % 2, :], coef[:, r % 2, :], ACT.Copy).then_inc(ch_ready, 1)

            u_high(0, 0)
            u_high(1, 0)
            v_high(0, 0)
            activate(0, 0)

            def step(r, i, into):
                n = i * 2 + r
                if into == 2:
                    act.wait_ge(a_ps, n + 1)
                    u_high(r, i + 1)
                if into:
                    if not is_first(n):
                        act.wait_ge(o_done, n)
                    v_high(r + 1, i + (r + 1) // 2)
                    activate(r + 1, n + 1)
            steps(act, step)

        @block.vector
        def _(dve):
            def u_low(r, n):
                dve.wait_ge(uh_ready, n + 1)
                nc.vector.tensor_tensor(ul[:, r % 2, :], raw_u(r), uh[:, r % 2, :].bitcast(F32), ALU.subtract).then_inc(ul_ready, 1)

            def v_low(r, n):
                dve.wait_ge(vh_ready, n + 1)
                nc.vector.tensor_tensor(vl[:, r % 2, :], raw_v(r), vh[:, r % 2, :].bitcast(F32), ALU.subtract).then_inc(vl_ready, 1)

            def weigh(r, n):
                dve.wait_ge(gelu_ready, n + 1)
                c = coef[:, r % 2, :]
                nc.vector.tensor_tensor(c, c, wt[:, bass.ds(n, 1), :].rearrange("p a s -> p (a s)"), ALU.mult).then_inc(coef_ready, 1)
                dve.wait_ge(ch_ready, n + 1)
                nc.vector.tensor_tensor(cl[:, r % 2, :], c, ch[:, r % 2, :].bitcast(F32), ALU.subtract).then_inc(cl_ready, 1)

            u_low(0, 0)
            u_low(1, 1)
            v_low(0, 0)
            weigh(0, 0)

            def step(r, i, into):
                n = i * 2 + r
                if into == 2:
                    u_low(r, n + 2)
                if into:
                    v_low(r + 1, n + 1)
                    weigh(r + 1, n + 1)
            steps(dve, step)
            dve.wait_ge(o_done, NKEYS)
            for t in range(NT):
                nc.vector.tensor_tensor(h[:, t, :], h[:, t, :], ps[:, 2 * t:2 * t + 2, :].rearrange("p b d -> p (b d)"),
                                        ALU.add).then_inc(peer_res, 1)

        @block.tensor
        def _(pe):
            xh, xl = T.parts[:, 0, :, :], T.parts[:, 1, :, :]

            def expert_in(r, n):
                pe.wait_ge(ul_ready, n + 1)
                b = r % 2
                wh, wl = (x[:, b, :].rearrange("p (k e) -> p k e", k=KB) for x in (uh, ul))
                for k in range(KB):
                    for m, (w, x) in enumerate(((wh, xh), (wh, xl), (wl, xh))):
                        last = nc.tensor.matmul(ps[:, 4 + b, 0:S], w[:, k, :], x[:, k, :], start=(k == 0 and m == 0),
                                                stop=(k == KB - 1 and m == 2))
                last.then_inc(a_ps, 1)

            def expert_out(r, n, final):
                pe.wait_ge(vl_ready, n + 1)
                pe.wait_ge(cl_ready, n + 1)
                b = r % 2
                for t in range(NT):
                    for m, (cc, w) in enumerate(((ch, vh), (ch, vl), (cl, vh))):
                        for half in range(2):
                            last = nc.tensor.matmul(ps[:, 2 * t + half, :], cc[:, b, t * P:(t + 1) * P],
                                                    w[:, b, half * BANK:(half + 1) * BANK], start=(m == 0 and is_first(n)),
                                                    stop=(m == 2 and final), skip_group_check=True)
                last.then_inc(o_done, 1)

            expert_in(0, 0)

            def step(r, i, into):
                n = i * 2 + r
                if into:
                    expert_in(r + 1, n + 1)
                expert_out(r, n, into == 0)
            steps(pe, step)
    stack.close()
    return T.dump("h2", [h[:, :, :]])


def norm_tokens(T, name, sync_extra=None, add_banks=False, store=None):
    nc, A, ps, sem, h, ss = T.nc, T.A, T.ps, T.sem, T.h, T.ss
    stack = ExitStack()
    gain = T.sb(stack, f"{name}_gain", [P, D])
    junk = T.sb(stack, f"{name}_junk", [P, D])
    gain_loaded, summed, squares, mean, root, normed, out_stored = (sem(f"{name}_{s}") for s in (
        "gain_loaded", "summed", "squares", "mean", "root", "normed", "stored"))
    with nc.Block() as block:
        @block.sync
        def _(sync):
            sync.dma_start(gain[:, :], A[name]).then_inc(gain_loaded, 16)
            if sync_extra:
                sync_extra(sync)
            if store is not None:
                for t in range(NT):
                    sync.wait_ge(normed, t + 1)
                    sync.dma_start(store[t * P:(t + 1) * P, :], h[:, t, :]).then_inc(out_stored, 16)
                sync.wait_ge(out_stored, 16 * NT)

        @block.scalar
        def _(act):
            if add_banks:
                act.wait_ge(summed, NT)
            for t in range(NT):
                nc.scalar.activation(junk[:, :], h[:, t, :], ACT.Square, accum_out=ss[:, t:t + 1]).then_inc(squares, 1)
                act.wait_ge(squares, t + 1)
            act.wait_ge(mean, 1)
            nc.scalar.activation(ss[:, 2:4], ss[:, 2:4], ACT.Sqrt).then_inc(root, 1)

        @block.vector
        def _(dve):
            link = T.link(dve, "dve", T.chain_dve)
            if add_banks:
                for t in range(NT):
                    nc.vector.tensor_tensor(h[:, t, :], h[:, t, :], ps[:, 2 * t:2 * t + 2, :].rearrange("p b d -> p (b d)"),
                                            ALU.add).then_inc(summed, 1)
                dve.wait_ge(summed, NT)
            dve.wait_ge(squares, NT)
            nc.vector.tensor_scalar(ss[:, 2:4], ss[:, 0:2], 1.0 / D, EPS, ALU.mult, ALU.add).then_inc(mean, 1)
            dve.wait_ge(root, 1)
            link(nc.vector.reciprocal(ss[:, 2:4], ss[:, 2:4]))
            dve.wait_ge(gain_loaded, 16)
            for t in range(NT):
                nc.vector.scalar_tensor_tensor(h[:, t, :], h[:, t, :], ss[:, 2 + t:3 + t], gain[:, :], ALU.mult,
                                               ALU.mult).then_inc(normed, 1)
    stack.close()


DHEADS, DK, CH = 4, 128, 64
NU = NT * 2 * DHEADS
G2_OUT, G2_EXP = 10, 14
LEVELS = 6


def second_block(T):
    nc, A, ps, sem = T.nc, T.A, T.ps, T.sem
    h, hT, ident = T.h, T.hT, T.ident
    ring = T.ring2 = Ring(T.arena[:, 0:RING2 * PW].rearrange("p (n c) -> p n c", n=RING2), RING2, *T.ring2_sems)
    low = T.low[:, :]
    high = T.arena[:, RING2 * PW:]

    def start_ring(sync):
        for g in range(RING2):
            ring.issue(sync, g, A["stream2"][g])

    norm_tokens(T, "norm_final", start_ring)
    if T.dump("x2", [h[:, :, :]]):
        return True

    stack = ExitStack()
    sb = lambda name, *shape: T.sb(stack, name, [P, *shape])
    low_c, high_c = Carve(low), Carve(high)
    qkv = low_c(12, S)
    xs = low_c(NT, D)
    sq = low_c(8, S)
    utok = high_c(2, NT, 256)
    high_c(1024)
    pool_m = high_c(NT, 4, S)
    more = Carve(high[:, 8192:])
    vT = more(DHEADS, S)
    rn = more(8, S)
    dp = more(4, S)
    z = more(DHEADS, S)
    oT = more(KB, S)
    masks = sb("masks", 2, LEVELS + 1, P)
    same_chunk = sb("same_chunk", P)
    ones = sb("ones", P)
    conv_w = sb("conv_w", 12, 5)
    ab_w = sb("ab_w", KB, 16)
    pool_w = sb("pool_w", 4, P)
    pool_scale = sb("pool_scale", 4)
    head_norm = sb("head_norm", 1)
    a_log = sb("a_log", 8)
    dt_bias = sb("dt_bias", 8)
    tok2 = sb("tok2", 2, NT, DHEADS, P)
    loads = [(pool_m, "pool_m"), (masks[:, :, :, :], "masks"), (same_chunk[:, :], "same_chunk"), (ones[:, :], "ones"),
             (conv_w[:, :, :], "conv_w"), (ab_w[:, :, :], "ab_w"), (pool_w[:, :, :], "pool_w"),
             (pool_scale[:, :], "pool_scale"), (head_norm[:, :], "head_norm"), (a_log[:, :], "a_log"),
             (dt_bias[:, :], "dt_bias")]
    c2 = sem("second_consts")

    def refill(sync):
        for dst, name in loads:
            sync.dma_start(dst, A[name]).then_inc(c2, 16)
        for g in range(RING2, G2_OUT + RING2):
            ring.issue(sync, g, T.stream2(g))

    def small(pe, done):
        pe.wait_ge(c2, 16 * len(loads))
        for t in range(NT):
            for k in range(KB):
                last = nc.tensor.matmul(ps[:, 4, t * 16:(t + 1) * 16], hT[:, k, t * P:(t + 1) * P], ab_w[:, k, :],
                                        start=(k == 0), stop=(k == KB - 1))
        last.then_inc(done, 1)

    front(T, "mix2", 2, ring, 0, [("F", 6, qkv.rearrange("p (n c) s -> p n (c s)", c=2), ACT.Copy),
                                  ("F", 2, z[:, :, :].rearrange("p (n c) s -> p n (c s)", c=2), ACT.Silu),
                                  ("T", 2, utok.rearrange("p n t c -> p n (t c)"), ACT.Copy)], small, refill, xs=xs)

    qk_high = Carve(high)
    qk_high(6144)
    qkT = qk_high(2, DHEADS, S)
    part = lambda i: (qkT[:, i, :, :], qkT[:, i, :, :], vT[:, :, :])[i] if i < 2 else vT[:, :, :]
    abr = sb("abr", 6, NT, 2, DHEADS)
    beta, g_ = abr[:, 4, :, :, :], abr[:, 5, :, :, :]
    centre, conv_done, silu_done, sq_ready, ss_ps, ss_sb, root, kv_ready, kv_ps, kv_sb = (sem(f"conv_{n}") for n in (
        "centre", "done", "silu", "sq", "ss_ps", "ss_sb", "root", "ready", "kv_ps", "kv_sb"))
    pool_ps, pool_sb, pool2_ps, g_in, g_exp, al_exp, a_in = (sem(f"pl_{n}") for n in ("ps", "sb", "ps2", "g_in", "g_exp", "al_exp", "a_in"))
    with nc.Block() as block:
        @block.scalar
        def _(act):
            link = T.link(act, "act", T.chain_act)
            for b in range(12):
                nc.scalar.activation(part(b // 4)[:, b % 4, :], qkv[:, b, :], ACT.Copy, scale=conv_w[:, b, 2:3]).then_inc(centre, 1)
            ab = ps[:, 4, 0:32].rearrange("p (t d c h) -> p t d c h", t=NT, d=2, c=2)
            nc.scalar.activation(beta, ab[:, :, :, 1, :], ACT.Sigmoid)
            nc.scalar.activation(abr[:, 0, :, :, :], ab[:, :, :, 0, :], ACT.Copy).then_inc(a_in, 1)
            act.wait_ge(g_in, 1)
            link(nc.scalar.activation(abr[:, 1, :, :, :], abr[:, 0, :, :, :], ACT.Abs))
            link(nc.scalar.activation(abr[:, 1, :, :, :], abr[:, 1, :, :, :], ACT.Exp, scale=-1.0))
            nc.scalar.activation(abr[:, 1, :, :, :], abr[:, 1, :, :, :], ACT.Ln, bias=1.0).then_inc(g_exp, 1)
            nc.scalar.activation(a_log[:, :], a_log[:, :], ACT.Exp).then_inc(al_exp, 1)
            for i in range(3):
                act.wait_ge(conv_done, i + 1)
                nc.scalar.activation(part(i), part(i), ACT.Silu).then_inc(silu_done, 1)
            act.wait_ge(ss_sb, 1)
            nc.scalar.activation(rn[:, :, :], rn[:, :, :], ACT.Sqrt).then_inc(root, 1)
            for b in range(4):
                act.wait_ge(kv_ps, b + 1)
                nc.scalar.activation(tok2[:, b // 2, b % 2, :, :], ps[:, 4 + b, :].rearrange("p (h d) -> p h d", h=DHEADS),
                                     ACT.Copy).then_inc(kv_sb, 1)
            act.wait_ge(pool_ps, 4)
            nc.scalar.activation(dp[:, :, :].rearrange("p g s -> p (g s)"), ps[:, 0:2, :].rearrange("p b c -> p (b c)"),
                                 ACT.Copy).then_inc(pool_sb, 1)
            act.wait_ge(pool2_ps, 1)
            for i in range(4):
                nc.scalar.activation(oT[:, 4 + i, :], ps[:, 2 + i // 2, (i % 2) * S:(i % 2 + 1) * S], ACT.Copy, scale=pool_scale[:, i:i + 1])

        @block.vector
        def _(dve):
            link = T.link(dve, "dve", T.chain_dve)
            dve.wait_ge(a_in, 1)
            dtb = dt_bias[:, :].rearrange("p (d h) -> p d h", d=2).unsqueeze(1).broadcast_to([P, NT, 2, DHEADS])
            nc.vector.tensor_tensor(abr[:, 0, :, :, :], abr[:, 0, :, :, :], dtb, ALU.add).then_inc(g_in, 1)
            dve.wait_ge(g_in, 1)
            dve.wait_ge(g_exp, 1)
            link(nc.vector.scalar_tensor_tensor(abr[:, 2, :, :, :], abr[:, 0, :, :, :], 0.0, abr[:, 1, :, :, :], ALU.max, ALU.add))
            dve.wait_ge(al_exp, 1)
            alb = a_log[:, :].rearrange("p (d h) -> p d h", d=2).unsqueeze(1).broadcast_to([P, NT, 2, DHEADS])
            link(nc.vector.scalar_tensor_tensor(g_, abr[:, 2, :, :, :], -1.0, alb, ALU.mult, ALU.mult))
            for i in range(3):
                dve.wait_ge(centre, 4 * (i + 1))
                for tap in (0, 1, 3, 4):
                    off = tap - 2
                    lo, hi = max(0, -off), min(S, S - off)
                    for b in range(4 * i, 4 * i + 4):
                        y = part(i)[:, b % 4, lo:hi]
                        last = nc.vector.scalar_tensor_tensor(y, qkv[:, b, lo + off:hi + off], conv_w[:, b, tap:tap + 1], y,
                                                              ALU.mult, ALU.add)
                    if tap < 4:
                        link(last)
                    else:
                        last.then_inc(conv_done, 1)
            dve.wait_ge(silu_done, 2)
            flat = qkT.rearrange("p c h s -> p (c h) s")
            nc.vector.tensor_tensor(sq, flat, flat, ALU.mult).then_inc(sq_ready, 1)
            dve.wait_ge(ss_ps, 1)
            nc.vector.tensor_scalar(rn[:, :, :].rearrange("p a s -> p (a s)"), ps[:, 0:4, :].rearrange("p b c -> p (b c)"),
                                    EPS, None, ALU.add).then_inc(ss_sb, 1)
            dve.wait_ge(root, 1)
            link(nc.vector.reciprocal(rn[:, :, :], rn[:, :, :]))
            nc.vector.scalar_tensor_tensor(flat[:, 0:4, :], flat[:, 0:4, :], DK ** -0.5, rn[:, 0:4, :], ALU.mult, ALU.mult)
            nc.vector.tensor_tensor(flat[:, 4:8, :], flat[:, 4:8, :], rn[:, 4:8, :], ALU.mult).then_inc(kv_ready, 1)

        @block.tensor
        def _(pe):
            pe.wait_ge(sq_ready, 1)
            for b in range(4):
                last = nc.tensor.matmul(ps[:, b, :], ones[:, :], sq[:, 2 * b:2 * b + 2, :].rearrange("p a s -> p (a s)"),
                                        start=True, stop=True)
            last.then_inc(ss_ps, 1)
            pe.wait_ge(kv_ready, 1)
            pe.wait_ge(silu_done, 3)
            for b in range(4):
                src = (qkT[:, 1, :, :], vT[:, :, :])[b // 2]
                for hd in range(DHEADS):
                    last = nc.tensor.transpose(ps[:, 4 + b, hd * P:(hd + 1) * P], src[:, hd, (b % 2) * P:(b % 2 + 1) * P], ident[:, :])
                last.then_inc(kv_ps, 1)
            for i in range(4):
                for t in range(NT):
                    last = nc.tensor.matmul(ps[:, i // 2, (i % 2) * S:(i % 2 + 1) * S], utok[:, i // 2, t, (i % 2) * P:(i % 2 + 1) * P],
                                            pool_m[:, t, i, :], start=(t == 0), stop=(t == NT - 1))
                last.then_inc(pool_ps, 1)
            pe.wait_ge(pool_sb, 1)
            for i in range(4):
                last = nc.tensor.matmul(ps[:, 2 + i // 2, (i % 2) * S:(i % 2 + 1) * S], pool_w[:, i, :], dp[:, i, :], start=True, stop=True)
            last.then_inc(pool2_ps, 1)
    if T.dump("conv", [qkT[:, :, :, :], vT[:, :, :], oT[:, 4:8, :], abr[:, 4:6, :, :, :]]):
        return True
    return delta(T, stack, z, oT, masks, same_chunk, ones, head_norm, tok2, qkT, beta, g_)


def delta(T, stack, z, oT, masks, same_chunk, ones, head_norm, tok2, qkT, beta, g_):
    nc, A, ps, sem = T.nc, T.A, T.ps, T.sem
    h, ident, ring = T.h, T.ident, T.ring2
    low_c = Carve(T.low[:, :])
    high_c = Carve(T.arena[:, RING2 * PW:])
    kb_, vb, kdec, qdec = (low_c(NU, P) for _ in range(4))
    at, qkm, eg = (high_c(NU, P) for _ in range(3))
    x_, xT = eg, high_c(NU, P)
    gbc, bbc = kb_, vb
    scal = T.sb(stack, "scal", [P, 6, NU])
    egl = T.sb(stack, "egl", [P, NT, 2, 2, DHEADS])
    grp = lambda x, b: x[:, 4 * b:4 * b + 4, :]
    bank4 = lambda b: ps[:, b, :].rearrange("p (h c) -> p h c", h=DHEADS)
    inc = lambda d: masks[:, d, LEVELS, :]
    names = ("bc_ready", "cum_ps", "scal_sb", "scal_exp", "row_ps", "eg_ready", "d2_in", "d2_ready", "brow_used", "kq_ps", "at_ready",
             "egl_ready", "mats_ready")
    bc_ready, cum_ps, scal_sb, scal_exp, row_ps, eg_ready, d2_in, d2_ready, brow_used, kq_ps, at_ready, egl_ready, mats_ready = (
        sem(f"dl_{n}") for n in names)
    all_units = lambda x: x.rearrange("p t d h -> p (t d h)")
    with nc.Block() as block:
        @block.vector
        def _(dve):
            link = T.link(dve, "dve", T.chain_dve)
            nc.vector.tensor_copy(gbc, all_units(g_).unsqueeze(2).broadcast_to([P, NU, P])).then_inc(bc_ready, 1)
            nc.vector.tensor_copy(bbc, all_units(beta).unsqueeze(2).broadcast_to([P, NU, P])).then_inc(bc_ready, 1)
            dve.wait_ge(cum_ps, 1)
            link(nc.vector.tensor_copy(scal[:, 0:2, :].rearrange("p a u -> p (a u)"), ps[:, 0, 0:2 * NU]))
            nc.vector.tensor_tensor(scal[:, 2, :], scal[:, 1, :], scal[:, 0, :], ALU.subtract).then_inc(scal_sb, 1)
            for b in range(4):
                dve.wait_ge(row_ps, b + 1)
                dve.wait_ge(eg_ready, b + 1)
                for u in range(4 * b, 4 * b + 4):
                    last = nc.vector.tensor_scalar(qkm[:, u, :], ps[:, b, (u % 4) * P:(u % 4 + 1) * P], scal[:, 0, u:u + 1], 0.0,
                                                   ALU.subtract, ALU.min)
                last.then_inc(d2_in, 1)
            for b in range(4):
                dve.wait_ge(d2_ready, b + 1)
                dve.wait_ge(row_ps, 4 + b + 1)
                nc.vector.tensor_tensor(grp(at, b), grp(qkm, b), bank4(4 + b), ALU.mult).then_inc(brow_used, 1)
            dve.wait_ge(brow_used, 4)
            for b in range(4):
                dve.wait_ge(kq_ps, 2 * (b // 2) + 1)
                nc.vector.tensor_tensor(grp(at, b), grp(at, b), bank4(b // 2), ALU.mult).then_inc(at_ready, 1)
                dve.wait_ge(kq_ps, 2 * (b // 2) + 2)
                link(nc.vector.tensor_tensor(grp(qkm, b), grp(qkm, b), bank4(2 + b // 2), ALU.mult))
                nc.vector.tensor_tensor(grp(qkm, b), grp(qkm, b), inc(b % 2).unsqueeze(1).broadcast_to([P, 4, P]), ALU.mult)
            dve.wait_ge(scal_exp, 2)
            link(nc.vector.tensor_tensor(scal[:, 3, :], scal[:, 4, :], all_units(beta), ALU.mult))
            for b in range(4):
                t = b // 2
                bc = lambda r: scal[:, r, 4 * b:4 * b + 4].unsqueeze(2).broadcast_to([P, 4, P])
                nc.vector.tensor_tensor(grp(kb_, b), tok2[:, 0, t, :, :], bc(3), ALU.mult)
                nc.vector.tensor_tensor(grp(vb, b), tok2[:, 1, t, :, :],
                                        all_units(beta)[:, 4 * b:4 * b + 4].unsqueeze(2).broadcast_to([P, 4, P]), ALU.mult).then_inc(mats_ready, 1)

        @block.gpsimd
        def _(pool):
            pool.wait_ge(eg_ready, 4)
            for d in range(2):
                for t in range(NT):
                    u = (2 * t + d) * 4
                    col = 63 if d == 0 else 0
                    ends = eg[:, u:u + 4, :].rearrange("p h (c s) -> p c h s", c=2)[:, :, :, col]
                    last = nc.gpsimd.tensor_copy(egl[:, t, d, :, :], ends)
            last.then_inc(egl_ready, 1)
            for b in range(4):
                nc.gpsimd.tensor_tensor(grp(qdec, b), qkT[:, 0, :, (b // 2) * P:(b // 2 + 1) * P], grp(eg, b), ALU.mult)
            pool.wait_ge(scal_exp, 2)
            for b in range(4):
                nc.gpsimd.tensor_tensor(grp(kdec, b), tok2[:, 0, b // 2, :, :],
                                        scal[:, 2, 4 * b:4 * b + 4].unsqueeze(2).broadcast_to([P, 4, P]), ALU.mult)

        @block.scalar
        def _(act):
            for b in range(4):
                act.wait_ge(row_ps, b + 1)
                nc.scalar.activation(grp(eg, b), bank4(b), ACT.Exp).then_inc(eg_ready, 1)
            act.wait_ge(scal_sb, 1)
            nc.scalar.activation(scal[:, 2, :], scal[:, 2, :], ACT.Exp).then_inc(scal_exp, 1)
            nc.scalar.activation(scal[:, 4, :], scal[:, 0, :], ACT.Exp).then_inc(scal_exp, 1)
            for b in range(4):
                act.wait_ge(d2_in, b + 1)
                nc.scalar.activation(grp(qkm, b), grp(qkm, b), ACT.Exp).then_inc(d2_ready, 1)

        @block.tensor
        def _(pe):
            for t in range(NT):
                for d in range(2):
                    u = (2 * t + d) * 4
                    nc.tensor.matmul(ps[:, 0, u:u + 4], inc(d), g_[:, t, d, :], start=True, stop=True)
            nc.tensor.matmul(ps[:, 0, NU:2 * NU], same_chunk[:, :], all_units(g_), start=True, stop=True).then_inc(cum_ps, 1)
            pe.wait_ge(bc_ready, 2)
            pe.wait_ge(scal_sb, 1)
            for b in range(4):
                for u in range(4 * b, 4 * b + 4):
                    last = nc.tensor.matmul(ps[:, b, (u % 4) * P:(u % 4 + 1) * P], gbc[:, u, :], inc(b % 2), start=True, stop=True)
                last.then_inc(row_ps, 1)
            for b in range(4):
                for u in range(4 * b, 4 * b + 4):
                    last = nc.tensor.matmul(ps[:, 4 + b, (u % 4) * P:(u % 4 + 1) * P], bbc[:, u, :], ident[:, :], start=True, stop=True)
                last.then_inc(row_ps, 1)
            pe.wait_ge(d2_in, 4)
            for t in range(NT):
                for c in range(2):
                    for hd in range(DHEADS):
                        cols = slice(t * P, (t + 1) * P)
                        last = nc.tensor.matmul(ps[:, 2 * c + t, hd * P:(hd + 1) * P], qkT[:, 1, hd, cols], qkT[:, 1 - c, hd, cols],
                                                start=True, stop=True)
                    last.then_inc(kq_ps, 1)
    if T.dump("mats", [at, qkm]):
        return True

    low_tri = tok2[:, 0, :, :, :].rearrange("p t h d -> p (t h) d")
    low_p = tok2[:, 1, :, :, :].rearrange("p t h d -> p (t h) d")
    alt = lambda n: low_tri[:, 4 * (n % 2):4 * (n % 2) + 4, :]
    pb = lambda n: low_p[:, 4 * (n % 2):4 * (n % 2) + 4, :]
    alt_ready, p_ps, p_sb, xx_ps, x_done = (sem(f"inv_{n}") for n in ("alt", "p_ps", "p_sb", "xx_ps", "x_done"))
    STEPS = 4 * LEVELS
    with nc.Block() as block:
        @block.gpsimd
        def _(pool):
            for n in range(STEPS):
                lev, b = n // 4, n % 4
                if n >= 2:
                    pool.wait_ge(p_ps, n - 1)
                if 2 <= n < 6:
                    pool.wait_ge(x_done, 2 * (n - 1))
                nc.gpsimd.tensor_tensor(alt(n), grp(at, b), masks[:, b % 2, lev, :].unsqueeze(1).broadcast_to([P, 4, P]),
                                        ALU.mult).then_inc(alt_ready, 1)

        @block.tensor
        def _(pe):
            def inner(n):
                lev, b = n // 4, n % 4
                pe.wait_ge(alt_ready, n + 1)
                if n >= 2:
                    if n - 2 < 4:
                        pe.wait_ge(x_done, 2 * (n - 1))
                    else:
                        pe.wait_ge(p_sb, n - 5)
                if lev:
                    pe.wait_ge(x_done, 2 * (n - 3))
                for q in range(4):
                    rhs = grp(x_, b)[:, q, :] if lev else ident[:, :]
                    last = nc.tensor.matmul(ps[:, n % 2, q * P:(q + 1) * P], alt(n)[:, q, :], rhs, start=True, stop=True)
                last.then_inc(p_ps, 1)

            def outer(n):
                lev, b = n // 4, n % 4
                if lev == 0:
                    return
                pe.wait_ge(p_sb, n - 3)
                if n - 2 >= 4:
                    pe.wait_ge(x_done, 2 * (n - 1))
                for q in range(4):
                    last = nc.tensor.matmul(ps[:, 2 + 2 * (n % 2), q * P:(q + 1) * P], grp(xT, b)[:, q, :], pb(n)[:, q, :], start=True, stop=True)
                for q in range(4):
                    last = nc.tensor.matmul(ps[:, 3 + 2 * (n % 2), q * P:(q + 1) * P], pb(n)[:, q, :], grp(xT, b)[:, q, :], start=True, stop=True)
                last.then_inc(xx_ps, 1)

            inner(0)
            for n in range(STEPS):
                if n + 1 < STEPS:
                    inner(n + 1)
                outer(n)

        @block.scalar
        def _(act):
            for n in range(4, STEPS):
                act.wait_ge(p_ps, n + 1)
                if n >= 6:
                    act.wait_ge(xx_ps, n - 5)
                nc.scalar.activation(pb(n), bank4(n % 2), ACT.Copy).then_inc(p_sb, 1)

        @block.vector
        def _(dve):
            eye = ident[:, :].unsqueeze(1).broadcast_to([P, 4, P])
            for n in range(STEPS):
                lev, b = n // 4, n % 4
                if lev == 0:
                    dve.wait_ge(p_ps, n + 1)
                    nc.vector.tensor_tensor(grp(x_, b), eye, bank4(n % 2), ALU.subtract).then_inc(x_done, 1)
                    dve.wait_ge(alt_ready, n + 1)
                    nc.vector.tensor_tensor(grp(xT, b), eye, alt(n), ALU.subtract).then_inc(x_done, 1)
                else:
                    dve.wait_ge(xx_ps, n - 3)
                    dve.wait_ge(x_done, 2 * (n - 3))
                    nc.vector.tensor_tensor(grp(x_, b), grp(x_, b), bank4(2 + 2 * (n % 2)), ALU.subtract).then_inc(x_done, 1)
                    nc.vector.tensor_tensor(grp(xT, b), grp(xT, b), bank4(3 + 2 * (n % 2)), ALU.subtract).then_inc(x_done, 1)
    if T.dump("inv", [xT]):
        return True

    wT, u_ = at, x_
    vnew = tok2[:, 0, :, :, :]
    state = tok2[:, 1, :, :, :]
    od = Carve(T.arena[:, RING2 * PW + 8192:])(2, DHEADS, S)
    wu_ps, w_sb, u_sb, v_ps, v_sb, s_ps, s_sb, o_ps, o_sb, o_sum, on_sq, on_ps, on_ms, on_rt, on_r, o_ready = (sem(f"scan_{n}") for n in (
        "wu_ps", "w_sb", "u_sb", "v_ps", "v_sb", "s_ps", "s_sb", "o_ps", "o_sb", "o_sum", "on_sq", "on_ps", "on_ms", "on_rt", "on_r", "o_ready"))
    steps = [(st, d) for st in range(4) for d in range(2)]

    def place(st, d):
        c = st if d == 0 else 3 - st
        t, lo = c // 2, CH * (c % 2)
        return c, (2 * t + d) * 4, slice(lo, lo + CH), t, c % 2

    with nc.Block() as block:
        @block.tensor
        def _(pe):
            for b in range(4):
                for q in range(4):
                    u = 4 * b + q
                    last = nc.tensor.matmul(ps[:, 2 * (b % 2), q * P:(q + 1) * P], kb_[:, u, :], xT[:, u, :], start=True, stop=True)
                last.then_inc(wu_ps, 1)
                for q in range(4):
                    u = 4 * b + q
                    last = nc.tensor.matmul(ps[:, 2 * (b % 2) + 1, q * P:(q + 1) * P], xT[:, u, :], vb[:, u, :], start=True, stop=True)
                last.then_inc(wu_ps, 1)
                if b >= 1:
                    pe.wait_ge(w_sb, b)
                    pe.wait_ge(u_sb, b)
            pe.wait_ge(w_sb, 4)
            for n, (st, d) in enumerate(steps):
                c, u0, cols, t, half = place(st, d)
                if st:
                    pe.wait_ge(s_sb, n - 1)
                    for q in range(4):
                        last = nc.tensor.matmul(ps[cols, 2 + d, q * P:(q + 1) * P], wT[:, u0 + q, cols], state[:, d, q, :], start=True, stop=True)
                    last.then_inc(v_ps, 1)
                pe.wait_ge(v_sb, n + 1)
                if st < 3:
                    for q in range(4):
                        last = nc.tensor.matmul(ps[:, 6 + d, q * P:(q + 1) * P], kdec[cols, u0 + q, :], vnew[cols, d, q, :], start=True, stop=True)
                    last.then_inc(s_ps, 1)
                if n >= 2:
                    pe.wait_ge(o_sb, n - 1)
                for q in range(4):
                    dst = ps[:, 4 + d, q * CH:(q + 1) * CH]
                    if st:
                        nc.tensor.matmul(dst, state[:, d, q, :], qdec[:, u0 + q, cols], start=True, stop=False)
                    last = nc.tensor.matmul(dst, vnew[cols, d, q, :], qkm[cols, u0 + q, cols], start=(st == 0), stop=True)
                last.then_inc(o_ps, 1)
            pe.wait_ge(on_sq, 1)
            sqf = od[:, 1, :, :].rearrange("p h s -> p (h s)")
            for b in range(2):
                last = nc.tensor.matmul(ps[:, b, :], ones[:, :], sqf[:, b * BANK:(b + 1) * BANK], start=True, stop=True)
            last.then_inc(on_ps, 1)

        @block.vector
        def _(dve):
            link = T.link(dve, "dve", T.chain_dve)
            for b in range(4):
                dve.wait_ge(wu_ps, 2 * b + 2)
                nc.vector.tensor_copy(grp(u_, b), bank4(2 * (b % 2) + 1)).then_inc(u_sb, 1)
            dve.wait_ge(u_sb, 4)
            for n, (st, d) in enumerate(steps):
                c, u0, cols, t, half = place(st, d)
                if st:
                    dve.wait_ge(v_ps, n - 1)
                    dve.wait_ge(o_ps, n - 1)
                    nc.vector.tensor_tensor(vnew[cols, d, :, :], u_[cols, u0:u0 + 4, :], bank4(2 + d)[cols], ALU.subtract).then_inc(v_sb, 1)
                else:
                    nc.vector.tensor_copy(vnew[cols, d, :, :], u_[cols, u0:u0 + 4, :]).then_inc(v_sb, 1)
                if st < 3:
                    dve.wait_ge(s_ps, n + 1)
                    if st == 0:
                        nc.vector.tensor_copy(state[:, d, :, :], bank4(6 + d)).then_inc(s_sb, 1)
                    else:
                        dve.wait_ge(s_sb, n - 1)
                        dve.wait_ge(o_ps, n + 1)
                        for q in range(4):
                            last = nc.vector.scalar_tensor_tensor(state[:, d, q, :], state[:, d, q, :], egl[:, t, d, half, q:q + 1],
                                                                  bank4(6 + d)[:, q, :], ALU.mult, ALU.add)
                        last.then_inc(s_sb, 1)
            dve.wait_ge(o_sb, 8)
            o, sqd = od[:, 0, :, :], od[:, 1, :, :]
            link(nc.vector.tensor_tensor(o, o, sqd, ALU.add))
            nc.vector.tensor_tensor(sqd, o, o, ALU.mult).then_inc(on_sq, 1)
            dve.wait_ge(on_ps, 1)
            nc.vector.tensor_scalar(sqd, ps[:, 0:2, :].rearrange("p b (h s) -> p (b h) s", h=2), 1.0 / DK, EPS, ALU.mult, ALU.add).then_inc(on_ms, 1)
            dve.wait_ge(on_rt, 1)
            link(nc.vector.reciprocal(sqd, sqd))
            link(nc.vector.scalar_tensor_tensor(o, o, head_norm[:, 0:1], sqd, ALU.mult, ALU.mult))
            nc.vector.tensor_tensor(oT[:, 0:4, :], o, z[:, :, :], ALU.mult).then_inc(o_ready, 1)

        @block.scalar
        def _(act):
            for b in range(4):
                act.wait_ge(wu_ps, 2 * b + 1)
                nc.scalar.activation(grp(wT, b), bank4(2 * (b % 2)), ACT.Copy).then_inc(w_sb, 1)
            for n, (st, d) in enumerate(steps):
                c, u0, cols, t, half = place(st, d)
                act.wait_ge(o_ps, n + 1)
                nc.scalar.activation(od[:, d, :, c * CH:(c + 1) * CH], ps[:, 4 + d, 0:S].rearrange("p (h s) -> p h s", h=4),
                                     ACT.Copy).then_inc(o_sb, 1)
            act.wait_ge(on_ms, 1)
            nc.scalar.activation(od[:, 1, :, :], od[:, 1, :, :], ACT.Sqrt).then_inc(on_rt, 1)

    res2 = sem("res2")
    with nc.Block() as block:
        @block.sync
        def _(sync):
            for g in range(G2_OUT + RING2, G2_EXP + RING2):
                ring.issue(sync, g, T.stream2(g))

        @block.tensor
        def _(pe):
            for c in range(4):
                ring.arrived(pe, G2_OUT + c)
                w = ring.piece(G2_OUT + c).rearrange("p (k c) -> p k c", k=KB)
                for t in range(NT):
                    for k in range(KB):
                        last = nc.tensor.matmul(ps[:, c, t * S:(t + 1) * S], oT[:, k, t * P:(t + 1) * P], w[:, k, :],
                                                start=(k == 0), stop=(k == KB - 1))
                last.then_inc(ring.used, 1)

        @block.vector
        def _(dve):
            for c in range(4):
                dve.wait_ge(ring.used, G2_OUT + c + 1)
                x = h[:, :, 256 * c:256 * (c + 1)]
                nc.vector.tensor_tensor(x, x, ps[:, c, :].rearrange("p (t c) -> p t c", t=NT), ALU.add).then_inc(res2, 1)
    stack.close()
    if T.dump("x3", [h[:, :, :]]):
        return True
    return experts(T)


def experts(T):
    nc, A, ps, sem = T.nc, T.A, T.ps, T.sem
    h, hT, ident, ring = T.h, T.hT, T.ident, T.ring2
    low_c, high_c = Carve(T.low[:, :]), Carve(T.arena[:, RING2 * PW:])
    xs = low_c(NT, D)
    xg = low_c(KB, NEXP * CAP)
    onehot = high_c(NT, NEXP * CAP)
    yb = high_c(D)
    sg, hh, hidT = high_c(BANK), high_c(BANK), high_c(4, P)
    stack = ExitStack()
    sb = lambda name, *shape: T.sb(stack, name, [P, *shape])
    router_w, ones, iota_s, tokid, zeros = sb("router_w", KB, NEXP), sb("ones2", P), sb("iota_s", S), sb("tokid", NT), sb("zeros2", BANK)
    probs, st = sb("probs", NT, NEXP), sb("st", 3, NT)
    pT = T.sb(stack, "probsT", [NEXP, 2, S])
    gate, place, place_f = T.sb(stack, "gate", [NEXP, CAP]), T.sb(stack, "place2", [NEXP, CAP], U32), T.sb(stack, "place_f", [NEXP, CAP])
    rep = T.sb(stack, "rep", [NEXP, 2, 4, CAP])
    diag = T.sb(stack, "diag", [NEXP, NEXP, CAP])
    cols = sb("cols", 2, NEXP)
    xe = sb("xe", KB, CAP)
    og = sb("og", S)
    loads = [(router_w[:, :, :], "router_w"), (ones[:, :], "ones"), (iota_s[:, :], "iota_s"), (tokid[:, :], "tokid")]
    c3 = sem("expert_consts")

    def refill(sync):
        for dst, name in loads:
            sync.dma_start(dst, A[name]).then_inc(c3, 16)

    def small(pe, done):
        pe.wait_ge(c3, 16 * len(loads))
        for t in range(NT):
            for k in range(KB):
                last = nc.tensor.matmul(ps[:, 4, t * NEXP:(t + 1) * NEXP], hT[:, k, t * P:(t + 1) * P], router_w[:, k, :],
                                        start=(k == 0), stop=(k == KB - 1))
        last.then_inc(done, 1)

    front(T, "ec", 3, ring, G2_EXP, [], small, refill, xs=xs)

    ex_sub, ex_exp, ex_p, pt_ps, pt_sb, rep_ready, cols_ps, bc_ps, oh_ready, xg_ps, xg_sb, z_ready = (sem(f"ec_{n}") for n in (
        "sub", "exp", "p", "pt_ps", "pt_sb", "rep", "cols_ps", "bc_ps", "oh", "xg_ps", "xg_sb", "zeros"))
    xe_ready = sem("ec_xe")
    with nc.Block() as block:
        @block.vector
        def _(dve):
            link = T.link(dve, "dve", T.chain_dve)
            nc.vector.memset(zeros[:, :], 0.0).then_inc(z_ready, 1)
            lgt = ps[:, 4, 0:NT * NEXP].rearrange("p (t e) -> p t e", t=NT)
            link(nc.vector.reduce_max(st[:, 0, :], lgt, AX.X))
            nc.vector.tensor_tensor(probs[:, :, :], lgt, st[:, 0, :].unsqueeze(2).broadcast_to([P, NT, NEXP]), ALU.subtract).then_inc(ex_sub, 1)
            dve.wait_ge(ex_exp, 1)
            link(nc.vector.reduce_sum(st[:, 1, :], probs[:, :, :], AX.X))
            link(nc.vector.reciprocal(st[:, 2, :], st[:, 1, :]))
            nc.vector.tensor_tensor(probs[:, :, :], probs[:, :, :], st[:, 2, :].unsqueeze(2).broadcast_to([P, NT, NEXP]), ALU.mult).then_inc(ex_p, 1)
            dve.wait_ge(pt_ps, 1)
            nc.vector.tensor_copy(pT[:, 0, :], ps[0:NEXP, 5, 0:S]).then_inc(pt_sb, 1)
            dve.wait_ge(pt_sb, 1)
            for r in range(CAP // 8):
                eight = slice(8 * r, 8 * r + 8)
                cur, nxt = pT[:, r % 2, :], pT[:, 1 - r % 2, :]
                link(nc.vector.max(gate[:, eight], cur))
                link(nc.vector.max_index(place[:, eight], gate[:, eight], cur))
                if r < CAP // 8 - 1:
                    link(nc.vector.match_replace(nxt, gate[:, eight], cur, -1.0))
            link(nc.vector.tensor_copy(place_f[:, :], place[:, :]))
            nc.vector.tensor_copy(rep[:, 0, :, :], place_f[:, :].unsqueeze(1).broadcast_to([NEXP, 4, CAP]))
            nc.vector.tensor_copy(rep[:, 1, :, :], gate[:, :].unsqueeze(1).broadcast_to([NEXP, 4, CAP]))
            nc.vector.tensor_tensor(diag[:, :, :], place_f[:, :].unsqueeze(1).broadcast_to([NEXP, NEXP, CAP]),
                                    ident[0:NEXP, 0:NEXP].unsqueeze(2).broadcast_to([NEXP, NEXP, CAP]), ALU.mult).then_inc(rep_ready, 1)
            dve.wait_ge(cols_ps, 1)
            nc.vector.tensor_copy(cols[:, :, :], ps[:, 6, 0:2 * NEXP].rearrange("p (a e) -> p a e", a=2))
            dve.wait_ge(bc_ps, 1)
            for t in range(NT):
                nc.vector.tensor_scalar(onehot[:, t, :], ps[:, 7, :], tokid[:, t:t + 1], None, ALU.is_equal).then_inc(oh_ready, 1)
            dve.wait_ge(xg_sb, KB)
            nc.vector.tensor_copy(xe[:, :, :], xg[:, :, 0:CAP]).then_inc(xe_ready, 1)

        @block.scalar
        def _(act):
            act.wait_ge(ex_sub, 1)
            nc.scalar.activation(probs[:, :, :], probs[:, :, :], ACT.Exp).then_inc(ex_exp, 1)
            for k in range(KB):
                act.wait_ge(xg_ps, k + 1)
                nc.scalar.activation(xg[:, k, :], ps[:, k % 4, :], ACT.Copy, scale=T.gains[:, 3, k:k + 1]).then_inc(xg_sb, 1)

        @block.tensor
        def _(pe):
            pe.wait_ge(ex_p, 1)
            for t in range(NT):
                last = nc.tensor.transpose(ps[0:NEXP, 5, t * P:(t + 1) * P], probs[:, t, :], ident[:, :])
            last.then_inc(pt_ps, 1)
            pe.wait_ge(rep_ready, 1)
            for a in range(2):
                last = nc.tensor.transpose(ps[:, 6, a * NEXP:(a + 1) * NEXP], rep[:, a, :, :].rearrange("p c s -> p (c s)"), ident[0:NEXP, 0:NEXP])
            last.then_inc(cols_ps, 1)
            nc.tensor.matmul(ps[:, 7, :], ones[0:NEXP, :], diag[:, :, :].rearrange("p e s -> p (e s)"), start=True, stop=True).then_inc(bc_ps, 1)
            pe.wait_ge(oh_ready, NT)
            for k in range(KB):
                if k >= 4:
                    pe.wait_ge(xg_sb, k - 3)
                for t in range(NT):
                    last = nc.tensor.matmul(ps[:, k % 4, :], xs[:, t, k * P:(k + 1) * P], onehot[:, t, :], start=(t == 0), stop=(t == NT - 1))
                last.then_inc(xg_ps, 1)
    if T.dump("xg", [xg, cols[:, :, :]]):
        return True

    sg_ready, hh_ready, t_ps, hid_ready, y_ready, og_ready = (sem(f"ex_{n}") for n in ("sg", "hh", "t_ps", "hid", "y", "og"))
    PER = 3 * KB
    used = lambda n, e: e * PER + (G2_EXP + n)
    with nc.Block() as block:
        @block.sync
        def _(sync):
            def load(e, r, turn):
                src = A["experts_in"][e, r // KB, r % KB] if r < 2 * KB else A["experts_down"][e, r - 2 * KB]
                ring.issue(sync, G2_EXP + r, src, turn)
            for r in range(RING2, PER):
                load(0, r, 0)
            with sync.Fori(1, NEXP) as e:
                for r in range(PER):
                    load(e, r, e * (PER // RING2))

        @block.tensor
        def _(pe):
            pe.wait_ge(z_ready, 1)
            for b in range(4):
                nc.tensor.matmul(ps[:, b, :], zeros[:, 0:P], zeros[:, :], start=True, stop=False, skip_group_check=True)
            with pe.Fori(0, NEXP) as e:
                turn = e * (PER // RING2)
                pe.wait_ge(xe_ready, e + 1)
                for r in range(2 * KB):
                    ring.arrived(pe, G2_EXP + r, turn)
                    w, k = ring.piece(G2_EXP + r), r % KB
                    for j in range(4):
                        last = nc.tensor.matmul(ps[32 * j:32 * (j + 1), 4 + r // KB, :], xe[:, k, :], w[:, j * BANK:(j + 1) * BANK],
                                                start=(k == 0), stop=(k == KB - 1), tile_position=(0, 32 * j))
                    last.then_inc(ring.used, 1)
                pe.wait_ge(hh_ready, e + 1)
                for i in range(4):
                    last = nc.tensor.transpose(ps[:, 4, i * P:(i + 1) * P], hh[:, i * P:(i + 1) * P], ident[:, :])
                last.then_inc(t_ps, 1)
                pe.wait_ge(hid_ready, e + 1)
                for r in range(KB):
                    ring.arrived(pe, G2_EXP + 2 * KB + r, turn)
                    w = ring.piece(G2_EXP + 2 * KB + r).rearrange("p (j d) -> p j d", j=4)
                    i, half = r // 2, r % 2
                    for j in range(4):
                        last = nc.tensor.matmul(ps[32 * j:32 * (j + 1), 6 + half, :], hidT[:, i, 32 * j:32 * (j + 1)], w[:, j, :],
                                                start=(i == 0), stop=(i == 3), tile_position=(0, 32 * j))
                    last.then_inc(ring.used, 1)
                pe.wait_ge(y_ready, e + 1)
                pe.wait_ge(og_ready, e + 1)
                for t in range(NT):
                    for half in range(2):
                        last = nc.tensor.matmul(ps[:, 2 * t + half, :], og[:, t * P:(t + 1) * P], yb[:, half * BANK:(half + 1) * BANK],
                                                start=False, stop=False, skip_group_check=True)
            for b in range(4):
                last = nc.tensor.matmul(ps[:, b, :], zeros[:, 0:P], zeros[:, :], start=False, stop=True, skip_group_check=True)

        @block.scalar
        def _(act):
            with act.Fori(0, NEXP) as e:
                act.wait_ge(ring.used, used(KB, e))
                nc.scalar.activation(sg, ps[:, 4, :], ACT.Silu).then_inc(sg_ready, 1)
                act.wait_ge(t_ps, e + 1)
                nc.scalar.activation(hidT.rearrange("p i c -> p (i c)"), ps[:, 4, :], ACT.Copy).then_inc(hid_ready, 1)
                act.wait_ge(ring.used, used(PER, e))
                nc.scalar.activation(yb, ps[:, 6:8, :].rearrange("p b c -> p (b c)"), ACT.Copy).then_inc(y_ready, 1)

        @block.vector
        def _(dve):
            def body(e, last_one):
                dve.wait_ge(sg_ready, e + 1)
                dve.wait_ge(ring.used, used(2 * KB, e))
                nc.vector.tensor_tensor(hh, sg, ps[:, 5, :], ALU.mult).then_inc(hh_ready, 1)
                nc.vector.tensor_scalar(og[:, :], iota_s[:, :], cols[:, 0, bass.ds(e, 1)], cols[:, 1, bass.ds(e, 1)],
                                        ALU.is_equal, ALU.mult).then_inc(og_ready, 1)
                if not last_one:
                    nc.vector.tensor_copy(xe[:, :, :], xg[:, :, bass.ds(e * CAP + CAP, CAP)]).then_inc(xe_ready, 1)
            with dve.Fori(0, NEXP - 1) as e:
                body(e, False)
            body(NEXP - 1, True)
    stack.close()
    norm_tokens(T, "norm_final_2", add_banks=True, store=T.out)
    return True


def host_arrays(inputs):
    import numpy as np

    f = {k: np.asarray(v) for k, v in inputs.items()}
    f32 = np.float32
    out = {"x": f["x"][0]}

    def col_pieces(w):
        n = w.shape[1] // 256
        return w.reshape(KB, P, n, 256).transpose(2, 1, 0, 3).reshape(n, P, PW)

    def half_pieces(w):
        n = w.shape[1] // P
        return w.reshape(KB, P, n, P).transpose(2, 1, 0, 3).reshape(n, P, HW)

    cols = lambda g: g.reshape(KB, P).T
    out["gains"] = np.stack([cols(f["norm_mix"][0]), cols(f["norm_ffn"][0]), cols(f["norm_mix_w_2"][0]),
                             cols(f["norm_ffn_w_2"][0])], axis=1)
    out["ident"] = np.eye(P, dtype=f32)
    w = f["w_in"][0]
    sizes = dict(fq=512, fk=512, fv=512, f=8, nq=512, kc=128, vc=128, ksl=128, vsl=128, kwn=128, vwn=128,
                 gate=24, merge=2048)
    parts, at = {}, 0
    for name, n in sizes.items():
        parts[name] = w[:, at:at + n]
        at += n
    twice = lambda a: np.concatenate([a[:, 0:64], a[:, 0:64], a[:, 64:128], a[:, 64:128]], axis=1)
    order = [parts["fq"], parts["fk"], parts["nq"], twice(parts["ksl"]), twice(parts["kwn"]), parts["kc"], parts["vc"],
             parts["merge"], parts["fv"], parts["vsl"], parts["vwn"]]
    w1 = f["nsa_cmp_w1"][0].reshape(2, 4, 8, DH, P).transpose(0, 1, 3, 2, 4).reshape(8, DH, HW)
    w1 = np.concatenate([w1, w1], axis=1)
    subk = f["peer_subkeys"][0].reshape(2, 8, P, P).transpose(0, 3, 1, 2).reshape(2, P, HW)
    out["stream1"] = np.concatenate([half_pieces(np.concatenate(order, axis=1)), w1,
                                     half_pieces(f["w_branch"][0].reshape(D, D)), half_pieces(f["w_out"][0]),
                                     half_pieces(f["peer_wq"][0]), subk], axis=0)
    u = f["peer_u"][0].reshape(NKEYS, P, KB, P).transpose(0, 3, 2, 1).reshape(NKEYS, P, HW)
    v = f["peer_v"][0].reshape(NKEYS, P, HW)
    out["peer"] = np.stack([u, v], axis=1)
    out["iota16"] = np.broadcast_to(np.arange(16, dtype=f32), (P, 16))
    out["iota128"] = np.broadcast_to(np.arange(P, dtype=f32), (P, P))
    small = np.zeros((KB, P, 160), f32)
    fw = parts["f"].reshape(KB, P, 8)
    small[:, :, 0:8] = fw
    small[:, :, 64:72] = fw
    small[:, :, 128:152] = parts["gate"].reshape(KB, P, 24)
    out["small_w"] = small.transpose(1, 0, 2)
    fb = np.zeros((P, 1), f32)
    fb[0:8, 0] = fb[64:72, 0] = f["fox_f_bias"][0]
    out["fbias"] = fb
    out["cmp_pos"] = np.concatenate([f["nsa_cmp_pos"][0].transpose(2, 0, 1)] * 2, axis=0)
    w2 = f["nsa_cmp_w2"][0].transpose(1, 0, 2)
    out["cmp_w2"] = np.concatenate([w2, w2], axis=2)

    w = f["w_in_2"][0]
    wm = np.concatenate([w[:, 0:2048], w[:, 2064:2576]], axis=1)
    out["stream2"] = np.concatenate([col_pieces(wm), col_pieces(f["w_out_2"][0])], axis=0)
    out["ab_w"] = w[:, 2048:2064].reshape(KB, P, 16).transpose(1, 0, 2)
    out["norm_final"] = np.broadcast_to(f["norm_final"], (P, D))
    out["norm_final_2"] = np.broadcast_to(f["norm_final_w_2"], (P, D))
    out["conv_w"] = f["conv_w_2"][0].reshape(5, 12, P).transpose(2, 1, 0)
    out["pool_w"] = f["pool_w_2"][0].transpose(1, 0, 2)
    out["pool_scale"] = f["pool_scale_2"][0].reshape(4, P).T
    out["head_norm"] = f["head_norm_w_2"][0].reshape(P, 1)
    out["a_log"] = np.broadcast_to(np.concatenate([f["a_log_fwd_2"][0], f["a_log_bwd_2"][0]]), (P, 8))
    out["dt_bias"] = np.broadcast_to(np.concatenate([f["dt_bias_fwd_2"][0], f["dt_bias_bwd_2"][0]]), (P, 8))
    out["router_w"] = f["router_w_2"][0].reshape(KB, P, NEXP).transpose(1, 0, 2)
    out["experts_in"] = np.stack([f["expert_w_gate_2"][0].reshape(NEXP, KB, P, PW), f["expert_w_up_2"][0].reshape(NEXP, KB, P, PW)], axis=1)
    out["experts_down"] = (f["expert_w_down_2"][0].reshape(NEXP, 4, 4, P, 2, BANK).transpose(0, 2, 4, 3, 1, 5)
                           .reshape(NEXP, KB, P, PW))

    out["ones"] = np.ones((P, P), f32)
    out["iota_s"] = np.broadcast_to(np.arange(S, dtype=f32), (P, S))
    out["tokid"] = np.arange(S, dtype=f32).reshape(NT, P).T
    i = np.arange(P)
    chunk = i[:, None] // CH == i[None, :] // CH
    masks = np.zeros((P, 2, LEVELS + 1, P), f32)
    for lev in range(LEVELS):
        b = 1 << lev
        pair = i[:, None] // (2 * b) == i[None, :] // (2 * b)
        m = pair & ((i[:, None] // b) % 2 == 0) & ((i[None, :] // b) % 2 == 1)
        masks[:, 0, lev], masks[:, 1, lev] = m, m.T
    masks[:, 0, LEVELS] = chunk & (i[:, None] <= i[None, :])
    masks[:, 1, LEVELS] = chunk & (i[:, None] >= i[None, :])
    out["masks"] = masks
    out["same_chunk"] = chunk.astype(f32)
    pm = np.zeros((S, 4, S), f32)
    for n, win in enumerate((2, 4, 8, 16)):
        lo = win // 2
        for t in range(S):
            a, b = max(t - lo, 0), min(t + win - lo, S)
            pm[a:b, n, t] = f32(1.0) / f32(b - a)
            pm[t, n, t] -= 1.0
    out["pool_m"] = pm.reshape(NT, P, 4, S).transpose(1, 0, 2, 3)
    def tables(positions):
        inv = np.power(f32(500000.0), -np.arange(0, 16, 2, dtype=f32) / f32(16))
        ang = positions.astype(f32)[:, None] * inv[None, :]
        cos, sin = np.ones((P, len(positions)), f32), np.zeros((P, len(positions)), f32)
        for base in (0, DH):
            for half in (0, 8):
                cos[base + half:base + half + 8] = np.cos(ang).T
                sin[base + half:base + half + 8] = np.sin(ang).T
        return np.stack([cos, sin], axis=1)

    out["tables"] = tables(np.arange(S))
    out["tables_cmp"] = tables(np.arange(16) * CMP_STRIDE + CMP_LEN - 1)
    rot = np.zeros((P, P), f32)
    for base in (0, DH):
        for i in range(8):
            rot[base + 8 + i, base + i] = -1.0
            rot[base + i, base + 8 + i] = 1.0
    out["rot"] = rot
    tri = np.where(np.arange(P)[None, :] <= np.arange(P)[:, None], 0.0, NEG).astype(f32)
    out["causal"] = np.concatenate([np.zeros((P, P), f32), tri], axis=1)
    end = np.arange(16) * CMP_STRIDE + CMP_LEN - 1
    seen = end[None, :] <= np.arange(S)[:, None]
    mc = np.stack([np.where(seen, 0.0, NEG), seen.astype(f32)], axis=0).astype(f32)
    out["mask_cmp"] = mc.reshape(2, NT, P, 16).transpose(2, 0, 1, 3)
    sel = np.zeros((P, 8, S), f32)
    for i in range(8):
        sel[i, i] = sel[64 + i, i] = 8.0
    out["sel8"] = sel
    return {k: np.ascontiguousarray(v, dtype=f32) for k, v in out.items()}


def kernel(**inputs):
    import numpy as np
    import concourse.bacc as bacc
    from concourse.bass_utils import run_bass_kernel_spmd

    nc = bacc.Bacc("TRN2", target_bir_lowering=False, num_devices=1)
    arrays = host_arrays(inputs)
    A = {name: nc.dram_tensor(f"in_{name}", a.shape, mybir.dt.from_np(a.dtype), kind="ExternalInput").ap()
         for name, a in arrays.items()}
    out = nc.dram_tensor("out", (S, D), F32, kind="ExternalOutput").ap()
    build_kernel(nc, A, out)
    r = run_bass_kernel_spmd(nc, [{f"in_{name}": a for name, a in arrays.items()}], core_ids=[0])
    return r.results[0]["out"].reshape(1, S, D)
```

```python
import concourse.bass as bass
from concourse import mybir
from contextlib import ExitStack

F32 = mybir.dt.float32
F32R = mybir.dt.float32r
U32 = mybir.dt.uint32
ALU = mybir.AluOpType
ACT = mybir.ActivationFunctionType
AX = mybir.AxisListType

P = 128
D = 1024
KB = D // P
S = 256
NT = S // P
HW = 1024
PW = 2048
BANK = 512
DH = 64
HEADS = 8
NCMP, CMP_LEN, CMP_STRIDE = 15, 32, 16
TOPK = 16
NKEYS = 128
NEXP, CAP = 16, 32
EPS = 1e-6
NEG = -1e30
SCALE = DH ** -0.5
RING1, RING2 = 4, 8


class Link:

    def __init__(self, eng, sem, n=0):
        self.eng, self.sem, self.n = eng, sem, n

    def __call__(self, ins):
        self.n += 1
        ins.then_inc(self.sem, 1)
        self.eng.wait_ge(self.sem, self.n)


class Carve:

    def __init__(self, tile):
        self.tile, self.at = tile, 0

    def __call__(self, *shape):
        n = 1
        for x in shape:
            n *= x
        part = self.tile[:, self.at:self.at + n]
        self.at += n
        names = "abcd"[:len(shape)]
        if len(shape) > 1:
            part = part.rearrange(f"p ({' '.join(names)}) -> p {' '.join(names)}", **dict(zip(names, shape)))
        return part


class Ring:

    def __init__(self, buf, slots, loaded, used):
        self.buf, self.slots, self.loaded, self.used = buf, slots, loaded, used
        self.issued = 0

    def piece(self, g):
        return self.buf[:, g % self.slots, :]

    def issue(self, sync, g, src, turn=0):
        if g >= self.slots:
            sync.wait_ge(self.used, g - self.slots + 1 + turn * self.slots)
        sync.dma_start(self.piece(g), src).then_inc(self.loaded[g % self.slots], 16)

    def arrived(self, eng, g, turn=0):
        eng.wait_ge(self.loaded[g % self.slots], 16 * (g // self.slots + 1) + 16 * turn)


def build_kernel(nc, A, out):
    ctx = ExitStack()
    with ctx:
        def sb(stack, name, shape, dt=F32):
            return stack.enter_context(nc.sbuf_tensor(name, shape, dt))

        stage_sems = []

        def lasting_sem(name):
            return ctx.enter_context(nc.semaphore(name))

        def sem(name):
            stage_sems.append(nc.alloc_semaphore(name))
            return stage_sems[-1]

        def next_block():
            nc.clear_and_free_semaphores(stage_sems)
            stage_sems.clear()
            with nc.Block():
                pass

        ident = sb(ctx, "ident", [P, P])
        h = sb(ctx, "h", [P, NT, D])
        gains = sb(ctx, "gains", [P, 4, KB])
        ss = sb(ctx, "ss", [P, 4])
        ps = ctx.enter_context(nc.psum_tensor("ps", [P, 8, BANK], F32))
        arena = sb(ctx, "arena", [P, NKEYS * S])
        first = ExitStack()
        ring1 = Ring(sb(first, "ring1", [P, RING1, HW]), RING1, [sem(f"ring1_loaded{i}") for i in range(RING1)], sem("ring1_used"))
        ring2_sems = [lasting_sem(f"ring2_loaded{i}") for i in range(RING2)], lasting_sem("ring2_used")
        consts_loaded = sem("consts_loaded")
        chain_act, chain_dve = lasting_sem("chain_act"), lasting_sem("chain_dve")
        links = {}

        def link(eng, name, s):
            old = links.get(name)
            links[name] = Link(eng, s, old.n if old else 0)
            return links[name]

        class T:
            pass
        T.nc, T.A, T.ctx, T.sb, T.sem, T.link, T.ps = nc, A, ctx, sb, sem, link, ps
        T.chain_act, T.chain_dve = chain_act, chain_dve
        T.ident, T.h, T.gains, T.ss = ident, h, gains, ss
        T.out, T.arena = out, arena
        T.ring1, T.ring2_sems = ring1, ring2_sems

        def stream1(g):
            return A["stream1"][g]
        T.stream1 = stream1

        def stream2(g):
            if g < G2_EXP:
                return A["stream2"][g]
            r = g - G2_EXP
            return A["experts_in"][0, r // KB, r % KB]
        T.stream2 = stream2

        x_loaded = sem("x_loaded")
        with nc.Block() as block:
            @block.sync
            def _(sync):
                sync.dma_start(h[:, :, :], A["x"].rearrange("(t p) d -> p t d", p=P)).then_inc(x_loaded, 16)
                for g in range(RING1):
                    ring1.issue(sync, g, stream1(g))
                ring1.issued = RING1

            @block.scalar
            def _(act):
                act.dma_start(gains[:, :, :], A["gains"]).then_inc(consts_loaded, 16)
                act.dma_start(ident[:, :], A["ident"]).then_inc(consts_loaded, 16)
                act.wait_ge(consts_loaded, 32)
                act.wait_ge(x_loaded, 16)
        split_tiles(T, first, "first")
        T.hT_stack = ExitStack()
        T.hT = sb(T.hT_stack, "hT", [P, KB, S])
        mixer1(T)
        peer(T)
        first.close()
        next_block()
        T.hT = sb(ctx, "hT2", [P, KB, S])
        second_block(T)


def split_tiles(T, stack, name):
    r = lambda n, shape: stack.enter_context(T.nc.sbuf_tensor(f"{name}_{n}", [P, *shape], F32R))
    T.parts = r("h_parts", (2, KB, S))
    T.w_parts = r("w_parts", (2, 2, HW))


def front(T, name, gain, ring, g0, groups, small, refill, xs=None):
    nc, ps, hT, h, ss = T.nc, T.ps, T.hT, T.h, T.ss
    sem = T.sem
    squares_done, mean_done, root_done, scaled = (sem(f"{name}_{s}") for s in ("squares", "mean", "root", "scaled"))
    bank_ready, bank_free = sem(f"{name}_bank_ready"), sem(f"{name}_bank_free")
    small_done = sem(f"{name}_small_done")
    h_high, h_low, w_high, w_low, unit_done = (sem(f"{name}_{s}") for s in ("h_high", "h_low", "w_high", "w_low", "unit_done"))
    TB = 4
    per = 2 if ring.slots == RING1 else 1
    n_split = sum(g[1] for g in groups if g[0] == "F")
    stack = ExitStack()
    if xs is None:
        xs = T.sb(stack, f"{name}_xs", [P, NT, D])

    def pieces_of(eng, body):
        done = 0
        for mode, pieces, dst, func in groups:
            loops = (pieces - 1) // 4 if per == 2 and pieces >= 8 else 0
            if loops:
                with eng.Fori(0, loops) as i:
                    for r in range(4):
                        body((mode, dst, func), r, done + r, i)
            for p in range(4 * loops, pieces):
                body((mode, dst, func), p, done + p, 0)
            done += pieces

    def raw(u):
        if per == 2:
            return ring.piece(g0 + u).rearrange("p (k c) -> p k c", k=KB)
        return ring.piece(g0 + u // 2).rearrange("p (k c) -> p k c", k=KB)[:, :, (u % 2) * P:(u % 2 + 1) * P]

    parts_of = lambda u: [T.w_parts[:, u % 2, a, :].rearrange("p (k c) -> p k c", k=KB) for a in range(2)]

    with nc.Block() as block:
        @block.sync
        def _(sync):
            refill(sync)

        @block.scalar
        def _(act):
            for t in range(NT):
                nc.scalar.activation(xs[:, t, :], h[:, t, :], ACT.Square, accum_out=ss[:, t:t + 1]).then_inc(squares_done, 1)
            act.wait_ge(mean_done, 1)
            nc.scalar.activation(ss[:, 2:4], ss[:, 2:4], ACT.Sqrt).then_inc(root_done, 1)

            def split_high(u, i):
                ring.arrived(act, g0 + (u if per == 2 else u // 2), i * 2)
                if u >= 2:
                    act.wait_ge(unit_done, i * 8 + (u - 1))
                nc.scalar.activation(parts_of(u)[0], raw(u), ACT.Copy).then_inc(w_high, 1)

            if n_split:
                split_high(0, 0)
                split_high(1, 0)
            for b in range(TB):
                act.wait_ge(bank_ready, b + 1)
                for kk in range(2):
                    k = 2 * b + kk
                    nc.scalar.activation(hT[:, k, :], ps[:, b, kk * S:(kk + 1) * S], ACT.Copy,
                                         scale=T.gains[:, gain, k:k + 1]).then_inc(bank_free, 1)
                if n_split:
                    act.wait_ge(bank_free, 2 * (b + 1))
                    nc.scalar.activation(T.parts[:, 0, 2 * b:2 * b + 2, :], hT[:, 2 * b:2 * b + 2, :], ACT.Copy).then_inc(h_high, 1)

            def body(group, p, n, i):
                mode, dst, func = group
                if n + 1 < n_split:
                    split_high(2 * n + 2, i)
                    split_high(2 * n + 3, i)
                if mode == "F":
                    act.wait_ge(unit_done, i * 8 + 2 * (n + 1))
                else:
                    act.wait_ge(ring.used, g0 + per * (n + 1))
                nc.scalar.activation(dst[:, i * 4 + p, :], ps[:, n % 4, :], func).then_inc(bank_free, 1)
            pieces_of(act, body)

        @block.vector
        def _(dve):
            link = T.link(dve, "dve", T.chain_dve)
            dve.wait_ge(squares_done, NT)
            nc.vector.tensor_scalar(ss[:, 2:4], ss[:, 0:2], 1.0 / D, EPS, ALU.mult, ALU.add).then_inc(mean_done, 1)
            dve.wait_ge(root_done, 1)
            link(nc.vector.reciprocal(ss[:, 2:4], ss[:, 2:4]))
            for t in range(NT):
                nc.vector.tensor_scalar(xs[:, t, :], h[:, t, :], ss[:, 2 + t:3 + t], None, ALU.mult).then_inc(scaled, 1)

            def split_low(u, i):
                dve.wait_ge(w_high, i * 8 + (u + 1))
                high, low = parts_of(u)
                nc.vector.tensor_tensor(low, raw(u), high.bitcast(F32), ALU.subtract).then_inc(w_low, 1)

            if n_split:
                split_low(0, 0)
                split_low(1, 0)
                for b in range(TB):
                    dve.wait_ge(h_high, b + 1)
                    two = slice(2 * b, 2 * b + 2)
                    nc.vector.tensor_tensor(T.parts[:, 1, two, :], hT[:, two, :], T.parts[:, 0, two, :].bitcast(F32),
                                            ALU.subtract).then_inc(h_low, 1)

            def body(group, p, n, i):
                if n + 1 < n_split:
                    split_low(2 * n + 2, i)
                    split_low(2 * n + 3, i)
            pieces_of(dve, body)

        @block.tensor
        def _(pe):
            pe.wait_ge(scaled, NT)
            for b in range(TB):
                for kk in range(2):
                    for t in range(NT):
                        k = 2 * b + kk
                        last = nc.tensor.transpose(ps[:, b, kk * S + t * P:kk * S + (t + 1) * P],
                                                   xs[:, t, k * P:(k + 1) * P], T.ident[:, :])
                last.then_inc(bank_ready, 1)
            pe.wait_ge(bank_free, KB)
            if n_split:
                pe.wait_ge(h_low, TB)

            def body(group, p, n, i):
                mode, bank = group[0], n % 4
                pe.wait_ge(bank_free, i * 4 + (KB + n - 3))
                for half in range(2):
                    g = g0 + (2 * n + half if per == 2 else n)
                    if mode == "F":
                        u = 2 * n + half
                        pe.wait_ge(w_low, i * 8 + (u + 1))
                        wh, wl = parts_of(u)
                        for k in range(KB):
                            for m, (w, x) in enumerate(((wh, 0), (wl, 0), (wh, 1))):
                                last = nc.tensor.matmul(ps[:, bank, half * S:(half + 1) * S], w[:, k, :], T.parts[:, x, k, :],
                                                        start=(k == 0 and m == 0), stop=(k == KB - 1 and m == 2))
                                if k == 0 and m == 0 and (per == 2 or half == 1):
                                    last.then_inc(ring.used, 1)
                        last.then_inc(unit_done, 1)
                        continue
                    if per == 2:
                        ring.arrived(pe, g, i * 2)
                        w = raw(2 * n + half)
                        for t in range(NT):
                            at = t * S + half * P
                            for k in range(KB):
                                last = nc.tensor.matmul(ps[:, bank, at:at + P], hT[:, k, t * P:(t + 1) * P], w[:, k, :],
                                                        start=(k == 0), stop=(k == KB - 1))
                        last.then_inc(ring.used, 1)
                    else:
                        if half == 0:
                            ring.arrived(pe, g)
                        w = ring.piece(g).rearrange("p (k c) -> p k c", k=KB)
                        for k in range(KB):
                            last = nc.tensor.matmul(ps[:, bank, half * S:(half + 1) * S], hT[:, k, half * P:(half + 1) * P],
                                                    w[:, k, :], start=(k == 0), stop=(k == KB - 1))
                        if half == 1:
                            last.then_inc(ring.used, 1)
            pieces_of(pe, body)
            small(pe, small_done)
    stack.close()
    return small_done


FQ, FK, NQ, KSL, KWN, KC, VC, MERGE = 0, 4, 8, 12, 14, 16, 17, 18
NEARLY = 36
NFULL = NKEYS - NEARLY
G_CMP, G_BRANCH, G_OUT, G_WQ, G_SUBK, G_EARLY = 40, 48, 56, 64, 80, 82
G_PEER = G_EARLY + NEARLY
G_LATE = G_PEER + 2 * NFULL


def mixer1(T):
    nc, A, ps, sem = T.nc, T.A, T.ps, T.sem
    stack = ExitStack()
    sb = lambda name, shape: T.sb(stack, name, shape)
    h, hT, ident, ring = T.h, T.hT, T.ident, T.ring1
    carve = T.carve = Carve(T.arena)
    proj = carve(34, S)
    vtok = carve(3, NT, 256)
    small_w = sb("small_w", [P, KB, 160])
    tables = sb("tables", [P, 2, S])
    tables_cmp = sb("tables_cmp", [P, 2, 16])
    rot = sb("rot", [P, P])
    causal = sb("causal", [P, S])
    mask_cmp = sb("mask_cmp", [P, 2, NT, 16])
    sel8 = carve(8, S)
    pos = sb("pos", [P, 2, CMP_LEN])
    w2 = sb("w2", [P, 2, P])
    fbias = sb("fbias", [P, 1])
    loads = [(small_w[:, :, :], "small_w"), (tables[:, :, :], "tables"), (tables_cmp[:, :, :], "tables_cmp"),
             (rot[:, :], "rot"), (causal[:, :], "causal"), (mask_cmp[:, :, :, :], "mask_cmp"),
             (sel8[:, :, :], "sel8"), (pos[:, :, :], "cmp_pos"), (w2[:, :, :], "cmp_w2"), (fbias[:, :], "fbias")]
    mix_consts = sem("mix_consts")

    def refill(sync):
        for g in range(RING1, G_CMP + RING1):
            ring.issue(sync, g, T.stream1(g))
            if g == RING1:
                for dst, name in loads:
                    sync.dma_start(dst, A[name]).then_inc(mix_consts, 16)

    def small(pe, done):
        pe.wait_ge(mix_consts, 16 * len(loads))
        for k in range(KB):
            nc.tensor.matmul(ps[:, 4, 0:S], small_w[:, k, 0:P], hT[:, k, :], start=(k == 0), stop=(k == KB - 1))
        for t in range(NT):
            for k in range(KB):
                last = nc.tensor.matmul(ps[:, 5, t * 24:(t + 1) * 24], hT[:, k, t * P:(t + 1) * P],
                                        small_w[:, k, P:P + 24], start=(k == 0), stop=(k == KB - 1))
        last.then_inc(done, 1)

    pieces = lambda t, a, b: t[:, 2 * a:2 * b, :].rearrange("p (n c) s -> p n (c s)", c=2)
    vdst = vtok[:, :, :, :].rearrange("p n t c -> p n (t c)")
    front(T, "mix", 0, ring, 0, [("F", 9, pieces(proj, 0, 9), ACT.Copy),
                                 ("F", 8, pieces(proj, 9, 17), ACT.Sigmoid),
                                 ("T", 3, vdst, ACT.Copy)], small, refill, xs=T.arena[:, -NT * D:].rearrange("p (t d) -> p t d", t=NT))

    gates = sb("gates", [P, NT, 24])
    clog = carve(2, S)
    ft = carve(4, S)
    ones_row = carve(S)
    rtmp = carve(2, 2 * S)
    kb = carve(2, CMP_LEN, 32)
    hsum = carve(2, P)
    hid = sb("hid", [P, 2, 2, 16])
    kcmp = sb("kcmp", [P, 2, 16])
    kc_raw = sb("kc_raw", [P, 2, 16])
    vcmp = sb("vcmp", [16, 2, DH])
    rot_done, rot_used, kb_ready, hid_ps, hid_ready = (sem(n) for n in ("rot_done", "rot_used", "kb_ready", "hid_ps", "hid_ready"))
    hsum_ready = sem("hsum_ready")
    kc_ps, kc_sb, kcr_ps, fz_ready, fe_ready, gates_ready = (sem(n) for n in ("kc_ps", "kc_sb", "kcr_ps", "fz_ready", "fe_ready", "gates_ready"))
    with nc.Block() as block:
        @block.sync
        def _(sync):
            for g in range(G_CMP + RING1, G_BRANCH + RING1):
                ring.issue(sync, g, T.stream1(g))

        @block.tensor
        def _(pe):
            for j in range(4):
                b = NQ + 2 * j
                if j >= 2:
                    pe.wait_ge(rot_used, j - 1)
                nc.tensor.matmul(ps[:, j % 2, :], rot[:, :], proj[:, b:b + 2, :].rearrange("p b s -> p (b s)"),
                                 start=True, stop=True).then_inc(rot_done, 1)
            pe.wait_ge(kb_ready, 5)
            for j in range(2):
                for lh in range(4):
                    g = G_CMP + 4 * j + lh
                    ring.arrived(pe, g)
                    w1 = ring.piece(g).rearrange("p (l c) -> p l c", l=8)
                    for ll in range(8):
                        for grp in range(2):
                            lo, at = DH * grp, 64 * grp + 32 * (ll % 2)
                            last = nc.tensor.matmul(ps[at:at + 32, 2 + j, 0:P], kb[lo:lo + DH, j, 8 * lh + ll, :],
                                                    w1[lo:lo + DH, ll, :], start=(lh == 0 and ll < 2),
                                                    stop=(lh == 3 and ll >= 6), tile_position=(lo, at))
                    last.then_inc(ring.used, 1)
            pe.wait_ge(fz_ready, 1)
            pe.wait_ge(gates_ready, 1)
            for j in range(2):
                pe.wait_ge(hsum_ready, j + 1)
                for grp in range(2):
                    for par in range(2):
                        at = 64 * grp + 32 * par
                        last = nc.tensor.matmul(ps[:, 4 + j, 16 * grp:16 * grp + NCMP], hsum[:, j, :],
                                                ident[:, at:at + NCMP], start=(par == 0), stop=(par == 1))
                last.then_inc(hid_ps, 1)
            pe.wait_ge(hid_ready, 4)
            for grp in range(2):
                nc.tensor.matmul(ps[:, 6, 16 * grp:16 * grp + NCMP], w2[:, 0, :], hid[:, 0, grp, 0:NCMP],
                                 start=True, stop=True)
            for grp in range(2):
                last = nc.tensor.matmul(ps[0:NCMP, 7, DH * grp:DH * (grp + 1)], hid[:, 1, grp, 0:NCMP],
                                        w2[:, 1, 0:DH], start=True, stop=True)
            last.then_inc(kc_ps, 1)
            pe.wait_ge(kc_sb, 1)
            nc.tensor.matmul(ps[:, 0, 0:32], rot[:, :], kc_raw[:, :, :].rearrange("p g n -> p (g n)"),
                             start=True, stop=True).then_inc(kcr_ps, 1)

        @block.scalar
        def _(act):
            link = T.link(act, "act", T.chain_act)
            nc.scalar.activation(gates[:, :, :], ps[:, 5, 0:48].rearrange("p (t c) -> p t c", t=NT), ACT.Sigmoid).then_inc(gates_ready, 1)
            act.wait_ge(fz_ready, 1)
            link(nc.scalar.activation(ft[:, 2, :], ft[:, 0, :], ACT.Abs))
            link(nc.scalar.activation(ft[:, 2, :], ft[:, 2, :], ACT.Exp, scale=-1.0))
            nc.scalar.activation(ft[:, 2, :], ft[:, 2, :], ACT.Ln, bias=1.0).then_inc(fe_ready, 1)
            for j in range(2):
                act.wait_ge(ring.used, G_CMP + 4 * (j + 1))
                nc.scalar.activation(hsum[:, j, :], ps[:, 2 + j, 0:P], ACT.Copy).then_inc(hsum_ready, 1)
            for j in range(2):
                act.wait_ge(hid_ps, j + 1)
                for grp in range(2):
                    nc.scalar.activation(hid[:, j, grp, 0:NCMP], ps[:, 4 + j, 16 * grp:16 * grp + NCMP], ACT.Gelu).then_inc(hid_ready, 1)

        @block.vector
        def _(dve):
            link = T.link(dve, "dve", T.chain_dve)
            nc.vector.memset(kb[:, :, :, NCMP:], 0.0).then_inc(kb_ready, 1)
            for j in range(2):
                tok = proj[:, KC + j, :].rearrange("p (a b) -> p a b", b=16)
                for lh in range(2):
                    nc.vector.tensor_tensor(
                        kb[:, j, 16 * lh:16 * (lh + 1), 0:NCMP],
                        tok[:, lh:lh + NCMP, :].rearrange("p n l -> p l n"),
                        pos[:, j, 16 * lh:16 * (lh + 1)].unsqueeze(2).broadcast_to([P, 16, NCMP]),
                        ALU.add).then_inc(kb_ready, 1)
            nc.vector.tensor_scalar(ft[:, 0, :], ps[:, 4, 0:S], fbias[:, 0:1], None, ALU.add).then_inc(fz_ready, 1)
            dve.wait_ge(fz_ready, 1)
            link(nc.vector.tensor_scalar(ft[:, 1, :], ft[:, 0, :], 0.0, None, ALU.min))
            link(nc.vector.memset(ones_row[:, :], 1.0))
            link(nc.vector.memset(kc_raw[:, :, :], 0.0))
            cos = tables[:, 0, :].unsqueeze(1).broadcast_to([P, 2, S])
            sin = tables[:, 1, :].unsqueeze(1).broadcast_to([P, 2, S])
            for j in range(4):
                b = NQ + 2 * j
                dve.wait_ge(rot_done, j + 1)
                tmp = rtmp[:, j % 2, :].rearrange("p (b s) -> p b s", b=2)
                nc.vector.tensor_tensor(tmp, ps[:, j % 2, :].rearrange("p (b s) -> p b s", b=2), sin,
                                        ALU.mult).then_inc(rot_used, 1)
                link(nc.vector.tensor_tensor(proj[:, b:b + 2, :], proj[:, b:b + 2, :], cos, ALU.mult))
                dve.wait_ge(rot_used, j + 1)
                link(nc.vector.tensor_tensor(proj[:, b:b + 2, :], proj[:, b:b + 2, :], tmp, ALU.add))
            dve.wait_ge(fe_ready, 1)
            link(nc.vector.tensor_tensor(ft[:, 3, :], ft[:, 1, :], ft[:, 2, :], ALU.subtract))
            link(nc.vector.tensor_tensor_scan(clog[:, 0, :], ones_row[:, :], ft[:, 3, :], 0.0, ALU.mult, ALU.add))
            nc.vector.tensor_scalar(clog[:, 1, :], clog[:, 0, :], -1.0, None, ALU.mult)
            dve.wait_ge(kc_ps, 1)
            nc.vector.tensor_copy(vcmp[0:NCMP, :, :], ps[0:NCMP, 7, 0:P].rearrange("p (g d) -> p g d", g=2))
            nc.vector.tensor_copy(kc_raw[:, :, 0:NCMP], ps[:, 6, 0:32].rearrange("p (g n) -> p g n", g=2)[:, :, 0:NCMP]).then_inc(kc_sb, 1)
            dve.wait_ge(kc_sb, 1)
            cc = tables_cmp[:, 0, :].unsqueeze(1).broadcast_to([P, 2, 16])
            cs = tables_cmp[:, 1, :].unsqueeze(1).broadcast_to([P, 2, 16])
            link(nc.vector.tensor_tensor(kcmp[:, :, :], kc_raw[:, :, :], cc, ALU.mult))
            dve.wait_ge(kcr_ps, 1)
            link(nc.vector.tensor_tensor(kc_raw[:, :, :], ps[:, 0, 0:32].rearrange("p (g n) -> p g n", g=2), cs, ALU.mult))
            link(nc.vector.tensor_tensor(kcmp[:, :, :], kcmp[:, :, :], kc_raw[:, :, :], ALU.add))
    attention(T, stack, proj, vtok, gates, clog, kcmp, vcmp, causal, mask_cmp, sel8)


FOX, CMP, SLC, WIN = range(4)


def attention(T, stack, proj, vtok, gates, clog, kcmp, vcmp, causal, mask_cmp, sel8):
    nc, A, ps, sem = T.nc, T.A, T.ps, T.sem
    ring = T.ring1
    yT = T.carve(2, 4, S)
    LB = 3
    lg = T.carve(LB, 4, S)
    stat = T.sb(stack, "stat", [P, LB, 4, 4])
    pT = T.carve(2, 4, 2, P)
    masked, max_ready, exp_done, p_ready = (sem(n) for n in ("att_masked", "att_max", "att_exp", "att_p"))
    scores, pt_ps, pt_sb, values_done, out_sb = (sem(n) for n in ("att_scores", "att_pt_ps", "att_pt_sb", "att_values", "att_out_sb"))
    units = [(t, hg, kind) for t in range(NT) for hg in range(2) for kind in (FOX, CMP, SLC, WIN)]
    sc = lambda n: ps[:, 2 * (n % 2):2 * (n % 2) + 2, :].rearrange("p a (b s) -> p a b s", b=2)
    slots = [(par, hp) for par in range(2) for hp in range(2)]
    width = lambda t, kind: NCMP if kind == CMP else P * (t + 1)
    quad = lambda ap: ap.rearrange("p (a b) s -> p a b s", a=2)

    def stages(*parts):
        for n in range(len(units) + len(parts) - 1):
            for lag, part in enumerate(parts):
                if part and 0 <= n - lag < len(units):
                    part(n - lag)

    with nc.Block() as block:
        @block.tensor
        def _(pe):
            def score(n):
                t, hg, kind = units[n]
                w = width(t, kind)
                if n >= 2:
                    pe.wait_ge(masked, n - 1)
                rows = slice(t * P, (t + 1) * P)
                for par, hp in slots:
                    lo, pair = DH * par, 2 * hg + hp
                    hd = 2 * pair + par
                    half = slice(lo, lo + DH)
                    dst = sc(n)[:, par, hp, 0:w]
                    if kind == FOX:
                        nc.tensor.matmul(dst, proj[half, FQ + pair, rows], proj[half, FK + pair, 0:w], start=True, stop=False)
                        nc.tensor.matmul(dst, clog[half, 0, rows], sel8[half, hd, 0:w], start=False, stop=False)
                        last = nc.tensor.matmul(dst, sel8[half, hd, 0:P], clog[half, 1, 0:w], start=False, stop=True)
                    else:
                        k = {CMP: kcmp[half, hg, 0:NCMP], SLC: proj[half, KSL + hg, 0:w], WIN: proj[half, KWN + hg, 0:w]}[kind]
                        last = nc.tensor.matmul(dst, proj[half, NQ + pair, rows], k, start=True, stop=True)
                last.then_inc(scores, 1)

            def transposes(n):
                t, hg, kind = units[n]
                pe.wait_ge(p_ready, n + 1)
                if n >= 1:
                    pe.wait_ge(pt_sb, n)
                blocks = 1 if kind == CMP else t + 1
                for q in range(4):
                    for b in range(blocks):
                        cols = slice(0, NCMP) if kind == CMP else slice(b * P, (b + 1) * P)
                        rows = NCMP if kind == CMP else P
                        at = ps[0:rows, 4 + q // 2, (q % 2) * S + b * P:(q % 2) * S + (b + 1) * P]
                        last = nc.tensor.transpose(at, lg[:, n % LB, q, cols], T.ident[:, :])
                last.then_inc(pt_ps, 1)

            def values(n):
                t, hg, kind = units[n]
                blocks = 1 if kind == CMP else t + 1
                pe.wait_ge(pt_sb, n + 1)
                first = kind in (FOX, CMP)
                done = sum(1 for u in units[:n] if u[2] in (FOX, WIN))
                if first and done:
                    pe.wait_ge(out_sb, done)
                for q, (par, hp) in enumerate(slots):
                    hl = 2 * hp + par
                    dst = ps[DH * par:DH * (par + 1), 6 + hp, 0:P]
                    for b in range(blocks):
                        v = {FOX: vtok[:, hg, b, hl * DH:(hl + 1) * DH], CMP: vcmp[0:NCMP, hg, :],
                             SLC: vtok[:, 2, b, hg * DH:(hg + 1) * DH],
                             WIN: vtok[:, 2, b, P + hg * DH:P + (hg + 1) * DH]}[kind]
                        rows = NCMP if kind == CMP else P
                        last = nc.tensor.matmul(dst, v, pT[0:rows, n % 2, q, b, :], start=(first and b == 0),
                                                stop=(kind in (FOX, WIN) and b == blocks - 1))
                last.then_inc(values_done, 1)

            stages(score, None, transposes, values)

        @block.vector
        def _(dve):
            link = T.link(dve, "dve", T.chain_dve)

            def mask_max(n):
                t, hg, kind = units[n]
                w = width(t, kind)
                dve.wait_ge(scores, n + 1)
                if n >= LB:
                    dve.wait_ge(pt_ps, n - LB + 1)
                if kind == CMP:
                    m = mask_cmp[:, 0, t, 0:w]
                else:
                    m = causal[:, S - w:S]
                x = lg[:, n % LB, :, 0:w]
                nc.vector.tensor_tensor(quad(x), sc(n)[:, :, :, 0:w],
                                        m.unsqueeze(1).unsqueeze(1).broadcast_to([P, 2, 2, w]), ALU.add).then_inc(masked, 1)
                dve.wait_ge(masked, n + 1)
                link(nc.vector.reduce_max(stat[:, n % LB, 0, :], x, AX.X))
                nc.vector.tensor_scalar(stat[:, n % LB, 1, :], stat[:, n % LB, 0, :], -SCALE, None, ALU.mult).then_inc(max_ready, 1)

            def normalise(n):
                t, hg, kind = units[n]
                w = width(t, kind)
                x = lg[:, n % LB, :, 0:w]
                dve.wait_ge(exp_done, 4 * (n + 1))
                link(nc.vector.reciprocal(stat[:, n % LB, 3, :], stat[:, n % LB, 2, :]))
                if kind != FOX:
                    g = gates[:, t, :].rearrange("p (g b a c) -> p g a b c", g=2, b=2, a=2)[:, hg, :, :, kind - 1]
                    r = stat[:, n % LB, 3, :].rearrange("p (a b) -> p a b", a=2)
                    link(nc.vector.tensor_tensor(r, r, g, ALU.mult))
                if kind == CMP:
                    m = mask_cmp[:, 1, t, 0:w].unsqueeze(1).broadcast_to([P, 4, w])
                    link(nc.vector.tensor_tensor(x, x, m, ALU.mult))
                nc.vector.tensor_tensor(x, x, stat[:, n % LB, 3, :].unsqueeze(2).broadcast_to([P, 4, w]), ALU.mult).then_inc(p_ready, 1)

            stages(mask_max, normalise)

        @block.scalar
        def _(act):
            def exps(n):
                t, hg, kind = units[n]
                w = width(t, kind)
                act.wait_ge(max_ready, n + 1)
                for q in range(4):
                    x = lg[:, n % LB, q, 0:w]
                    nc.scalar.activation(x, x, ACT.Exp, bias=stat[:, n % LB, 1, q:q + 1], scale=SCALE,
                                         accum_out=stat[:, n % LB, 2, q:q + 1]).then_inc(exp_done, 1)

            def evacuate(n):
                t, hg, kind = units[n]
                act.wait_ge(pt_ps, n + 1)
                if n >= 2:
                    act.wait_ge(values_done, n - 1)
                rows, blocks = (NCMP, 1) if kind == CMP else (P, t + 1)
                src = ps[0:rows, 4:6, :].rearrange("p c (q b s) -> p (c q) b s", q=2, b=2)[:, :, 0:blocks, :]
                nc.scalar.activation(pT[0:rows, n % 2, :, 0:blocks, :], src, ACT.Copy).then_inc(pt_sb, 1)

            def output(n):
                t, hg, kind = units[n]
                if kind in (FOX, WIN):
                    act.wait_ge(values_done, n + 1)
                    nc.scalar.activation(yT[:, kind == WIN, 2 * hg:2 * hg + 2, t * P:(t + 1) * P],
                                         ps[:, 6:8, 0:P], ACT.Copy).then_inc(out_sb, 1)

            stages(exps, None, evacuate, output)


    merged = T.carve(KB, S)
    mt = T.carve(2, 2, 2 * S)
    up_used, merge_ready, res_done = sem("up_used"), sem("merge_ready"), sem("res_done")
    h, ident = T.h, T.ident
    with nc.Block() as block:
        @block.sync
        def _(sync):
            for g in range(G_BRANCH + RING1, G_WQ + RING1):
                ring.issue(sync, g, T.stream1(g))

        @block.tensor
        def _(pe):
            for c in range(4):
                if c >= 2:
                    pe.wait_ge(up_used, 2 * (c - 1))
                for half in range(2):
                    g = G_BRANCH + 2 * c + half
                    ring.arrived(pe, g)
                    w = ring.piece(g).rearrange("p (k c) -> p k c", k=KB)
                    for n in range(2):
                        for k in range(4):
                            last = nc.tensor.matmul(ps[:, 2 * (c % 2) + n, half * S:(half + 1) * S], w[:, 4 * n + k, :],
                                                    yT[:, n, k, :], start=(k == 0), stop=(k == 3))
                    last.then_inc(ring.used, 1)
            pe.wait_ge(merge_ready, 4)
            for c in range(8):
                g = G_OUT + c
                ring.arrived(pe, g)
                w = ring.piece(g).rearrange("p (k c) -> p k c", k=KB)
                for t in range(NT):
                    at = t * S + (c % 2) * P
                    for k in range(KB):
                        last = nc.tensor.matmul(ps[:, 4 + c // 2, at:at + P], merged[:, k, t * P:(t + 1) * P],
                                                w[:, k, :], start=(k == 0), stop=(k == KB - 1))
                last.then_inc(ring.used, 1)

        @block.vector
        def _(dve):
            for c in range(4):
                dve.wait_ge(ring.used, G_BRANCH + 2 * (c + 1))
                if c >= 2:
                    dve.wait_ge(merge_ready, c - 1)
                for n in range(2):
                    gate = proj[:, MERGE + 8 * n + 2 * c:MERGE + 8 * n + 2 * c + 2, :].rearrange("p b s -> p (b s)")
                    nc.vector.tensor_tensor(mt[:, c % 2, n, :], ps[:, 2 * (c % 2) + n, :], gate, ALU.mult).then_inc(up_used, 1)
                dve.wait_ge(up_used, 2 * (c + 1))
                nc.vector.tensor_tensor(merged[:, 2 * c:2 * c + 2, :].rearrange("p b s -> p (b s)"),
                                        mt[:, c % 2, 0, :], mt[:, c % 2, 1, :], ALU.add).then_inc(merge_ready, 1)
            for c in range(4):
                dve.wait_ge(ring.used, G_OUT + 2 * (c + 1))
                x = h[:, :, 256 * c:256 * (c + 1)]
                nc.vector.tensor_tensor(x, x, ps[:, 4 + c, :].rearrange("p (t c) -> p t c", t=NT), ALU.add).then_inc(res_done, 1)
    stack.close()


def top16(T, dve, link, src, work, vals, idxs):
    nc = T.nc
    step = lambda f: [f(n) for n in range(len(src))][-1]
    link(step(lambda n: nc.vector.max(vals[n][:, 0:8], src[n])))
    step(lambda n: nc.vector.max_index(idxs[n][:, 0:8], vals[n][:, 0:8], src[n]))
    link(step(lambda n: nc.vector.match_replace(work[n], vals[n][:, 0:8], src[n], -3e38)))
    link(step(lambda n: nc.vector.max(vals[n][:, 8:16], work[n])))
    return link(step(lambda n: nc.vector.max_index(idxs[n][:, 8:16], vals[n][:, 8:16], work[n])))


def peer_in(T, high, low, bank):
    wh, wl = (x.rearrange("p (k e) -> p k e", k=KB) for x in (high, low))
    for k in range(KB):
        for m, (w, x) in enumerate(((wh, 0), (wh, 1), (wl, 0))):
            last = T.nc.tensor.matmul(T.ps[:, bank, 0:S], w[:, k, :], T.parts[:, x, k, :], start=(k == 0 and m == 0),
                                      stop=(k == KB - 1 and m == 2))
    return last


def peer(T):
    nc, A, ps, sem, ring = T.nc, T.A, T.ps, T.sem, T.ring1
    h, hT, ident = T.h, T.hT, T.ident
    arena = T.arena
    HK = HEADS * TOPK
    outer = ExitStack()
    keyT = T.sb(outer, "keyT", [P, 3, S])

    stack = ExitStack()
    qT = arena[:, 0:16 * S].rearrange("p (h s) -> p h s", h=16)
    dst = qT.rearrange("p (n c) s -> p n (c s)", c=2)

    def refill(sync):
        for g in range(G_WQ + RING1, G_EARLY):
            ring.issue(sync, g, T.stream1(g))

    front(T, "ffn", 1, ring, G_WQ, [("F", 8, dst, ACT.Copy)], lambda pe, done: None, refill,
          xs=arena[:, -NT * D:].rearrange("p (t d) -> p t d", t=NT))

    sc = arena[:, 4096:8192].rearrange("p (t n k) -> p t n k", t=NT, n=16)
    work = arena[:, 8192:12288].rearrange("p (t n k) -> p t n k", t=NT, n=16)
    cand = arena[:, 12288:14336].rearrange("p (h i j) -> p h i j", h=HEADS, i=TOPK)
    work2 = arena[:, 14336:16384].rearrange("p (h i) -> p h i", h=HEADS)
    eq = arena[:, 16384:18432].rearrange("p (m j) -> p m j", j=TOPK)
    v16 = arena[:, 19712:20224].rearrange("p (t n k) -> p t n k", t=NT, n=16)
    i16 = arena[:, 20224:20736].bitcast(U32).rearrange("p (t n k) -> p t n k", t=NT, n=16)
    i16f = arena[:, 18432:18944].rearrange("p (t n k) -> p t n k", t=NT, n=16)
    top = arena[:, 20736:20992].rearrange("p (t h k) -> p t h k", t=NT, h=HEADS)
    place = arena[:, 20992:21248].bitcast(U32).rearrange("p (t h k) -> p t h k", t=NT, h=HEADS)
    ab = arena[:, 21248:21504].bitcast(U32).rearrange("p (c k) -> p c k", c=2)
    abf = arena[:, 21504:21760].rearrange("p (c k) -> p c k", c=2)
    assert 21760 <= NFULL * S
    third = stack.enter_context(nc.sbuf_tensor("w_parts3", [P, 2, HW], F32R))
    early_part = lambda r, a: third[:, a, :] if r % 3 == 2 else T.w_parts[:, r % 3, a, :]
    key = arena[:, 18944:19712].rearrange("p (t c k) -> p t c k", t=NT, c=3)
    sm = T.sb(stack, "sm", [P, NT, HEADS])
    iota16 = T.sb(stack, "iota16", [P, TOPK])
    iota_loaded, sc_ps, sc_sb, w_sub, w_exp, key_ready, key_ps = (sem(n) for n in (
        "iota_loaded", "key_sc_ps", "key_sc_sb", "key_sub", "key_exp", "key_ready", "key_ps"))
    key_sb, early_high, early_low, early_ps, early_done = (sem(n) for n in (
        "key_sb", "early_high", "early_low", "early_ps", "early_done"))
    wt = arena[:, :].rearrange("p (a s) -> p a s", a=NKEYS)
    raw_early = lambda r: ring.piece(G_EARLY + r)
    E = 12
    with nc.Block() as block:
        @block.sync
        def _(sync):
            sync.dma_start(iota16[:, :], A["iota16"]).then_inc(iota_loaded, 16)

            def load(r, u):
                sync.dma_start(raw_early(r), A["peer"][u + NFULL, 0]).then_inc(ring.loaded[(G_EARLY + r) % RING1], 16)
            load(0, 0)
            load(1, 1)
            sync.wait_ge(sc_ps, 8)
            load(2, 2)
            load(3, 3)
            for u in range(4, E):
                sync.wait_ge(early_low, u - 3)
                load(u, u)
            with sync.Fori(1, NEARLY // E) as i:
                for r in range(E):
                    sync.wait_ge(early_low, i * E + (r - 3))
                    load(r, i * E + r)

        def early(eng, body):
            for r in range(E):
                body(r, 0, r)
            with eng.Fori(1, NEARLY // E) as i:
                for r in range(E):
                    body(r, i, i * E + r)

        @block.gpsimd
        def _(pool):
            def body(r, i, u):
                pool.wait_ge(early_high, u + 1)
                nc.gpsimd.tensor_tensor(early_part(r, 1), raw_early(r), early_part(r, 0).bitcast(F32),
                                        ALU.subtract).then_inc(early_low, 1)
            early(pool, body)

        @block.tensor
        def _(pe):
            for n in range(2):
                ring.arrived(pe, G_SUBK + n)
            for b in range(8):
                t, n0 = b // 4, 4 * (b % 4)
                for n in range(n0, n0 + 4):
                    sub = ring.piece(G_SUBK + n // 8).rearrange("p (h k) -> p h k", h=8)
                    last = nc.tensor.matmul(ps[:, b, (n - n0) * P:(n - n0 + 1) * P], qT[:, n, t * P:(t + 1) * P],
                                            sub[:, n % 8, :], start=True, stop=True)
                last.then_inc(sc_ps, 1)
            pe.wait_ge(sc_sb, 6)

            def body(r, i, u):
                pe.wait_ge(early_low, u + 1)
                if not (isinstance(u, int) and u < 2):
                    pe.wait_ge(early_done, u - 1)
                peer_in(T, early_part(r, 0), early_part(r, 1), 4 + r % 2).then_inc(early_ps, 1)
            early(pe, body)
            for t in range(NT):
                pe.wait_ge(key_ready, 2 * NT + t + 1)
                for c in range(3):
                    last = nc.tensor.transpose(ps[:, t, c * P:(c + 1) * P], key[:, t, c, :], ident[:, :])
                last.then_inc(key_ps, 1)

        @block.scalar
        def _(act):
            def high(r, i):
                ring.arrived(act, G_EARLY + r, i * (E // 4))
                nc.scalar.activation(early_part(r, 0), raw_early(r), ACT.Copy).then_inc(early_high, 1)
            high(0, 0)
            high(1, 0)
            for b in range(8):
                t, n0 = b // 4, 4 * (b % 4)
                act.wait_ge(sc_ps, b + 1)
                nc.scalar.activation(sc[:, t, n0:n0 + 4, :], ps[:, b, :].rearrange("p (n k) -> p n k", n=4),
                                     ACT.Copy).then_inc(sc_sb, 1)

            high(2, 0)

            def body(r, i, u, more=True):
                act.wait_ge(early_ps, u + 1)
                if more:
                    high((r + 3) % E, i + (r + 3) // E)
                nc.scalar.activation(wt[:, bass.ds(u + NFULL, 1), :].rearrange("p a s -> p (a s)"), ps[:, 4 + r % 2, 0:S],
                                     ACT.Gelu).then_inc(early_done, 1)
            with act.Fori(0, NEARLY // E - 1) as i:
                for r in range(E):
                    body(r, i, i * E + r)
            for r in range(E):
                body(r, NEARLY // E - 1, NEARLY - E + r, r < E - 3)
            for t in range(NT):
                act.wait_ge(w_sub, t + 1)
                nc.scalar.activation(key[:, t, 2, :], key[:, t, 2, :], ACT.Exp).then_inc(w_exp, 1)
            for t in range(NT):
                act.wait_ge(key_ps, t + 1)
                nc.scalar.activation(keyT[:, :, t * P:(t + 1) * P], ps[:, t, 0:3 * P].rearrange("p (c s) -> p c s", c=3),
                                     ACT.Copy).then_inc(key_sb, 1)

        @block.vector
        def _(dve):
            link = T.link(dve, "dve", T.chain_dve)
            dve.wait_ge(iota_loaded, 16)
            for t in range(NT):
                dve.wait_ge(sc_sb, 4 * (t + 1))
                top16(T, dve, link, [sc[:, t, n, :] for n in range(16)], [work[:, t, n, :] for n in range(16)],
                      [v16[:, t, n, :] for n in range(16)], [i16[:, t, n, :] for n in range(16)])
                nc.vector.tensor_copy(i16f[:, t, :, :], i16[:, t, :, :])
                halves = v16[:, t, :, :].rearrange("p (h c) k -> p h c k", c=2)
                full = [P, HEADS, TOPK, TOPK]
                link(nc.vector.tensor_tensor(cand[:, :, :, :], halves[:, :, 0, :].unsqueeze(3).broadcast_to(full),
                                             halves[:, :, 1, :].unsqueeze(2).broadcast_to(full), ALU.add))
                flat = cand[:, :, :, :].rearrange("p h i j -> p h (i j)")
                top16(T, dve, link, [flat[:, n, :] for n in range(HEADS)], [work2[:, n, :] for n in range(HEADS)],
                      [top[:, t, n, :] for n in range(HEADS)], [place[:, t, n, :] for n in range(HEADS)])
                flat_place = place[:, t, :, :].rearrange("p h k -> p (h k)")
                nc.vector.tensor_scalar(ab[:, 0, :], flat_place, 4, None, ALU.logical_shift_right)
                link(nc.vector.tensor_scalar(ab[:, 1, :], flat_place, 15, None, ALU.bitwise_and))
                link(nc.vector.tensor_copy(abf[:, :, :], ab[:, :, :]))
                idx = i16f[:, t, :, :].rearrange("p (h c) k -> p h c k", c=2)
                for c in range(2):
                    link(nc.vector.tensor_tensor(eq[:, :, :], abf[:, c, :].unsqueeze(2).broadcast_to([P, HK, TOPK]),
                                                 iota16[:, :].unsqueeze(1).broadcast_to([P, HK, TOPK]), ALU.is_equal))
                    by_head = eq[:, :, :].rearrange("p (h k) j -> p h k j", h=HEADS)
                    link(nc.vector.tensor_tensor(by_head, by_head, idx[:, :, c, :].unsqueeze(2).broadcast_to(full), ALU.mult))
                    nc.vector.reduce_sum(key[:, t, c, :], eq[:, :, :], AX.X).then_inc(key_ready, 1)
                    dve.wait_ge(key_ready, NT * t + c + 1)
                w = key[:, t, 2, :].rearrange("p (h k) -> p h k", h=HEADS)
                nc.vector.tensor_tensor(w, top[:, t, :, :], top[:, t, :, 0:1].broadcast_to([P, HEADS, TOPK]),
                                        ALU.subtract).then_inc(w_sub, 1)
            for t in range(NT):
                w = key[:, t, 2, :].rearrange("p (h k) -> p h k", h=HEADS)
                dve.wait_ge(w_exp, t + 1)
                link(nc.vector.reduce_sum(sm[:, t, :], w, AX.X))
                link(nc.vector.reciprocal(sm[:, t, :], sm[:, t, :]))
                nc.vector.tensor_tensor(w, w, sm[:, t, :].unsqueeze(2).broadcast_to([P, HEADS, TOPK]),
                                        ALU.mult).then_inc(key_ready, 1)
    stack.close()

    oh1 = T.sb(outer, "oh1", [P, 2, 4, NKEYS])
    oh2 = T.sb(outer, "oh2", [P, 2, 4, NKEYS])
    iota128 = T.sb(outer, "iota128", [P, NKEYS])
    wl = T.sb(outer, "w_late", [P, 2, 4, NEARLY])
    i128_loaded, oh1_ready, oh2_ready, oh2_abs, oh2_act, wt_ps, wt_sb, wl_sb, wl_used = (sem(n) for n in (
        "i128_loaded", "oh1_ready", "oh2_ready", "oh2_abs", "oh2_act", "wt_ps", "wt_sb", "wl_sb", "wl_used"))
    with nc.Block() as block:
        @block.sync
        def _(sync):
            sync.dma_start(iota128[:, :], A["iota128"]).then_inc(i128_loaded, 16)
            for g in range(G_PEER, G_PEER + RING1):
                sync.dma_start(ring.piece(g), A["peer"][(g - G_PEER) // 2, (g - G_PEER) % 2]).then_inc(ring.loaded[g % RING1], 16)

        steps = S // 4

        def tokens(eng, body):
            for r in range(2):
                body(r, r, 0, True)
            with eng.Fori(1, steps // 2) as i:
                for r in range(2):
                    body(i * 2 + r, r, i, False)

        @block.vector
        def _(dve):
            dve.wait_ge(i128_loaded, 16)

            def body(n, r, i, first):
                if not first:
                    dve.wait_ge(wt_ps, i * 2 + (r - 1))
                base = n * 4
                for q in range(2):
                    last = nc.vector.tensor_scalar(oh2[:, r, q, :], iota128[:, :], keyT[:, 1, bass.ds(base + q, 1)], None, ALU.is_equal)
                last.then_inc(oh2_ready, 1)
                for q in range(4):
                    last = nc.vector.tensor_scalar(oh1[:, r, q, :], iota128[:, :], keyT[:, 0, bass.ds(base + q, 1)],
                                                   keyT[:, 2, bass.ds(base + q, 1)], ALU.is_equal, ALU.mult)
                last.then_inc(oh1_ready, 1)
            tokens(dve, body)

        @block.gpsimd
        def _(pool):
            def body(n, r, i, first):
                pool.wait_ge(wl_sb, i * 2 + (r + 1))
                x = wt[:, NFULL:, bass.ds(n * 4, 4)].rearrange("p a s -> p s a")
                nc.gpsimd.tensor_tensor(x, x, wl[:, r, :, :], ALU.mult).then_inc(wl_used, 1)
            tokens(pool, body)

        @block.tensor
        def _(pe):
            def body(n, r, i, first):
                pe.wait_ge(oh2_ready, i * 2 + (r + 1))
                pe.wait_ge(oh2_act, i * 2 + (r + 1))
                pe.wait_ge(oh1_ready, i * 2 + (r + 1))
                if not first:
                    pe.wait_ge(wl_sb, i * 2 + (r - 1))
                for q in range(4):
                    last = nc.tensor.matmul(ps[:, r, q * P:(q + 1) * P], oh2[:, r, q, :], oh1[:, r, q, :], start=True, stop=True)
                last.then_inc(wt_ps, 1)
            tokens(pe, body)

        @block.scalar
        def _(act):
            def distance(n, r):
                for q in range(2, 4):
                    last = nc.scalar.activation(oh2[:, r, q, :], iota128[:, :], ACT.Abs, bias=keyT[:, 1, bass.ds(n * 4 + q, 1)],
                                                scale=-1.0)
                last.then_inc(oh2_abs, 1)

            def onehot(r, i):
                act.wait_ge(oh2_abs, i * 2 + (r + 1))
                nc.scalar.activation(oh2[:, r, 2:4, :], oh2[:, r, 2:4, :], ACT.Relu, bias=1.0, scale=-1.0).then_inc(oh2_act, 1)

            def out(n, r, i, first):
                act.wait_ge(wt_ps, i * 2 + (r + 1))
                w = ps[:, r, :].rearrange("p (s a) -> p s a", s=4)
                nc.scalar.activation(wt[:, 0:NFULL, bass.ds(n * 4, 4)].rearrange("p a s -> p s a"), w[:, :, 0:NFULL],
                                     ACT.Copy).then_inc(wt_sb, 1)
                if not first:
                    act.wait_ge(wl_used, i * 2 + (r - 1))
                nc.scalar.activation(wl[:, r, :, :], w[:, :, NFULL:], ACT.Copy).then_inc(wl_sb, 1)

            act.wait_ge(i128_loaded, 16)
            distance(0, 0)
            onehot(0, 0)
            distance(1, 1)

            def turn(i, first):
                onehot(1, i - 1)
                act.wait_ge(wt_ps, i * 2 - 1)
                distance(i * 2, 0)
                out(i * 2 - 2, 0, i - 1, first)
                onehot(0, i)
                act.wait_ge(wt_ps, i * 2)
                distance(i * 2 + 1, 1)
                out(i * 2 - 1, 1, i - 1, first)
            turn(1, True)
            with act.Fori(2, steps // 2) as i:
                turn(i, False)
            onehot(1, steps // 2 - 1)
            out(steps - 2, 0, steps // 2 - 1, False)
            out(steps - 1, 1, steps // 2 - 1, False)

    outer.close()
    T.hT_stack.close()
    stack = ExitStack()
    part = lambda name, *shape: stack.enter_context(nc.sbuf_tensor(name, [P, *shape], F32R))
    uh, ul = T.w_parts[:, :, 0, :], T.w_parts[:, :, 1, :]
    vh, vl = (part(n, 2, HW) for n in ("v_high", "v_low"))
    ch, cl = part("coef_high", 2, S), part("coef_low", 2, S)
    coef = T.sb(stack, "coef", [P, 2, S])
    names = ("uh", "ul", "vh", "vl", "a_ps", "gelu", "coef", "ch", "cl", "o_done", "res")
    uh_ready, ul_ready, vh_ready, vl_ready, a_ps, gelu_ready, coef_ready, ch_ready, cl_ready, o_done, peer_res = (
        sem(f"peer_{n}") for n in names)
    raw_u = lambda r: ring.piece(G_PEER + 2 * (r % 2))
    raw_v = lambda r: ring.piece(G_PEER + 2 * (r % 2) + 1)
    TURNS = NFULL // 2

    def steps(eng, step):
        step(0, 0, 2)
        step(1, 0, 2)
        with eng.Fori(1, TURNS - 1) as i:
            step(0, i, 2)
            step(1, i, 2)
        step(0, TURNS - 1, 1)
        step(1, TURNS - 1, 0)

    def late(eng, body):
        with eng.Fori(0, NEARLY // 4) as i:
            for r in range(4):
                body(r, i, i * 4 + (NFULL + r))

    raw_late = lambda r: ring.piece(G_LATE + r)
    late_coef = lambda n: wt[:, bass.ds(n, 1), :].rearrange("p a s -> p (a s)")
    is_first = lambda n: isinstance(n, int) and n == 0

    with nc.Block() as block:
        @block.sync
        def _(sync):
            with sync.Fori(1, TURNS) as i:
                for r in range(4):
                    sync.wait_ge(vl_ready if r % 2 else ul_ready, i * 2 + (r // 2 - 1))
                    sync.dma_start(ring.piece(G_PEER + r), A["peer"][i * 2 + r // 2, r % 2]).then_inc(ring.loaded[(G_PEER + r) % RING1], 16)

            def load(r, j):
                sync.dma_start(raw_late(r), A["peer"][j + NFULL, 1]).then_inc(ring.loaded[(G_LATE + r) % RING1], 16)
            for r in range(4):
                sync.wait_ge(vl_ready if r % 2 else ul_ready, NFULL + (r // 2 - 1))
                load(r, r)
            with sync.Fori(1, NEARLY // 4) as i:
                for r in range(4):
                    sync.wait_ge(vl_ready, i * 4 + (NFULL + r - 3))
                    load(r, i * 4 + r)

        @block.scalar
        def _(act):
            def u_high(r, turn):
                ring.arrived(act, G_PEER + 2 * (r % 2), turn)
                nc.scalar.activation(uh[:, r % 2, :], raw_u(r), ACT.Copy).then_inc(uh_ready, 1)

            def v_high(r, turn):
                ring.arrived(act, G_PEER + 2 * (r % 2) + 1, turn)
                nc.scalar.activation(vh[:, r % 2, :], raw_v(r), ACT.Copy).then_inc(vh_ready, 1)

            def activate(r, n):
                act.wait_ge(a_ps, n + 1)
                nc.scalar.activation(coef[:, r % 2, :], ps[:, 4 + r % 2, 0:S], ACT.Gelu).then_inc(gelu_ready, 1)
                act.wait_ge(coef_ready, n + 1)
                nc.scalar.activation(ch[:, r % 2, :], coef[:, r % 2, :], ACT.Copy).then_inc(ch_ready, 1)

            u_high(0, 0)
            u_high(1, 0)
            v_high(0, 0)
            activate(0, 0)

            def step(r, i, into):
                n = i * 2 + r
                if into == 2:
                    act.wait_ge(a_ps, n + 1)
                    u_high(r, i + 1)
                if into:
                    if not is_first(n):
                        act.wait_ge(o_done, n)
                    v_high(r + 1, i + (r + 1) // 2)
                    activate(r + 1, n + 1)
            steps(act, step)

            def late_high(r, i, n):
                act.wait_ge(o_done, n - 1)
                ring.arrived(act, G_LATE + r, i)
                nc.scalar.activation(vh[:, r % 2, :], raw_late(r), ACT.Copy).then_inc(vh_ready, 1)
                nc.scalar.activation(ch[:, r % 2, :], late_coef(n), ACT.Copy).then_inc(ch_ready, 1)
            late(act, late_high)

        @block.vector
        def _(dve):
            def u_low(r, n):
                dve.wait_ge(uh_ready, n + 1)
                nc.vector.tensor_tensor(ul[:, r % 2, :], raw_u(r), uh[:, r % 2, :].bitcast(F32), ALU.subtract).then_inc(ul_ready, 1)

            def v_low(r, n):
                dve.wait_ge(vh_ready, n + 1)
                nc.vector.tensor_tensor(vl[:, r % 2, :], raw_v(r), vh[:, r % 2, :].bitcast(F32), ALU.subtract).then_inc(vl_ready, 1)

            def weigh(r, n):
                dve.wait_ge(gelu_ready, n + 1)
                c = coef[:, r % 2, :]
                nc.vector.tensor_tensor(c, c, wt[:, bass.ds(n, 1), :].rearrange("p a s -> p (a s)"), ALU.mult).then_inc(coef_ready, 1)
                dve.wait_ge(ch_ready, n + 1)
                nc.vector.tensor_tensor(cl[:, r % 2, :], c, ch[:, r % 2, :].bitcast(F32), ALU.subtract).then_inc(cl_ready, 1)

            u_low(0, 0)
            u_low(1, 1)
            v_low(0, 0)
            weigh(0, 0)

            def step(r, i, into):
                n = i * 2 + r
                if into == 2:
                    u_low(r, n + 2)
                if into:
                    v_low(r + 1, n + 1)
                    weigh(r + 1, n + 1)
            steps(dve, step)

            def late_low(r, i, n):
                dve.wait_ge(vh_ready, n + 1)
                nc.vector.tensor_tensor(vl[:, r % 2, :], raw_late(r), vh[:, r % 2, :].bitcast(F32), ALU.subtract).then_inc(vl_ready, 1)
                dve.wait_ge(ch_ready, n + 1)
                nc.vector.tensor_tensor(cl[:, r % 2, :], late_coef(n), ch[:, r % 2, :].bitcast(F32), ALU.subtract).then_inc(cl_ready, 1)
            late(dve, late_low)
            dve.wait_ge(o_done, NKEYS)
            for t in range(NT):
                nc.vector.tensor_tensor(h[:, t, :], h[:, t, :], ps[:, 2 * t:2 * t + 2, :].rearrange("p b d -> p (b d)"),
                                        ALU.add).then_inc(peer_res, 1)

        @block.tensor
        def _(pe):
            def expert_in(r, n):
                pe.wait_ge(ul_ready, n + 1)
                b = r % 2
                peer_in(T, uh[:, b, :], ul[:, b, :], 4 + b).then_inc(a_ps, 1)

            def expert_out(r, n):
                pe.wait_ge(vl_ready, n + 1)
                pe.wait_ge(cl_ready, n + 1)
                b = r % 2
                for t in range(NT):
                    for m, (cc, w) in enumerate(((ch, vh), (ch, vl), (cl, vh))):
                        for half in range(2):
                            last = nc.tensor.matmul(ps[:, 2 * t + half, :], cc[:, b, t * P:(t + 1) * P],
                                                    w[:, b, half * BANK:(half + 1) * BANK], start=(m == 0 and is_first(n)),
                                                    stop=(m == 2), skip_group_check=True)
                last.then_inc(o_done, 1)

            expert_in(0, 0)

            def step(r, i, into):
                n = i * 2 + r
                if into:
                    expert_in(r + 1, n + 1)
                expert_out(r, n)
            steps(pe, step)
            late(pe, lambda r, i, n: expert_out(r, n))
    stack.close()


def norm_tokens(T, name, sync_extra=None, add_banks=False, store=None):
    nc, A, ps, sem, h, ss = T.nc, T.A, T.ps, T.sem, T.h, T.ss
    stack = ExitStack()
    gain = T.sb(stack, f"{name}_gain", [P, D])
    junk = T.sb(stack, f"{name}_junk", [P, D])
    gain_loaded, summed, squares, mean, root, normed, out_stored = (sem(f"{name}_{s}") for s in (
        "gain_loaded", "summed", "squares", "mean", "root", "normed", "stored"))
    with nc.Block() as block:
        @block.sync
        def _(sync):
            sync.dma_start(gain[:, :], A[name]).then_inc(gain_loaded, 16)
            if sync_extra:
                sync_extra(sync)
            if store is not None:
                for t in range(NT):
                    sync.wait_ge(normed, t + 1)
                    sync.dma_start(store[t * P:(t + 1) * P, :], h[:, t, :]).then_inc(out_stored, 16)
                sync.wait_ge(out_stored, 16 * NT)

        @block.scalar
        def _(act):
            if add_banks:
                act.wait_ge(summed, NT)
            for t in range(NT):
                nc.scalar.activation(junk[:, :], h[:, t, :], ACT.Square, accum_out=ss[:, t:t + 1]).then_inc(squares, 1)
                act.wait_ge(squares, t + 1)
            act.wait_ge(mean, 1)
            nc.scalar.activation(ss[:, 2:4], ss[:, 2:4], ACT.Sqrt).then_inc(root, 1)

        @block.vector
        def _(dve):
            link = T.link(dve, "dve", T.chain_dve)
            if add_banks:
                for t in range(NT):
                    nc.vector.tensor_tensor(h[:, t, :], h[:, t, :], ps[:, 2 * t:2 * t + 2, :].rearrange("p b d -> p (b d)"),
                                            ALU.add).then_inc(summed, 1)
                dve.wait_ge(summed, NT)
            dve.wait_ge(squares, NT)
            nc.vector.tensor_scalar(ss[:, 2:4], ss[:, 0:2], 1.0 / D, EPS, ALU.mult, ALU.add).then_inc(mean, 1)
            dve.wait_ge(root, 1)
            link(nc.vector.reciprocal(ss[:, 2:4], ss[:, 2:4]))
            dve.wait_ge(gain_loaded, 16)
            for t in range(NT):
                nc.vector.scalar_tensor_tensor(h[:, t, :], h[:, t, :], ss[:, 2 + t:3 + t], gain[:, :], ALU.mult,
                                               ALU.mult).then_inc(normed, 1)
    stack.close()


DHEADS, DK, CH = 4, 128, 64
NU = NT * 2 * DHEADS
G2_OUT, G2_EXP = 10, 14
LEVELS = 6


def second_block(T):
    nc, A, ps, sem = T.nc, T.A, T.ps, T.sem
    h, hT, ident = T.h, T.hT, T.ident
    ring = T.ring2 = Ring(T.arena[:, 0:RING2 * PW].rearrange("p (n c) -> p n c", n=RING2), RING2, *T.ring2_sems)
    high = T.arena[:, RING2 * PW:]

    def start_ring(sync):
        for g in range(RING2):
            ring.issue(sync, g, A["stream2"][g])

    norm_tokens(T, "norm_final", start_ring)

    stack = ExitStack()
    sb = lambda name, *shape: T.sb(stack, name, [P, *shape])
    high_c = Carve(high)
    utok = high_c(2, NT, 256)
    pool_m = high_c(NT, 4, S)
    qkv = high_c(12, S)
    more = Carve(high[:, 8192:])
    vT = more(DHEADS, S)
    xs = more(NT, D)
    dp = more(4, S)
    z = more(DHEADS, S)
    oT = more(KB, S)
    masks = sb("masks", 2, LEVELS + 1, P)
    same_chunk = sb("same_chunk", P)
    ones = sb("ones", P)
    conv_w = sb("conv_w", 12, 5)
    ab_w = sb("ab_w", KB, 16)
    pool_w = sb("pool_w", 4, P)
    pool_scale = sb("pool_scale", 4)
    head_norm = sb("head_norm", 1)
    a_log = sb("a_log", 8)
    dt_bias = sb("dt_bias", 8)
    tok2 = sb("tok2", 2, NT, DHEADS, P)
    loads = [(pool_m, "pool_m"), (masks[:, :, :, :], "masks"), (same_chunk[:, :], "same_chunk"), (ones[:, :], "ones"),
             (conv_w[:, :, :], "conv_w"), (ab_w[:, :, :], "ab_w"), (pool_w[:, :, :], "pool_w"),
             (pool_scale[:, :], "pool_scale"), (head_norm[:, :], "head_norm"), (a_log[:, :], "a_log"),
             (dt_bias[:, :], "dt_bias")]
    c2 = sem("second_consts")

    def refill(sync):
        for dst, name in loads:
            sync.dma_start(dst, A[name]).then_inc(c2, 16)
        for g in range(RING2, G2_OUT + RING2):
            ring.issue(sync, g, T.stream2(g))

    def small(pe, done):
        pe.wait_ge(c2, 16 * len(loads))
        for t in range(NT):
            for k in range(KB):
                last = nc.tensor.matmul(ps[:, 4, t * 16:(t + 1) * 16], hT[:, k, t * P:(t + 1) * P], ab_w[:, k, :],
                                        start=(k == 0), stop=(k == KB - 1))
        last.then_inc(done, 1)

    split_stack = ExitStack()
    split_tiles(T, split_stack, "second")
    front(T, "mix2", 2, ring, 0, [("F", 6, qkv.rearrange("p (n c) s -> p n (c s)", c=2), ACT.Copy),
                                  ("F", 2, z[:, :, :].rearrange("p (n c) s -> p n (c s)", c=2), ACT.Silu),
                                  ("T", 2, utok.rearrange("p n t c -> p n (t c)"), ACT.Copy)], small, refill, xs=xs)

    split_stack.close()
    T.low = T.sb(stack, "low", [P, 4 * PW])
    low_c = Carve(T.low)
    sq = low_c(8, S)
    diag = low_c(16, P)
    taps = low_c(DHEADS, 5, P)
    rs = sb("rs", 16)
    qk_high = Carve(high)
    qk_high(6144)
    qkT = qk_high(2, DHEADS, S)
    part = lambda i: (qkT[:, i, :, :], qkT[:, i, :, :], vT[:, :, :])[i] if i < 2 else vT[:, :, :]
    abr = sb("abr", 6, NT, 2, DHEADS)
    beta, g_ = abr[:, 4, :, :, :], abr[:, 5, :, :, :]
    centre, conv_done, silu_done, sq_ready, ss_ps, ss_sb, root, kv_ready, kv_ps, kv_sb = (sem(f"conv_{n}") for n in (
        "centre", "done", "silu", "sq", "ss_ps", "ss_sb", "root", "ready", "kv_ps", "kv_sb"))
    taps_ready, v_ps, v_silu, diag_ready, bc_ps, ab_in = (sem(f"conv_{n}") for n in ("taps", "v_ps", "v_silu", "diag", "bc_ps", "ab_in"))
    pool_ps, pool_sb, pool2_ps, g_in, g_exp, al_exp, a_in = (sem(f"pl_{n}") for n in ("ps", "sb", "ps2", "g_in", "g_exp", "al_exp", "a_in"))
    with nc.Block() as block:
        @block.scalar
        def _(act):
            link = T.link(act, "act", T.chain_act)
            for b in range(8):
                nc.scalar.activation(part(b // 4)[:, b % 4, :], qkv[:, b, :], ACT.Copy, scale=conv_w[:, b, 2:3]).then_inc(centre, 1)
            for b in range(DHEADS):
                for tap in range(5):
                    last = nc.scalar.activation(taps[:, b, tap, :], ident[:, :], ACT.Copy, scale=conv_w[:, 8 + b, tap:tap + 1])
                last.then_inc(taps_ready, 1)
            ab = ps[:, 4, 0:32].rearrange("p (t d c h) -> p t d c h", t=NT, d=2, c=2)
            nc.scalar.activation(abr[:, 0, :, :, :], ab[:, :, :, 0, :], ACT.Copy).then_inc(a_in, 1)
            nc.scalar.activation(beta, ab[:, :, :, 1, :], ACT.Sigmoid).then_inc(ab_in, 1)
            act.wait_ge(conv_done, 1)
            nc.scalar.activation(part(0), part(0), ACT.Silu).then_inc(silu_done, 1)
            for i in range(2):
                act.wait_ge(v_ps, i + 1)
                nc.scalar.activation(vT[:, 2 * i:2 * i + 2, :].rearrange("p a s -> p (a s)"), ps[:, 5 + i, :], ACT.Silu).then_inc(v_silu, 1)
            act.wait_ge(conv_done, 2)
            nc.scalar.activation(part(1), part(1), ACT.Silu).then_inc(silu_done, 1)
            act.wait_ge(g_in, 1)
            link(nc.scalar.activation(abr[:, 1, :, :, :], abr[:, 0, :, :, :], ACT.Abs))
            link(nc.scalar.activation(abr[:, 1, :, :, :], abr[:, 1, :, :, :], ACT.Exp, scale=-1.0))
            nc.scalar.activation(a_log[:, :], a_log[:, :], ACT.Exp).then_inc(al_exp, 1)
            nc.scalar.activation(abr[:, 1, :, :, :], abr[:, 1, :, :, :], ACT.Ln, bias=1.0).then_inc(g_exp, 1)
            act.wait_ge(ss_sb, 1)
            nc.scalar.activation(rs[:, :], rs[:, :], ACT.Sqrt).then_inc(root, 1)
            for n, b in enumerate((2, 3, 0, 1)):
                act.wait_ge(kv_ps, n + 1)
                nc.scalar.activation(tok2[:, b // 2, b % 2, :, :], ps[:, 4 + b, :].rearrange("p (h d) -> p h d", h=DHEADS),
                                     ACT.Copy).then_inc(kv_sb, 1)
            act.wait_ge(pool_ps, 4)
            nc.scalar.activation(dp[:, :, :].rearrange("p g s -> p (g s)"), ps[:, 0:2, :].rearrange("p b c -> p (b c)"),
                                 ACT.Copy).then_inc(pool_sb, 1)
            act.wait_ge(pool2_ps, 1)
            for i in range(4):
                nc.scalar.activation(oT[:, 4 + i, :], ps[:, 2 + i // 2, (i % 2) * S:(i % 2 + 1) * S], ACT.Copy, scale=pool_scale[:, i:i + 1])

        @block.vector
        def _(dve):
            link = T.link(dve, "dve", T.chain_dve)
            for i in range(2):
                dve.wait_ge(centre, 4 * (i + 1))
                for tap in (0, 1, 3, 4):
                    off = tap - 2
                    lo, hi = max(0, -off), min(S, S - off)
                    for b in range(4 * i, 4 * i + 4):
                        y = part(i)[:, b % 4, lo:hi]
                        last = nc.vector.scalar_tensor_tensor(y, qkv[:, b, lo + off:hi + off], conv_w[:, b, tap:tap + 1], y,
                                                              ALU.mult, ALU.add)
                    if tap < 4:
                        link(last)
                    else:
                        last.then_inc(conv_done, 1)
            dve.wait_ge(a_in, 1)
            dtb = dt_bias[:, :].rearrange("p (d h) -> p d h", d=2).unsqueeze(1).broadcast_to([P, NT, 2, DHEADS])
            nc.vector.tensor_tensor(abr[:, 0, :, :, :], abr[:, 0, :, :, :], dtb, ALU.add).then_inc(g_in, 1)
            flat = qkT.rearrange("p c h s -> p (c h) s")
            for i in range(2):
                dve.wait_ge(silu_done, i + 1)
                half = flat[:, 4 * i:4 * i + 4, :]
                nc.vector.tensor_tensor(sq[:, 4 * i:4 * i + 4, :], half, half, ALU.mult).then_inc(sq_ready, 1)
            dve.wait_ge(ss_ps, 1)
            nc.vector.tensor_scalar(rs[:, :], ps[:, 0, 0:16], EPS, None, ALU.add).then_inc(ss_sb, 1)
            dve.wait_ge(root, 1)
            link(nc.vector.reciprocal(rs[:, :], rs[:, :]))
            link(nc.vector.tensor_scalar(rs[:, 0:8], rs[:, 0:8], DK ** -0.5, None, ALU.mult))
            for i in range(2):
                nc.vector.tensor_tensor(diag[:, 8 * i:8 * i + 8, :], ident[:, :].unsqueeze(1).broadcast_to([P, 8, P]),
                                        rs[:, 8 * i:8 * i + 8].unsqueeze(2).broadcast_to([P, 8, P]), ALU.mult).then_inc(diag_ready, 1)
            dve.wait_ge(g_in, 1)
            dve.wait_ge(g_exp, 1)
            link(nc.vector.scalar_tensor_tensor(abr[:, 2, :, :, :], abr[:, 0, :, :, :], 0.0, abr[:, 1, :, :, :], ALU.max, ALU.add))
            dve.wait_ge(al_exp, 1)
            alb = a_log[:, :].rearrange("p (d h) -> p d h", d=2).unsqueeze(1).broadcast_to([P, NT, 2, DHEADS])
            nc.vector.scalar_tensor_tensor(g_, abr[:, 2, :, :, :], -1.0, alb, ALU.mult, ALU.mult)
            for b in range(4):
                dve.wait_ge(bc_ps, b + 1)
                two = flat[:, 2 * b:2 * b + 2, :]
                nc.vector.tensor_tensor(two, two, ps[:, b, :].rearrange("p (a s) -> p a s", a=2), ALU.mult).then_inc(kv_ready, 1)

        @block.tensor
        def _(pe):
            for b in range(DHEADS):
                pe.wait_ge(taps_ready, b + 1)
                for n, tap in enumerate((2, 0, 1, 3, 4)):
                    off = tap - 2
                    lo, hi = max(0, -off), min(S, S - off)
                    at = (b % 2) * S
                    last = nc.tensor.matmul(ps[:, 5 + b // 2, at + lo:at + hi], taps[:, b, tap, :], qkv[:, 8 + b, lo + off:hi + off],
                                            start=(n == 0), stop=(n == 4), skip_group_check=True)
                if b % 2:
                    last.then_inc(v_ps, 1)
            for i in range(2):
                pe.wait_ge(sq_ready, i + 1)
                for a in range(4 * i, 4 * i + 4):
                    for t in range(NT):
                        last = nc.tensor.matmul(ps[:, 0, a * NT + t:a * NT + t + 1], sq[:, a, t * P:(t + 1) * P], ones[:, 0:1],
                                                start=True, stop=True)
            last.then_inc(ss_ps, 1)
            for b in range(4):
                pe.wait_ge(diag_ready, b // 2 + 1)
                nc.tensor.matmul(ps[:, b, :], ones[:, :], diag[:, 4 * b:4 * b + 4, :].rearrange("p a c -> p (a c)"),
                                 start=True, stop=True).then_inc(bc_ps, 1)
            pe.wait_ge(v_silu, 2)
            pe.wait_ge(ab_in, 1)
            for b in (2, 3, 0, 1):
                if b == 0:
                    pe.wait_ge(kv_ready, 4)
                src = (qkT[:, 1, :, :], vT[:, :, :])[b // 2]
                for hd in range(DHEADS):
                    last = nc.tensor.transpose(ps[:, 4 + b, hd * P:(hd + 1) * P], src[:, hd, (b % 2) * P:(b % 2 + 1) * P], ident[:, :])
                last.then_inc(kv_ps, 1)
            for i in range(4):
                for t in range(NT):
                    last = nc.tensor.matmul(ps[:, i // 2, (i % 2) * S:(i % 2 + 1) * S], utok[:, i // 2, t, (i % 2) * P:(i % 2 + 1) * P],
                                            pool_m[:, t, i, :], start=(t == 0), stop=(t == NT - 1))
                last.then_inc(pool_ps, 1)
            pe.wait_ge(pool_sb, 1)
            for i in range(4):
                last = nc.tensor.matmul(ps[:, 2 + i // 2, (i % 2) * S:(i % 2 + 1) * S], pool_w[:, i, :], dp[:, i, :], start=True, stop=True)
            last.then_inc(pool2_ps, 1)
    delta(T, stack, z, oT, masks, same_chunk, ones, head_norm, tok2, qkT, beta, g_)


def delta(T, stack, z, oT, masks, same_chunk, ones, head_norm, tok2, qkT, beta, g_):
    nc, A, ps, sem = T.nc, T.A, T.ps, T.sem
    h, ident, ring = T.h, T.ident, T.ring2
    low_c = Carve(T.low[:, :])
    high_c = Carve(T.arena[:, RING2 * PW:])
    kb_, vb, kdec, qdec = (low_c(NU, P) for _ in range(4))
    at, qkm, eg = (high_c(NU, P) for _ in range(3))
    x_, xT = eg, high_c(NU, P)
    gbc, bbc = kb_, vb
    scal = T.sb(stack, "scal", [P, 6, NU])
    egl = T.sb(stack, "egl", [P, NT, 2, 2, DHEADS])
    grp = lambda x, b: x[:, 4 * b:4 * b + 4, :]
    bank4 = lambda b: ps[:, b, :].rearrange("p (h c) -> p h c", h=DHEADS)
    inc = lambda d: masks[:, d, LEVELS, :]
    names = ("bc_ready", "cum_ps", "scal_sb", "scal_exp", "row_ps", "eg_ready", "d2_in", "d2_ready", "brow_used", "kq_ps", "at_ready",
             "egl_ready", "mats_ready")
    bc_ready, cum_ps, scal_sb, scal_exp, row_ps, eg_ready, d2_in, d2_ready, brow_used, kq_ps, at_ready, egl_ready, mats_ready = (
        sem(f"dl_{n}") for n in names)
    all_units = lambda x: x.rearrange("p t d h -> p (t d h)")
    with nc.Block() as block:
        @block.vector
        def _(dve):
            link = T.link(dve, "dve", T.chain_dve)
            nc.vector.tensor_copy(gbc, all_units(g_).unsqueeze(2).broadcast_to([P, NU, P])).then_inc(bc_ready, 1)
            nc.vector.tensor_copy(bbc, all_units(beta).unsqueeze(2).broadcast_to([P, NU, P])).then_inc(bc_ready, 1)
            dve.wait_ge(cum_ps, 1)
            link(nc.vector.tensor_copy(scal[:, 0:2, :].rearrange("p a u -> p (a u)"), ps[:, 0, 0:2 * NU]))
            nc.vector.tensor_tensor(scal[:, 2, :], scal[:, 1, :], scal[:, 0, :], ALU.subtract).then_inc(scal_sb, 1)
            for b in range(4):
                dve.wait_ge(row_ps, b + 1)
                dve.wait_ge(eg_ready, b + 1)
                for u in range(4 * b, 4 * b + 4):
                    last = nc.vector.tensor_scalar(qkm[:, u, :], ps[:, b, (u % 4) * P:(u % 4 + 1) * P], scal[:, 0, u:u + 1], 0.0,
                                                   ALU.subtract, ALU.min)
                last.then_inc(d2_in, 1)
            for b in range(4):
                dve.wait_ge(d2_ready, b + 1)
                dve.wait_ge(row_ps, 4 + b + 1)
                nc.vector.tensor_tensor(grp(at, b), grp(qkm, b), bank4(4 + b), ALU.mult).then_inc(brow_used, 1)
            dve.wait_ge(brow_used, 4)
            for b in range(4):
                dve.wait_ge(kq_ps, 2 * (b // 2) + 1)
                nc.vector.tensor_tensor(grp(at, b), grp(at, b), bank4(b // 2), ALU.mult).then_inc(at_ready, 1)
                dve.wait_ge(kq_ps, 2 * (b // 2) + 2)
                link(nc.vector.tensor_tensor(grp(qkm, b), grp(qkm, b), bank4(2 + b // 2), ALU.mult))
                nc.vector.tensor_tensor(grp(qkm, b), grp(qkm, b), inc(b % 2).unsqueeze(1).broadcast_to([P, 4, P]), ALU.mult)
            dve.wait_ge(scal_exp, 2)
            link(nc.vector.tensor_tensor(scal[:, 3, :], scal[:, 4, :], all_units(beta), ALU.mult))

        @block.gpsimd
        def _(pool):
            pool.wait_ge(eg_ready, 4)
            for d in range(2):
                for t in range(NT):
                    u = (2 * t + d) * 4
                    col = 63 if d == 0 else 0
                    ends = eg[:, u:u + 4, :].rearrange("p h (c s) -> p c h s", c=2)[:, :, :, col]
                    last = nc.gpsimd.tensor_copy(egl[:, t, d, :, :], ends)
            last.then_inc(egl_ready, 1)
            for b in range(4):
                nc.gpsimd.tensor_tensor(grp(qdec, b), qkT[:, 0, :, (b // 2) * P:(b // 2 + 1) * P], grp(eg, b), ALU.mult)

        @block.scalar
        def _(act):
            for b in range(4):
                act.wait_ge(row_ps, b + 1)
                nc.scalar.activation(grp(eg, b), bank4(b), ACT.Exp).then_inc(eg_ready, 1)
            act.wait_ge(scal_sb, 1)
            nc.scalar.activation(scal[:, 2, :], scal[:, 2, :], ACT.Exp).then_inc(scal_exp, 1)
            nc.scalar.activation(scal[:, 4, :], scal[:, 0, :], ACT.Exp).then_inc(scal_exp, 1)
            for b in range(4):
                act.wait_ge(d2_in, b + 1)
                nc.scalar.activation(grp(qkm, b), grp(qkm, b), ACT.Exp).then_inc(d2_ready, 1)

        @block.tensor
        def _(pe):
            for t in range(NT):
                for d in range(2):
                    u = (2 * t + d) * 4
                    nc.tensor.matmul(ps[:, 0, u:u + 4], inc(d), g_[:, t, d, :], start=True, stop=True)
            nc.tensor.matmul(ps[:, 0, NU:2 * NU], same_chunk[:, :], all_units(g_), start=True, stop=True).then_inc(cum_ps, 1)
            pe.wait_ge(bc_ready, 2)
            pe.wait_ge(scal_sb, 1)
            for b in range(4):
                for u in range(4 * b, 4 * b + 4):
                    last = nc.tensor.matmul(ps[:, b, (u % 4) * P:(u % 4 + 1) * P], gbc[:, u, :], inc(b % 2), start=True, stop=True)
                last.then_inc(row_ps, 1)
            for b in range(4):
                for u in range(4 * b, 4 * b + 4):
                    last = nc.tensor.matmul(ps[:, 4 + b, (u % 4) * P:(u % 4 + 1) * P], bbc[:, u, :], ident[:, :], start=True, stop=True)
                last.then_inc(row_ps, 1)
            pe.wait_ge(d2_in, 4)
            for t in range(NT):
                for c in range(2):
                    for hd in range(DHEADS):
                        cols = slice(t * P, (t + 1) * P)
                        last = nc.tensor.matmul(ps[:, 2 * c + t, hd * P:(hd + 1) * P], qkT[:, 1, hd, cols], qkT[:, 1 - c, hd, cols],
                                                start=True, stop=True)
                    last.then_inc(kq_ps, 1)

    spare = T.arena[:, RING2 * PW + 8192 + 1024:]
    low_tri, low_p = (spare[:, 1024 * i:1024 * (i + 1)].rearrange("p (a d) -> p a d", a=8) for i in range(2))
    alt = lambda n: low_tri[:, 4 * (n % 2):4 * (n % 2) + 4, :]
    pb = lambda n: low_p[:, 4 * (n % 2):4 * (n % 2) + 4, :]
    alt_ready, p_ps, p_sb, xx_ps, x_done = (sem(f"inv_{n}") for n in ("alt", "p_ps", "p_sb", "xx_ps", "x_done"))
    STEPS = 4 * LEVELS
    xs_after = lambda n: 2 * (n + 1) - max(0, n + 5 - STEPS)
    with nc.Block() as block:
        @block.gpsimd
        def _(pool):
            for n in range(STEPS):
                lev, b = n // 4, n % 4
                if n >= 2:
                    pool.wait_ge(p_ps, n - 1)
                if 2 <= n < 6:
                    pool.wait_ge(x_done, xs_after(n - 2))
                nc.gpsimd.tensor_tensor(alt(n), grp(at, b), masks[:, b % 2, lev, :].unsqueeze(1).broadcast_to([P, 4, P]),
                                        ALU.mult).then_inc(alt_ready, 1)
                if 12 <= n < 16:
                    g = n - 12
                    nc.gpsimd.tensor_tensor(grp(kdec, g), tok2[:, 0, g // 2, :, :],
                                            scal[:, 2, 4 * g:4 * g + 4].unsqueeze(2).broadcast_to([P, 4, P]), ALU.mult)

        @block.tensor
        def _(pe):
            def inner(n):
                lev, b = n // 4, n % 4
                pe.wait_ge(alt_ready, n + 1)
                if n >= 2:
                    if n - 2 < 4:
                        pe.wait_ge(x_done, xs_after(n - 2))
                    else:
                        pe.wait_ge(p_sb, n - 5)
                if lev:
                    pe.wait_ge(x_done, xs_after(n - 4))
                for q in range(4):
                    rhs = grp(x_, b)[:, q, :] if lev else ident[:, :]
                    last = nc.tensor.matmul(ps[:, n % 2, q * P:(q + 1) * P], alt(n)[:, q, :], rhs, start=True, stop=True)
                last.then_inc(p_ps, 1)

            def outer(n):
                lev, b = n // 4, n % 4
                if lev == 0:
                    return
                pe.wait_ge(p_sb, n - 3)
                if n - 2 >= 4:
                    pe.wait_ge(x_done, xs_after(n - 2))
                for q in range(4 if lev < LEVELS - 1 else 0):
                    last = nc.tensor.matmul(ps[:, 2 + 2 * (n % 2), q * P:(q + 1) * P], grp(xT, b)[:, q, :], pb(n)[:, q, :], start=True, stop=True)
                for q in range(4):
                    last = nc.tensor.matmul(ps[:, 3 + 2 * (n % 2), q * P:(q + 1) * P], pb(n)[:, q, :], grp(xT, b)[:, q, :], start=True, stop=True)
                last.then_inc(xx_ps, 1)

            inner(0)
            for n in range(STEPS):
                if n + 1 < STEPS:
                    inner(n + 1)
                outer(n)

        @block.scalar
        def _(act):
            for n in range(4, STEPS):
                act.wait_ge(p_ps, n + 1)
                if n >= 6:
                    act.wait_ge(xx_ps, n - 5)
                nc.scalar.activation(pb(n), bank4(n % 2), ACT.Copy).then_inc(p_sb, 1)

        @block.vector
        def _(dve):
            eye = ident[:, :].unsqueeze(1).broadcast_to([P, 4, P])
            for n in range(STEPS):
                lev, b = n // 4, n % 4
                if lev == 0:
                    dve.wait_ge(p_ps, n + 1)
                    nc.vector.tensor_tensor(grp(x_, b), eye, bank4(n % 2), ALU.subtract).then_inc(x_done, 1)
                    dve.wait_ge(alt_ready, n + 1)
                    nc.vector.tensor_tensor(grp(xT, b), eye, alt(n), ALU.subtract).then_inc(x_done, 1)
                else:
                    dve.wait_ge(xx_ps, n - 3)
                    dve.wait_ge(x_done, xs_after(n - 4))
                    if lev < LEVELS - 1:
                        nc.vector.tensor_tensor(grp(x_, b), grp(x_, b), bank4(2 + 2 * (n % 2)), ALU.subtract).then_inc(x_done, 1)
                    nc.vector.tensor_tensor(grp(xT, b), grp(xT, b), bank4(3 + 2 * (n % 2)), ALU.subtract).then_inc(x_done, 1)
                if 8 <= n < 16:
                    g = n % 4
                    dst, src, by = ((kb_, tok2[:, 0], scal[:, 3, :]), (vb, tok2[:, 1], all_units(beta)))[n // 4 - 2]
                    nc.vector.tensor_tensor(grp(dst, g), src[:, g // 2, :, :],
                                            by[:, 4 * g:4 * g + 4].unsqueeze(2).broadcast_to([P, 4, P]), ALU.mult)

    wT, u_ = at, x_
    vnew = tok2[:, 0, :, :, :]
    state = tok2[:, 1, :, :, :]
    od = Carve(T.arena[:, RING2 * PW + 8192:])(2, DHEADS, S)
    wu_ps, w_sb, u_sb, v_ps, v_sb, s_ps, s_sb, o_ps, o_sb, o_sum, on_sq, on_ps, on_ms, on_rt, on_r, o_ready = (sem(f"scan_{n}") for n in (
        "wu_ps", "w_sb", "u_sb", "v_ps", "v_sb", "s_ps", "s_sb", "o_ps", "o_sb", "o_sum", "on_sq", "on_ps", "on_ms", "on_rt", "on_r", "o_ready"))
    on_diag, on_bc = sem("scan_on_diag"), sem("scan_on_bc")
    orn = T.sb(stack, "orn", [P, 8])
    odiag = kb_[:, 0:8, :]
    steps = [(st, d) for st in range(4) for d in range(2)]

    def place(st, d):
        c = st if d == 0 else 3 - st
        t, lo = c // 2, CH * (c % 2)
        return c, (2 * t + d) * 4, slice(lo, lo + CH), t, c % 2

    with nc.Block() as block:
        @block.tensor
        def _(pe):
            for b in range(4):
                for q in range(4):
                    u = 4 * b + q
                    last = nc.tensor.matmul(ps[:, 2 * (b % 2), q * P:(q + 1) * P], kb_[:, u, :], xT[:, u, :], start=True, stop=True)
                last.then_inc(wu_ps, 1)
                for q in range(4):
                    u = 4 * b + q
                    last = nc.tensor.matmul(ps[:, 2 * (b % 2) + 1, q * P:(q + 1) * P], xT[:, u, :], vb[:, u, :], start=True, stop=True)
                last.then_inc(wu_ps, 1)
                if b >= 1:
                    pe.wait_ge(w_sb, b)
                    pe.wait_ge(u_sb, b)
            pe.wait_ge(w_sb, 4)
            for st in range(4):
                both = [(2 * st + d, d, *place(st, d)) for d in range(2)]
                for n, d, c, u0, cols, t, half in both:
                    if st:
                        pe.wait_ge(s_sb, n - 1)
                        for q in range(4):
                            last = nc.tensor.matmul(ps[cols, 2 + d, q * P:(q + 1) * P], wT[:, u0 + q, cols], state[:, d, q, :], start=True, stop=True)
                        last.then_inc(v_ps, 1)
                for n, d, c, u0, cols, t, half in both:
                    pe.wait_ge(v_sb, n + 1)
                    if st < 3:
                        for q in range(4):
                            last = nc.tensor.matmul(ps[:, 6 + d, q * P:(q + 1) * P], kdec[cols, u0 + q, :], vnew[cols, d, q, :], start=True, stop=True)
                        last.then_inc(s_ps, 1)
                for n, d, c, u0, cols, t, half in both:
                    if st:
                        pe.wait_ge(o_sb, n - 1)
                    for q in range(4):
                        dst = ps[:, 4 + d, q * CH:(q + 1) * CH]
                        if st:
                            nc.tensor.matmul(dst, state[:, d, q, :], qdec[:, u0 + q, cols], start=True, stop=False)
                        last = nc.tensor.matmul(dst, vnew[cols, d, q, :], qkm[cols, u0 + q, cols], start=(st == 0), stop=True)
                    last.then_inc(o_ps, 1)
            pe.wait_ge(on_sq, 1)
            for hd in range(DHEADS):
                for t in range(NT):
                    last = nc.tensor.matmul(ps[:, 0, hd * NT + t:hd * NT + t + 1], od[:, 1, hd, t * P:(t + 1) * P], ones[:, 0:1],
                                            start=True, stop=True)
            last.then_inc(on_ps, 1)
            for b in range(2):
                pe.wait_ge(on_diag, b + 1)
                nc.tensor.matmul(ps[:, 2 + b, :], ones[:, :], odiag[:, 4 * b:4 * b + 4, :].rearrange("p a c -> p (a c)"),
                                 start=True, stop=True).then_inc(on_bc, 1)

        @block.vector
        def _(dve):
            link = T.link(dve, "dve", T.chain_dve)
            for b in range(4):
                dve.wait_ge(wu_ps, 2 * b + 2)
                nc.vector.tensor_copy(grp(u_, b), bank4(2 * (b % 2) + 1)).then_inc(u_sb, 1)
            dve.wait_ge(u_sb, 4)
            for st in range(4):
                both = [(2 * st + d, d, *place(st, d)) for d in range(2)]
                for n, d, c, u0, cols, t, half in both:
                    if st:
                        dve.wait_ge(v_ps, n - 1)
                        dve.wait_ge(o_ps, n - 1)
                        nc.vector.tensor_tensor(vnew[cols, d, :, :], u_[cols, u0:u0 + 4, :], bank4(2 + d)[cols], ALU.subtract).then_inc(v_sb, 1)
                    else:
                        nc.vector.tensor_copy(vnew[cols, d, :, :], u_[cols, u0:u0 + 4, :]).then_inc(v_sb, 1)
                for n, d, c, u0, cols, t, half in both:
                    if st == 3:
                        continue
                    dve.wait_ge(s_ps, n + 1)
                    if st == 0:
                        nc.vector.tensor_copy(state[:, d, :, :], bank4(6 + d)).then_inc(s_sb, 1)
                    else:
                        dve.wait_ge(s_sb, n - 1)
                        dve.wait_ge(o_ps, n + 1)
                        for q in range(4):
                            last = nc.vector.scalar_tensor_tensor(state[:, d, q, :], state[:, d, q, :], egl[:, t, d, half, q:q + 1],
                                                                  bank4(6 + d)[:, q, :], ALU.mult, ALU.add)
                        last.then_inc(s_sb, 1)
            dve.wait_ge(o_sb, 8)
            o, sqd = od[:, 0, :, :], od[:, 1, :, :]
            link(nc.vector.tensor_tensor(o, o, sqd, ALU.add))
            nc.vector.tensor_tensor(sqd, o, o, ALU.mult).then_inc(on_sq, 1)
            dve.wait_ge(on_ps, 1)
            nc.vector.tensor_scalar(orn[:, :], ps[:, 0, 0:8], 1.0 / DK, EPS, ALU.mult, ALU.add).then_inc(on_ms, 1)
            link(nc.vector.scalar_tensor_tensor(o, o, head_norm[:, 0:1], z[:, :, :], ALU.mult, ALU.mult))
            dve.wait_ge(on_rt, 1)
            link(nc.vector.reciprocal(orn[:, :], orn[:, :]))
            for b in range(2):
                nc.vector.tensor_tensor(odiag[:, 4 * b:4 * b + 4, :], ident[:, :].unsqueeze(1).broadcast_to([P, 4, P]),
                                        orn[:, 4 * b:4 * b + 4].unsqueeze(2).broadcast_to([P, 4, P]), ALU.mult).then_inc(on_diag, 1)
            for b in range(2):
                dve.wait_ge(on_bc, b + 1)
                nc.vector.tensor_tensor(oT[:, 2 * b:2 * b + 2, :], o[:, 2 * b:2 * b + 2, :], ps[:, 2 + b, :].rearrange("p (a s) -> p a s", a=2),
                                        ALU.mult).then_inc(o_ready, 1)

        @block.scalar
        def _(act):
            for b in range(4):
                act.wait_ge(wu_ps, 2 * b + 1)
                nc.scalar.activation(grp(wT, b), bank4(2 * (b % 2)), ACT.Copy).then_inc(w_sb, 1)
            for n, (st, d) in enumerate(steps):
                c, u0, cols, t, half = place(st, d)
                act.wait_ge(o_ps, n + 1)
                nc.scalar.activation(od[:, d, :, c * CH:(c + 1) * CH], ps[:, 4 + d, 0:S].rearrange("p (h s) -> p h s", h=4),
                                     ACT.Copy).then_inc(o_sb, 1)
            act.wait_ge(on_ms, 1)
            nc.scalar.activation(orn[:, :], orn[:, :], ACT.Sqrt).then_inc(on_rt, 1)

    res2 = sem("res2")
    with nc.Block() as block:
        @block.sync
        def _(sync):
            for g in range(G2_OUT + RING2, G2_EXP + RING2):
                ring.issue(sync, g, T.stream2(g))

        @block.tensor
        def _(pe):
            for c in range(4):
                ring.arrived(pe, G2_OUT + c)
                w = ring.piece(G2_OUT + c).rearrange("p (k c) -> p k c", k=KB)
                for t in range(NT):
                    for k in range(KB):
                        last = nc.tensor.matmul(ps[:, c, t * S:(t + 1) * S], oT[:, k, t * P:(t + 1) * P], w[:, k, :],
                                                start=(k == 0), stop=(k == KB - 1))
                last.then_inc(ring.used, 1)

        @block.vector
        def _(dve):
            for c in range(4):
                dve.wait_ge(ring.used, G2_OUT + c + 1)
                x = h[:, :, 256 * c:256 * (c + 1)]
                nc.vector.tensor_tensor(x, x, ps[:, c, :].rearrange("p (t c) -> p t c", t=NT), ALU.add).then_inc(res2, 1)
    stack.close()
    experts(T)


def experts(T):
    nc, A, ps, sem = T.nc, T.A, T.ps, T.sem
    h, hT, ident, ring = T.h, T.hT, T.ident, T.ring2
    expert_stack = ExitStack()
    low_c, high_c = Carve(T.sb(expert_stack, "low2", [P, 3 * PW])), Carve(T.arena[:, RING2 * PW:])
    xs = low_c(NT, D)
    xg = low_c(KB, NEXP * CAP)
    r_tile = lambda name, *shape: expert_stack.enter_context(nc.sbuf_tensor(name, [P, *shape], F32R))
    onehot = r_tile("onehot", NT, NEXP * CAP)
    xs_parts = r_tile("xs_parts", 2, NT, D)
    yb = high_c(D)
    sg, hh, hidT = high_c(BANK), high_c(BANK), high_c(4, P)
    stack = ExitStack()
    sb = lambda name, *shape: T.sb(stack, name, [P, *shape])
    router_w, ones, iota_s, tokid, zeros = sb("router_w", KB, NEXP), sb("ones2", P), sb("iota_s", S), sb("tokid", NT), sb("zeros2", BANK)
    probs, st = sb("probs", NT, NEXP), sb("st", 3, NT)
    pT = T.sb(stack, "probsT", [NEXP, 2, S])
    gate, place, place_f = T.sb(stack, "gate", [NEXP, CAP]), T.sb(stack, "place2", [NEXP, CAP], U32), T.sb(stack, "place_f", [NEXP, CAP])
    rep = T.sb(stack, "rep", [NEXP, 2, 4, CAP])
    diag = T.sb(stack, "diag", [NEXP, NEXP, CAP])
    cols = sb("cols", 2, NEXP)
    xe = sb("xe", KB, CAP)
    og = sb("og", S)
    loads = [(router_w[:, :, :], "router_w"), (ones[:, :], "ones"), (iota_s[:, :], "iota_s"), (tokid[:, :], "tokid")]
    c3 = sem("expert_consts")

    def refill(sync):
        for dst, name in loads:
            sync.dma_start(dst, A[name]).then_inc(c3, 16)

    def small(pe, done):
        pe.wait_ge(c3, 16 * len(loads))
        for t in range(NT):
            for k in range(KB):
                last = nc.tensor.matmul(ps[:, 4, t * NEXP:(t + 1) * NEXP], hT[:, k, t * P:(t + 1) * P], router_w[:, k, :],
                                        start=(k == 0), stop=(k == KB - 1))
        last.then_inc(done, 1)

    front(T, "ec", 3, ring, G2_EXP, [], small, refill, xs=xs)

    ex_sub, ex_exp, ex_p, pt_ps, pt_sb, rep_ready, cols_ps, bc_ps, oh_ready, xg_ps, xg_sb, z_ready = (sem(f"ec_{n}") for n in (
        "sub", "exp", "p", "pt_ps", "pt_sb", "rep", "cols_ps", "bc_ps", "oh", "xg_ps", "xg_sb", "zeros"))
    xe_ready, xs_high, xs_low = sem("ec_xe"), sem("ec_xs_high"), sem("ec_xs_low")
    with nc.Block() as block:
        @block.vector
        def _(dve):
            link = T.link(dve, "dve", T.chain_dve)
            nc.vector.memset(zeros[:, :], 0.0).then_inc(z_ready, 1)
            lgt = ps[:, 4, 0:NT * NEXP].rearrange("p (t e) -> p t e", t=NT)
            link(nc.vector.reduce_max(st[:, 0, :], lgt, AX.X))
            nc.vector.tensor_tensor(probs[:, :, :], lgt, st[:, 0, :].unsqueeze(2).broadcast_to([P, NT, NEXP]), ALU.subtract).then_inc(ex_sub, 1)
            dve.wait_ge(ex_exp, 1)
            link(nc.vector.reduce_sum(st[:, 1, :], probs[:, :, :], AX.X))
            link(nc.vector.reciprocal(st[:, 2, :], st[:, 1, :]))
            nc.vector.tensor_tensor(probs[:, :, :], probs[:, :, :], st[:, 2, :].unsqueeze(2).broadcast_to([P, NT, NEXP]), ALU.mult).then_inc(ex_p, 1)
            dve.wait_ge(pt_ps, 1)
            nc.vector.tensor_copy(pT[:, 0, :], ps[0:NEXP, 5, 0:S]).then_inc(pt_sb, 1)
            dve.wait_ge(pt_sb, 1)
            for r in range(CAP // 8):
                eight = slice(8 * r, 8 * r + 8)
                cur, nxt = pT[:, r % 2, :], pT[:, 1 - r % 2, :]
                link(nc.vector.max(gate[:, eight], cur))
                link(nc.vector.max_index(place[:, eight], gate[:, eight], cur))
                if r < CAP // 8 - 1:
                    link(nc.vector.match_replace(nxt, gate[:, eight], cur, -1.0))
            link(nc.vector.tensor_copy(place_f[:, :], place[:, :]))
            nc.vector.tensor_copy(rep[:, 0, :, :], place_f[:, :].unsqueeze(1).broadcast_to([NEXP, 4, CAP]))
            nc.vector.tensor_copy(rep[:, 1, :, :], gate[:, :].unsqueeze(1).broadcast_to([NEXP, 4, CAP]))
            nc.vector.tensor_tensor(diag[:, :, :], place_f[:, :].unsqueeze(1).broadcast_to([NEXP, NEXP, CAP]),
                                    ident[0:NEXP, 0:NEXP].unsqueeze(2).broadcast_to([NEXP, NEXP, CAP]), ALU.mult).then_inc(rep_ready, 1)
            dve.wait_ge(cols_ps, 1)
            nc.vector.tensor_copy(cols[:, :, :], ps[:, 6, 0:2 * NEXP].rearrange("p (a e) -> p a e", a=2))
            dve.wait_ge(bc_ps, 1)
            for t in range(NT):
                nc.vector.tensor_scalar(onehot[:, t, :], ps[:, 7, :], tokid[:, t:t + 1], None, ALU.is_equal).then_inc(oh_ready, 1)
            dve.wait_ge(xg_sb, KB)
            nc.vector.tensor_copy(xe[:, :, :], xg[:, :, 0:CAP]).then_inc(xe_ready, 1)

        @block.scalar
        def _(act):
            act.wait_ge(ex_sub, 1)
            nc.scalar.activation(probs[:, :, :], probs[:, :, :], ACT.Exp).then_inc(ex_exp, 1)
            nc.scalar.activation(xs_parts[:, 0, :, :], xs[:, :, :], ACT.Copy).then_inc(xs_high, 1)
            for k in range(KB):
                act.wait_ge(xg_ps, k + 1)
                nc.scalar.activation(xg[:, k, :], ps[:, k % 4, :], ACT.Copy, scale=T.gains[:, 3, k:k + 1]).then_inc(xg_sb, 1)

        @block.gpsimd
        def _(pool):
            pool.wait_ge(xs_high, 1)
            nc.gpsimd.tensor_tensor(xs_parts[:, 1, :, :], xs[:, :, :], xs_parts[:, 0, :, :].bitcast(F32), ALU.subtract).then_inc(xs_low, 1)

        @block.tensor
        def _(pe):
            pe.wait_ge(ex_p, 1)
            for t in range(NT):
                last = nc.tensor.transpose(ps[0:NEXP, 5, t * P:(t + 1) * P], probs[:, t, :], ident[:, :])
            last.then_inc(pt_ps, 1)
            pe.wait_ge(rep_ready, 1)
            for a in range(2):
                last = nc.tensor.transpose(ps[:, 6, a * NEXP:(a + 1) * NEXP], rep[:, a, :, :].rearrange("p c s -> p (c s)"), ident[0:NEXP, 0:NEXP])
            last.then_inc(cols_ps, 1)
            nc.tensor.matmul(ps[:, 7, :], ones[0:NEXP, :], diag[:, :, :].rearrange("p e s -> p (e s)"), start=True, stop=True).then_inc(bc_ps, 1)
            pe.wait_ge(oh_ready, NT)
            pe.wait_ge(xs_low, 1)
            for k in range(KB):
                if k >= 4:
                    pe.wait_ge(xg_sb, k - 3)
                for t in range(NT):
                    for a in range(2):
                        last = nc.tensor.matmul(ps[:, k % 4, :], xs_parts[:, a, t, k * P:(k + 1) * P], onehot[:, t, :],
                                                start=(t == 0 and a == 0), stop=(t == NT - 1 and a == 1))
                last.then_inc(xg_ps, 1)

    sg_ready, hh_ready, t_ps, hid_ready, y_ready, og_ready = (sem(f"ex_{n}") for n in ("sg", "hh", "t_ps", "hid", "y", "og"))
    PER = 3 * KB
    used = lambda n, e: e * PER + (G2_EXP + n)
    with nc.Block() as block:
        @block.sync
        def _(sync):
            def load(e, r, turn):
                src = A["experts_in"][e, r // KB, r % KB] if r < 2 * KB else A["experts_down"][e, r - 2 * KB]
                ring.issue(sync, G2_EXP + r, src, turn)
            for r in range(RING2, PER):
                load(0, r, 0)
            with sync.Fori(1, NEXP) as e:
                for r in range(PER):
                    load(e, r, e * (PER // RING2))

        @block.tensor
        def _(pe):
            pe.wait_ge(z_ready, 1)
            for b in range(4):
                nc.tensor.matmul(ps[:, b, :], zeros[:, 0:P], zeros[:, :], start=True, stop=False, skip_group_check=True)
            with pe.Fori(0, NEXP) as e:
                turn = e * (PER // RING2)
                pe.wait_ge(xe_ready, e + 1)
                for r in range(2 * KB):
                    ring.arrived(pe, G2_EXP + r, turn)
                    w, k = ring.piece(G2_EXP + r), r % KB
                    for j in range(4):
                        last = nc.tensor.matmul(ps[32 * j:32 * (j + 1), 4 + r // KB, :], xe[:, k, :], w[:, j * BANK:(j + 1) * BANK],
                                                start=(k == 0), stop=(k == KB - 1), tile_position=(0, 32 * j))
                    last.then_inc(ring.used, 1)
                pe.wait_ge(hh_ready, e + 1)
                for i in range(4):
                    last = nc.tensor.transpose(ps[:, 4, i * P:(i + 1) * P], hh[:, i * P:(i + 1) * P], ident[:, :])
                last.then_inc(t_ps, 1)
                pe.wait_ge(hid_ready, e + 1)
                for r in range(KB):
                    ring.arrived(pe, G2_EXP + 2 * KB + r, turn)
                    w = ring.piece(G2_EXP + 2 * KB + r).rearrange("p (j d) -> p j d", j=4)
                    i, half = r // 2, r % 2
                    for j in range(4):
                        last = nc.tensor.matmul(ps[32 * j:32 * (j + 1), 6 + half, :], hidT[:, i, 32 * j:32 * (j + 1)], w[:, j, :],
                                                start=(i == 0), stop=(i == 3), tile_position=(0, 32 * j))
                    last.then_inc(ring.used, 1)
                pe.wait_ge(y_ready, e + 1)
                pe.wait_ge(og_ready, e + 1)
                for t in range(NT):
                    for half in range(2):
                        last = nc.tensor.matmul(ps[:, 2 * t + half, :], og[:, t * P:(t + 1) * P], yb[:, half * BANK:(half + 1) * BANK],
                                                start=False, stop=False, skip_group_check=True)
            for b in range(4):
                last = nc.tensor.matmul(ps[:, b, :], zeros[:, 0:P], zeros[:, :], start=False, stop=True, skip_group_check=True)

        @block.scalar
        def _(act):
            with act.Fori(0, NEXP) as e:
                act.wait_ge(ring.used, used(KB, e))
                nc.scalar.activation(sg, ps[:, 4, :], ACT.Silu).then_inc(sg_ready, 1)
                act.wait_ge(t_ps, e + 1)
                nc.scalar.activation(hidT.rearrange("p i c -> p (i c)"), ps[:, 4, :], ACT.Copy).then_inc(hid_ready, 1)
                act.wait_ge(ring.used, used(PER, e))
                nc.scalar.activation(yb, ps[:, 6:8, :].rearrange("p b c -> p (b c)"), ACT.Copy).then_inc(y_ready, 1)

        @block.vector
        def _(dve):
            def body(e, last_one):
                dve.wait_ge(sg_ready, e + 1)
                dve.wait_ge(ring.used, used(2 * KB, e))
                nc.vector.tensor_tensor(hh, sg, ps[:, 5, :], ALU.mult).then_inc(hh_ready, 1)
                nc.vector.tensor_scalar(og[:, :], iota_s[:, :], cols[:, 0, bass.ds(e, 1)], cols[:, 1, bass.ds(e, 1)],
                                        ALU.is_equal, ALU.mult).then_inc(og_ready, 1)
                if not last_one:
                    nc.vector.tensor_copy(xe[:, :, :], xg[:, :, bass.ds(e * CAP + CAP, CAP)]).then_inc(xe_ready, 1)
            with dve.Fori(0, NEXP - 1) as e:
                body(e, False)
            body(NEXP - 1, True)
    stack.close()
    expert_stack.close()
    norm_tokens(T, "norm_final_2", add_banks=True, store=T.out)


def host_arrays(inputs):
    import numpy as np

    f = {k: np.asarray(v) for k, v in inputs.items()}
    f32 = np.float32
    out = {"x": f["x"][0]}

    def col_pieces(w):
        n = w.shape[1] // 256
        return w.reshape(KB, P, n, 256).transpose(2, 1, 0, 3).reshape(n, P, PW)

    def half_pieces(w):
        n = w.shape[1] // P
        return w.reshape(KB, P, n, P).transpose(2, 1, 0, 3).reshape(n, P, HW)

    cols = lambda g: g.reshape(KB, P).T
    out["gains"] = np.stack([cols(f["norm_mix"][0]), cols(f["norm_ffn"][0]), cols(f["norm_mix_w_2"][0]),
                             cols(f["norm_ffn_w_2"][0])], axis=1)
    out["ident"] = np.eye(P, dtype=f32)
    w = f["w_in"][0]
    sizes = dict(fq=512, fk=512, fv=512, f=8, nq=512, kc=128, vc=128, ksl=128, vsl=128, kwn=128, vwn=128,
                 gate=24, merge=2048)
    parts, at = {}, 0
    for name, n in sizes.items():
        parts[name] = w[:, at:at + n]
        at += n
    twice = lambda a: np.concatenate([a[:, 0:64], a[:, 0:64], a[:, 64:128], a[:, 64:128]], axis=1)
    order = [parts["fq"], parts["fk"], parts["nq"], twice(parts["ksl"]), twice(parts["kwn"]), parts["kc"], parts["vc"],
             parts["merge"], parts["fv"], parts["vsl"], parts["vwn"]]
    w1 = f["nsa_cmp_w1"][0].reshape(2, 4, 8, DH, P).transpose(0, 1, 3, 2, 4).reshape(8, DH, HW)
    w1 = np.concatenate([w1, w1], axis=1)
    subk = f["peer_subkeys"][0].reshape(2, 8, P, P).transpose(0, 3, 1, 2).reshape(2, P, HW)
    out["stream1"] = np.concatenate([half_pieces(np.concatenate(order, axis=1)), w1,
                                     half_pieces(f["w_branch"][0].reshape(D, D)), half_pieces(f["w_out"][0]),
                                     half_pieces(f["peer_wq"][0]), subk], axis=0)
    u = f["peer_u"][0].reshape(NKEYS, P, KB, P).transpose(0, 3, 2, 1).reshape(NKEYS, P, HW)
    v = f["peer_v"][0].reshape(NKEYS, P, HW)
    out["peer"] = np.stack([u, v], axis=1)
    out["iota16"] = np.broadcast_to(np.arange(16, dtype=f32), (P, 16))
    out["iota128"] = np.broadcast_to(np.arange(P, dtype=f32), (P, P))
    small = np.zeros((KB, P, 160), f32)
    fw = parts["f"].reshape(KB, P, 8)
    small[:, :, 0:8] = fw
    small[:, :, 64:72] = fw
    small[:, :, 128:152] = parts["gate"].reshape(KB, P, 24)
    out["small_w"] = small.transpose(1, 0, 2)
    fb = np.zeros((P, 1), f32)
    fb[0:8, 0] = fb[64:72, 0] = f["fox_f_bias"][0]
    out["fbias"] = fb
    out["cmp_pos"] = np.concatenate([f["nsa_cmp_pos"][0].transpose(2, 0, 1)] * 2, axis=0)
    w2 = f["nsa_cmp_w2"][0].transpose(1, 0, 2)
    out["cmp_w2"] = np.concatenate([w2, w2], axis=2)

    w = f["w_in_2"][0]
    wm = np.concatenate([w[:, 0:2048], w[:, 2064:2576]], axis=1)
    out["stream2"] = np.concatenate([col_pieces(wm), col_pieces(f["w_out_2"][0])], axis=0)
    out["ab_w"] = w[:, 2048:2064].reshape(KB, P, 16).transpose(1, 0, 2)
    out["norm_final"] = np.broadcast_to(f["norm_final"], (P, D))
    out["norm_final_2"] = np.broadcast_to(f["norm_final_w_2"], (P, D))
    out["conv_w"] = f["conv_w_2"][0].reshape(5, 12, P).transpose(2, 1, 0)
    out["pool_w"] = f["pool_w_2"][0].transpose(1, 0, 2)
    out["pool_scale"] = f["pool_scale_2"][0].reshape(4, P).T
    out["head_norm"] = f["head_norm_w_2"][0].reshape(P, 1)
    out["a_log"] = np.broadcast_to(np.concatenate([f["a_log_fwd_2"][0], f["a_log_bwd_2"][0]]), (P, 8))
    out["dt_bias"] = np.broadcast_to(np.concatenate([f["dt_bias_fwd_2"][0], f["dt_bias_bwd_2"][0]]), (P, 8))
    out["router_w"] = f["router_w_2"][0].reshape(KB, P, NEXP).transpose(1, 0, 2)
    out["experts_in"] = np.stack([f["expert_w_gate_2"][0].reshape(NEXP, KB, P, PW), f["expert_w_up_2"][0].reshape(NEXP, KB, P, PW)], axis=1)
    out["experts_down"] = (f["expert_w_down_2"][0].reshape(NEXP, 4, 4, P, 2, BANK).transpose(0, 2, 4, 3, 1, 5)
                           .reshape(NEXP, KB, P, PW))

    out["ones"] = np.ones((P, P), f32)
    out["iota_s"] = np.broadcast_to(np.arange(S, dtype=f32), (P, S))
    out["tokid"] = np.arange(S, dtype=f32).reshape(NT, P).T
    i = np.arange(P)
    chunk = i[:, None] // CH == i[None, :] // CH
    masks = np.zeros((P, 2, LEVELS + 1, P), f32)
    for lev in range(LEVELS):
        b = 1 << lev
        pair = i[:, None] // (2 * b) == i[None, :] // (2 * b)
        m = pair & ((i[:, None] // b) % 2 == 0) & ((i[None, :] // b) % 2 == 1)
        masks[:, 0, lev], masks[:, 1, lev] = m, m.T
    masks[:, 0, LEVELS] = chunk & (i[:, None] <= i[None, :])
    masks[:, 1, LEVELS] = chunk & (i[:, None] >= i[None, :])
    out["masks"] = masks
    out["same_chunk"] = chunk.astype(f32)
    pm = np.zeros((S, 4, S), f32)
    for n, win in enumerate((2, 4, 8, 16)):
        lo = win // 2
        for t in range(S):
            a, b = max(t - lo, 0), min(t + win - lo, S)
            pm[a:b, n, t] = f32(1.0) / f32(b - a)
            pm[t, n, t] -= 1.0
    out["pool_m"] = pm.reshape(NT, P, 4, S).transpose(1, 0, 2, 3)
    def tables(positions):
        inv = np.power(f32(500000.0), -np.arange(0, 16, 2, dtype=f32) / f32(16))
        ang = positions.astype(f32)[:, None] * inv[None, :]
        cos, sin = np.ones((P, len(positions)), f32), np.zeros((P, len(positions)), f32)
        for base in (0, DH):
            for half in (0, 8):
                cos[base + half:base + half + 8] = np.cos(ang).T
                sin[base + half:base + half + 8] = np.sin(ang).T
        return np.stack([cos, sin], axis=1)

    out["tables"] = tables(np.arange(S))
    out["tables_cmp"] = tables(np.arange(16) * CMP_STRIDE + CMP_LEN - 1)
    rot = np.zeros((P, P), f32)
    for base in (0, DH):
        for i in range(8):
            rot[base + 8 + i, base + i] = -1.0
            rot[base + i, base + 8 + i] = 1.0
    out["rot"] = rot
    tri = np.where(np.arange(P)[None, :] <= np.arange(P)[:, None], 0.0, NEG).astype(f32)
    out["causal"] = np.concatenate([np.zeros((P, P), f32), tri], axis=1)
    end = np.arange(16) * CMP_STRIDE + CMP_LEN - 1
    seen = end[None, :] <= np.arange(S)[:, None]
    mc = np.stack([np.where(seen, 0.0, NEG), seen.astype(f32)], axis=0).astype(f32)
    out["mask_cmp"] = mc.reshape(2, NT, P, 16).transpose(2, 0, 1, 3)
    sel = np.zeros((P, 8, S), f32)
    for i in range(8):
        sel[i, i] = sel[64 + i, i] = 8.0
    out["sel8"] = sel
    return {k: np.ascontiguousarray(v, dtype=f32) for k, v in out.items()}


def kernel(**inputs):
    import numpy as np
    import concourse.bacc as bacc
    from concourse.bass_utils import run_bass_kernel_spmd

    nc = bacc.Bacc("TRN2", target_bir_lowering=False, num_devices=1)
    arrays = host_arrays(inputs)
    A = {name: nc.dram_tensor(f"in_{name}", a.shape, mybir.dt.from_np(a.dtype), kind="ExternalInput").ap()
         for name, a in arrays.items()}
    out = nc.dram_tensor("out", (S, D), F32, kind="ExternalOutput").ap()
    build_kernel(nc, A, out)
    r = run_bass_kernel_spmd(nc, [{f"in_{name}": a for name, a in arrays.items()}], core_ids=[0])
    return r.results[0]["out"].reshape(1, S, D)
```
